# Optimizing a Trainium2 kernel written in Bass

```python
import jax, jax.numpy as jnp
from jax import lax
import numpy as np

D_MODEL = 1024
BATCH = 1
SEQ = 256
DEPTH = 2
DEC_BATCH = 8
DEC_SEQ = 1
PAST_LEN = 2048
PAGE_SIZE = 128

MIX_WIDTH = D_MODEL
HG_WIDTH = MIX_WIDTH // 2
HG_HEADS = 4
HG_DK = HG_WIDTH // HG_HEADS
HG_DV = HG_DK
POOL_WIDTH = MIX_WIDTH - HG_WIDTH
POOL_WINDOWS = (2, 4, 8, 16)
POOL_GROUPS = len(POOL_WINDOWS)
POOL_GROUP_W = POOL_WIDTH // POOL_GROUPS
POOL_BUF = max(POOL_WINDOWS) - 1
IN_WIDTH = 4 * HG_WIDTH + POOL_WIDTH
CHUNK = 64
D_FF = 2816
N_EXPERTS = 8
TOP_K = 2
D_FF_E = 1408
N_DENSE = (DEPTH + 1) // 2
N_MOE = DEPTH // 2
EPS = 1e-6

kernel_name = "hgrn2_pool_hybrid_decoder_step"

def rmsnorm(x, g):
    xf = x.astype(jnp.float32)
    y = xf * lax.rsqrt(jnp.mean(xf * xf, axis=-1, keepdims=True) + EPS)
    return (y * g.astype(jnp.float32)).astype(x.dtype)

def lower_bounds(lb_logits):
    p = jax.nn.softmax(lb_logits.astype(jnp.float32), axis=0)
    return jnp.cumsum(p, axis=0) - p[0:1]

def hgrn2_scan(q, logf, k, v, S0):
    B, H, L, _ = q.shape
    C = CHUNK if L >= CHUNK else L
    pad = (-L) % C
    if pad:
        pw = ((0, 0), (0, 0), (0, pad), (0, 0))
        q, logf, k, v = jnp.pad(q, pw), jnp.pad(logf, pw), jnp.pad(k, pw), jnp.pad(v, pw)
    n = (L + pad) // C

    def to_chunks(a):
        return jnp.moveaxis(a.reshape(B, H, n, C, a.shape[-1]), 2, 0)

    causal = jnp.tril(jnp.ones((C, C), dtype=bool))[:, :, None]

    def step(S, xs):
        qc, lfc, kc, vc = xs
        b = jnp.cumsum(lfc, axis=2)
        diff = b[:, :, :, None, :] - b[:, :, None, :, :]
        decay = jnp.exp(jnp.where(causal, diff, -jnp.inf))
        scores = jnp.einsum('bhtk,bhtsk,bhsk->bhts', qc, decay, kc)
        o = (jnp.einsum('bhts,bhsv->bhtv', scores, vc)
             + jnp.einsum('bhtk,bhkv->bhtv', qc * jnp.exp(b), S))
        bC = b[:, :, -1:, :]
        S_new = (jnp.exp(bC[:, :, 0, :])[..., None] * S
                 + jnp.einsum('bhsk,bhsv->bhkv', kc * jnp.exp(bC - b), vc))
        return S_new, o

    S, o = lax.scan(step, S0, (to_chunks(q), to_chunks(logf), to_chunks(k), to_chunks(v)))
    o = jnp.moveaxis(o, 0, 2).reshape(B, H, n * C, -1)[:, :, :L]
    return o, S

def multiscale_pool(u, buf, start_pos, w_pool, scale):
    B, L, _ = u.shape
    z = jnp.concatenate([buf.astype(jnp.float32), u.astype(jnp.float32)], axis=1)
    cs = jnp.concatenate([jnp.zeros((B, 1, POOL_WIDTH), jnp.float32), jnp.cumsum(z, axis=1)], axis=1)
    end = cs[:, POOL_BUF + 1:POOL_BUF + 1 + L]
    pos = start_pos + jnp.arange(L)
    cur = z[:, POOL_BUF:]
    outs = []
    for gi, w in enumerate(POOL_WINDOWS):
        sl = slice(gi * POOL_GROUP_W, (gi + 1) * POOL_GROUP_W)
        begin = cs[:, POOL_BUF + 1 - w:POOL_BUF + 1 - w + L, sl]
        cnt = jnp.minimum(pos + 1, w).astype(jnp.float32)[None, :, None]
        outs.append((end[..., sl] - begin) / cnt - cur[..., sl])
    d = jnp.stack(outs, axis=2)
    y = jnp.einsum('blgc,gcd->blgd', d, w_pool.astype(jnp.float32)).reshape(B, L, POOL_WIDTH)
    y = y * scale.astype(jnp.float32)
    new_buf = z[:, -POOL_BUF:]
    return y.astype(u.dtype), new_buf.astype(buf.dtype)

def mixer(h, S0, buf, start_pos, lb, w_in, w_o, hg_norm, w_pool, pool_scale):
    B, L, _ = h.shape
    proj = h @ w_in
    q, fx, ix, g, u = jnp.split(proj, [HG_WIDTH, 2 * HG_WIDTH, 3 * HG_WIDTH, 4 * HG_WIDTH], axis=-1)

    def heads(a):
        return a.reshape(B, L, HG_HEADS, -1).transpose(0, 2, 1, 3).astype(jnp.float32)

    f = lb + (1.0 - lb) * jax.nn.sigmoid(fx.astype(jnp.float32))
    o, S = hgrn2_scan(heads(jax.nn.silu(q.astype(jnp.float32))), heads(jnp.log(f)), heads(1.0 - f),
                      heads(ix), S0.astype(jnp.float32))
    o = o.transpose(0, 2, 1, 3)
    o = o * lax.rsqrt(jnp.mean(o * o, axis=-1, keepdims=True) + EPS)
    o = o * hg_norm.astype(jnp.float32).reshape(HG_HEADS, HG_DV)
    o = o.reshape(B, L, HG_WIDTH) * jax.nn.silu(g.astype(jnp.float32))
    yp, new_buf = multiscale_pool(u, buf, start_pos, w_pool, pool_scale)
    y = jnp.concatenate([o.astype(h.dtype), yp], axis=-1) @ w_o
    return y, S.astype(S0.dtype), new_buf

def swiglu(h, wg, wu, wd):
    return (jax.nn.silu(h @ wg) * (h @ wu)) @ wd

def moe(h, router, wg, wu, wd):
    logits = (h @ router).astype(jnp.float32)
    top_v, top_i = lax.top_k(logits, TOP_K)
    gates = jax.nn.softmax(top_v, axis=-1)
    combine = jnp.sum(jax.nn.one_hot(top_i, N_EXPERTS, dtype=jnp.float32) * gates[..., None], axis=-2)
    y = jnp.zeros_like(h)
    for e in range(N_EXPERTS):
        y = y + combine[..., e:e + 1].astype(h.dtype) * swiglu(h, wg[e], wu[e], wd[e])
    return y

def trunk(x, S_in, buf_in, start_pos, lb_logits, norm_mix, w_in, w_o, hg_norm, pool_w, pool_scale,
          norm_ffn, ffn_w_gate, ffn_w_up, ffn_w_down, router, moe_w_gate, moe_w_up, moe_w_down, norm_final):
    lbs = lower_bounds(lb_logits)
    S_out, buf_out = [], []
    for l in range(DEPTH):
        h = rmsnorm(x, norm_mix[l])
        y, S, b = mixer(h, S_in[l], buf_in[l], start_pos, lbs[l], w_in[l], w_o[l], hg_norm[l], pool_w[l], pool_scale[l])
        S_out.append(S)
        buf_out.append(b)
        x = x + y
        h = rmsnorm(x, norm_ffn[l])
        if l % 2 == 0:
            j = l // 2
            x = x + swiglu(h, ffn_w_gate[j], ffn_w_up[j], ffn_w_down[j])
        else:
            j = l // 2
            x = x + moe(h, router[j], moe_w_gate[j], moe_w_up[j], moe_w_down[j])
    return rmsnorm(x, norm_final), jnp.stack(S_out), jnp.stack(buf_out)

def setup_inputs(seed: int = 0) -> dict:
    key = jax.random.key(seed)
    ks = jax.random.split(key, 24)
    f32 = jnp.float32

    def nrm(k, shape, scale):
        return jax.random.normal(k, shape, f32) * scale

    return {
        "x_prompt": nrm(ks[0], (BATCH, SEQ, D_MODEL), 1.0),
        "x_sample": nrm(ks[1], (DEC_BATCH, DEC_SEQ, D_MODEL), 1.0),
        "state_hgrn": nrm(ks[2], (DEPTH, DEC_BATCH, HG_HEADS, HG_DK, HG_DV), 0.5),
        "state_pool": nrm(ks[3], (DEPTH, DEC_BATCH, POOL_BUF, POOL_WIDTH), 1.0),
        "lb_logits": nrm(ks[4], (DEPTH, HG_WIDTH), 0.5),
        "norm_mix": 1.0 + nrm(ks[5], (DEPTH, D_MODEL), 0.02),
        "w_in": nrm(ks[6], (DEPTH, D_MODEL, IN_WIDTH), D_MODEL ** -0.5),
        "w_o": nrm(ks[7], (DEPTH, MIX_WIDTH, D_MODEL), MIX_WIDTH ** -0.5),
        "hg_norm": 1.0 + nrm(ks[8], (DEPTH, HG_WIDTH), 0.02),
        "pool_w": nrm(ks[9], (DEPTH, POOL_GROUPS, POOL_GROUP_W, POOL_GROUP_W), POOL_GROUP_W ** -0.5),
        "pool_scale": 1.0 + nrm(ks[10], (DEPTH, POOL_WIDTH), 0.1),
        "norm_ffn": 1.0 + nrm(ks[11], (DEPTH, D_MODEL), 0.02),
        "ffn_w_gate": nrm(ks[12], (N_DENSE, D_MODEL, D_FF), D_MODEL ** -0.5),
        "ffn_w_up": nrm(ks[13], (N_DENSE, D_MODEL, D_FF), D_MODEL ** -0.5),
        "ffn_w_down": nrm(ks[14], (N_DENSE, D_FF, D_MODEL), D_FF ** -0.5),
        "router": nrm(ks[15], (N_MOE, D_MODEL, N_EXPERTS), D_MODEL ** -0.5),
        "moe_w_gate": nrm(ks[16], (N_MOE, N_EXPERTS, D_MODEL, D_FF_E), D_MODEL ** -0.5),
        "moe_w_up": nrm(ks[17], (N_MOE, N_EXPERTS, D_MODEL, D_FF_E), D_MODEL ** -0.5),
        "moe_w_down": nrm(ks[18], (N_MOE, N_EXPERTS, D_FF_E, D_MODEL), D_FF_E ** -0.5),
        "norm_final": 1.0 + nrm(ks[19], (D_MODEL,), 0.02),
    }

def reference(x_prompt, x_sample, state_hgrn, state_pool, lb_logits, norm_mix, w_in, w_o, hg_norm, pool_w,
              pool_scale, norm_ffn, ffn_w_gate, ffn_w_up, ffn_w_down, router, moe_w_gate, moe_w_up, moe_w_down,
              norm_final):
    B = x_prompt.shape[0]
    S_zero = jnp.zeros((DEPTH, B, HG_HEADS, HG_DK, HG_DV), state_hgrn.dtype)
    buf_zero = jnp.zeros((DEPTH, B, POOL_BUF, POOL_WIDTH), state_pool.dtype)
    y_prompt, new_hgrn_prompt, new_pool_prompt = trunk(
        x_prompt, S_zero, buf_zero, 0, lb_logits, norm_mix, w_in, w_o, hg_norm, pool_w, pool_scale,
        norm_ffn, ffn_w_gate, ffn_w_up, ffn_w_down, router, moe_w_gate, moe_w_up, moe_w_down, norm_final)
    y_sample, new_hgrn_sample, new_pool_sample = trunk(
        x_sample, state_hgrn, state_pool, PAST_LEN, lb_logits, norm_mix, w_in, w_o, hg_norm, pool_w, pool_scale,
        norm_ffn, ffn_w_gate, ffn_w_up, ffn_w_down, router, moe_w_gate, moe_w_up, moe_w_down, norm_final)
    return (y_prompt, y_sample, new_hgrn_prompt, new_hgrn_sample, new_pool_prompt, new_pool_sample)


_drawn_inputs = setup_inputs


def setup_inputs(seed=0):
    import zlib

    import numpy as np

    out = dict(_drawn_inputs(seed))
    spreads = {}
    factors = {'hg_norm': 4.005, 'norm_final': 8.009, 'norm_ffn': 3.549}
    for name, (base, spread) in spreads.items():
        noise = np.random.default_rng([zlib.crc32(name.encode()), seed]).standard_normal(out[name].shape)
        drawn = base * np.exp(spread * noise) if base else spread * noise
        out[name] = __import__('jax').numpy.asarray(drawn.astype(out[name].dtype))
    for name, factor in factors.items():
        out[name] = (out[name] * factor).astype(out[name].dtype)
    return out
```

```python
import concourse.bass as bass
from concourse import mybir
from contextlib import ExitStack

D_MODEL = 1024
SEQ = 256
DEC = 8
DEPTH = 2
T = SEQ + DEC
KT = D_MODEL // 128
HEADS = 4
HG_WIDTH = HEADS * 128
IN_WIDTH = 5 * HG_WIDTH
POOL_BUF = 15
WINDOWS = (2, 4, 8, 16)
D_FF = 2816
FT = D_FF // 128
N_EXPERTS = 8
D_FF_E = 1408
FE = D_FF_E // 128
EPS = 1e-6
CAP = 128
SEG = 128
TOKEN_TILES = ((0, 128), (128, 128), (256, DEC))
LEVELS = (1, 2, 4, 8, 16, 32, 64)
PAD = 16

C_IDENT, C_ONES, C_BEFORE, C_IOTA = 0, 128, 256, 384
C_MASK = 512
C_CORR = C_MASK + 128 * (1 + len(LEVELS))
C_PICK = C_CORR + 4 * PAD
C_LOWER = C_PICK + 4 * DEC
C_COLS = C_LOWER + N_EXPERTS * N_EXPERTS

V_MIX, V_FFN, V_FINAL, V_LB, V_HG, V_POOL = 0, 16, 32, 40, 48, 56
V_COLS = 64

RING = 4
PASSES = []
_n = 0
for _name, _units, _kts in (("in0", 20, KT), ("out0", 8, KT), ("ffn_up0", 2 * FT, KT), ("ffn_down0", 16, FT // 2),
                            ("in1", 20, KT), ("out1", 8, KT)):
    PASSES.append((_name, _n, _units, _kts))
    _n += _units
PASS = {p[0]: p for p in PASSES}
IN0 = [PASS["in0"][1], PASS["in1"][1]]
WO0 = [PASS["out0"][1], PASS["out1"][1]]
GU0 = PASS["ffn_up0"][1]
DN0 = PASS["ffn_down0"][1]
LAST_UNIT = _n

RAW_RING = 9
SPLIT_RING = 3
HEAD_UNITS = 2 * KT
TURN_UNITS = 2 * KT + FE
LOAD_AHEAD = 2


def build_program(nc, a, o):
    f32 = mybir.dt.float32
    f32r = mybir.dt.float32r
    i32 = mybir.dt.int32
    ALU = mybir.AluOpType
    ACT = mybir.ActivationFunctionType
    AX = mybir.AxisListType
    ds = bass.ds

    ctx = ExitStack()
    with ctx:
        def sb(name, shape, dt=f32):
            return ctx.enter_context(nc.sbuf_tensor("sb_" + name, shape, dt))

        def sem(name):
            return ctx.enter_context(nc.semaphore(name))

        consts = sb("consts", [128, C_COLS])
        ident = consts[:, C_IDENT:C_IDENT + 128]
        ones = consts[:, C_ONES:C_ONES + 128]
        before = consts[:, C_BEFORE:C_BEFORE + 128]
        iota = consts[:, C_IOTA:C_IOTA + 128]
        corr = consts[:, C_CORR:C_CORR + 4 * PAD].rearrange("p (g t) -> p g t", g=4)
        pick = consts[:, C_PICK:C_PICK + 4 * DEC].rearrange("p (g b) -> p g b", g=4)
        xT = sb("xT", [128, KT, T])
        vecs = sb("vecs", [128, V_COLS])
        vec_rows = sb("vec_rows", [V_COLS, 128])
        lbound = sb("lbound", [128, DEPTH, HEADS])
        lspan = sb("lspan", [128, DEPTH, HEADS])
        lb_tmp = sb("lb_tmp", [128, 4, HEADS])
        eps = sb("eps", [128, 1])
        root = sb("root", [128, T])
        rstd = sb("rstd", [128, T])
        pool_w = sb("pool_w", [128, 4, 128])
        raw = [sb(f"raw{i}", [128, FE, 128]) for i in range(RING)]
        w_hi = [sb(f"w_hi{i}", [128, FE, 128], f32r) for i in range(RING)]
        w_lo = [sb(f"w_lo{i}", [128, FE, 128], f32r) for i in range(RING)]
        router = sb("router", [128, KT, N_EXPERTS])
        logits = sb("logits", [128, 3, N_EXPERTS])
        rank = sb("rank", [128, 3, N_EXPERTS])
        first = sb("first", [128, 3, N_EXPERTS])
        second = sb("second", [128, 3, N_EXPERTS])
        chosen = sb("chosen", [128, 3, N_EXPERTS])
        picked = sb("picked", [128, 3, N_EXPERTS])
        tops = sb("tops", [128, 4, 3])
        gates = sb("gates", [128, 3, N_EXPERTS])
        slot = sb("slot", [128, 3, N_EXPERTS])
        over = sb("over", [128, 3, N_EXPERTS])
        slot_gate = sb("slot_gate", [128, N_EXPERTS])
        longest = sb("longest", [128, 1])
        longest_i = sb("longest_i", [128, 1], i32)
        arena_base = (nc.sbuf_base + 31) // 32 * 32
        arena_end = nc.sbuf_usable_end

        def at(name, shape, offset, dt=f32):
            size = 4
            for n in shape[1:]:
                size *= n
            assert arena_base + offset + size <= arena_end, (name, arena_base + offset + size - arena_end)
            return nc.alloc_sbuf_tensor_at("at_" + name, shape, dt, offset=arena_base + offset)

        act_hi = at("act_hi", [128, KT, T], 0, f32r)
        act_lo = at("act_lo", [128, KT, T], 8448, f32r)
        values = at("values", [128, 2, HG_WIDTH], 0)
        kdecT = at("kdecT", [128, 2, HG_WIDTH], 4096)
        hgo = at("hgo", [128, HEADS, T], 8192)
        hgo_sq = at("hgo_sq", [128, HEADS, T], 12416)
        state = at("state", [128, DEC, HEADS, 128], 16896)
        proj = at("proj", [128, 4, HEADS, T], 33280)
        mix_hi = at("mix_hi", [128, KT, T], 50176, f32r)
        mix_lo = at("mix_lo", [128, KT, T], 58624, f32r)
        up = at("up", [128, 4, PAD + T], 67072)
        win_a = at("win_a", [128, 4, PAD + T], 71552)
        win_b = at("win_b", [128, 4, PAD + T], 76032)
        sig = at("sig", [128, HEADS, T], 80512)
        keys = at("keys", [128, HEADS, T], 84736)
        logf = at("logf", [128, HEADS, SEQ], 88960)
        kdec = at("kdec", [128, HEADS, SEQ], 88960)
        decay = at("decay", [128, HEADS, SEQ], 93056)
        diff = [at(f"diff{i}", [128, HEADS, SEQ], 97152 + 4096 * i) for i in range(2)]
        sided = [at(f"sided{i}", [128, HEADS, SEQ], 105344 + 4096 * i) for i in range(2)]
        scores = at("scores", [128, 2, HEADS, SEG], 113536)
        scores_x = at("scores_x", [128, HEADS, SEG], 117632)
        pool_past = at("pool_past", [DEC * POOL_BUF, HG_WIDTH], 119680)
        segments = at("segments", [128, HEADS, SEQ], 109440)
        hg_rstd = at("hg_rstd", [128, HEADS, T], 97152)
        hg_tmp = at("hg_tmp", [128, HEADS, T], 101376)
        new_state = at("new_state", [128, HEADS, 128], 105600)
        pool_tail = at("pool_tail", [POOL_BUF + DEC, HG_WIDTH], 80512)
        square = at("square", [128, KT, T], 84736)
        x_rows = at("x_rows", [128, 3, D_MODEL], 97152)
        ffn_hi = at("ffn_hi", [128, FT, T], 33280, f32r)
        ffn_lo = at("ffn_lo", [128, FT, T], 56512, f32r)
        gate_in = [at(f"gate_in{i}", [128, T], 93440 + 1056 * i) for i in range(2)]
        gate_act = [at(f"gate_act{i}", [128, T], 95552 + 1056 * i) for i in range(2)]
        up_in = [at(f"up_in{i}", [128, T], 97664 + 1056 * i) for i in range(2)]
        packed = at("packed", [128, N_EXPERTS, 2, KT * CAP], 0, f32r)
        slot_hot = at("slot_hot", [128, N_EXPERTS, T], 65536, f32r)
        act_e = at("act_e", [128, D_FF_E], 73984)
        hid_hi = at("hid_hi", [128, FE, CAP], 79616, f32r)
        hid_lo = at("hid_lo", [128, FE, CAP], 85248, f32r)
        raw_e = raw + [at(f"raw_e{i}", [128, FE, 128], 90880 + 5632 * i) for i in range(RAW_RING - RING)]
        x_hi, x_lo = w_hi[3][:, 0:KT, :], w_lo[3][:, 0:KT, :]
        square_m = at("square_m", [128, KT, T], 33280)
        h_hi = at("h_hi", [128, 3, D_MODEL], 73984, f32r)
        scaled_m = at("scaled_m", [128, KT, T], 88960)
        h_lo = at("h_lo", [128, 3, D_MODEL], 97408, f32r)
        token_hot = at("token_hot", [128, 3, N_EXPERTS, CAP], 109696, f32r)
        greater = at("greater", [128, 3, N_EXPERTS, N_EXPERTS], 41728)
        equal = at("equal", [128, 3, N_EXPERTS, N_EXPERTS], 42496)
        h_all = at("h_all", [128, KT, T], 0)
        gate_w_all = at("gate_w_all", [128, KT, 128], 8448)
        up_w_all = at("up_w_all", [128, KT, 128], 12544)
        down_w_all = at("down_w_all", [128, D_MODEL], 16640)
        act_all = at("act_all", [128, T], 20736)
        over_all = at("over_all", [128, T], 21792)
        over_col = at("over_col", [128, 3], 22848)
        square_f = at("square_f", [128, KT, T], 90880)
        scaled_f = at("scaled_f", [128, KT, T], 99328)
        y_rows = at("y_rows", [128, 3, D_MODEL], 107776)

        h_saved = nc.dram_tensor("h_saved", (128, KT * T), f32).ap()
        bank = [ctx.enter_context(nc.psum_tensor(f"bank{i}", [128, 512], f32)) for i in range(8)]

        consts_in = sem("consts_in"); vecs_in = sem("vecs_in"); x_in = sem("x_in")
        state_in = sem("state_in"); past_in = sem("past_in"); pool_w_in = sem("pool_w_in")
        raw_full = [sem(f"raw_full{i}") for i in range(RING)]
        hi_done = sem("hi_done"); lo_done = sem("lo_done"); unit_used = sem("unit_used"); bank_read = sem("bank_read")
        vecs_turned = sem("vecs_turned"); vecs_ready = sem("vecs_ready"); lb_step = sem("lb_step"); lb_exp = sem("lb_exp")
        eps_set = sem("eps_set")
        x_turned = sem("x_turned"); x_loaded = sem("x_loaded")
        squared = sem("squared"); norm_hi = sem("norm_hi"); norm_lo = sem("norm_lo"); summed = sem("summed")
        rooted = sem("rooted"); rstd_done = sem("rstd_done")
        sig_done = sem("sig_done"); q_gated = sem("q_gated"); forget_done = sem("forget_done"); keys_done = sem("keys_done")
        g_gated = sem("g_gated"); logf_done = sem("logf_done"); decay_done = sem("decay_done"); segments_set = sem("segments_set")
        scores_zeroed = sem("scores_zeroed"); diff_done = sem("diff_done"); diff_exp = sem("diff_exp"); sided_done = sem("sided_done")
        scored = sem("scored"); scores_taken = sem("scores_taken")
        v_turned = sem("v_turned"); v_copied = sem("v_copied")
        state_decayed = sem("state_decayed"); v_spread = sem("v_spread"); state_done = sem("state_done"); state_out = sem("state_out")
        attended = sem("attended"); hgo_copied = sem("hgo_copied")
        end_exp = sem("end_exp"); kdec_done = sem("kdec_done"); kdec_turned = sem("kdec_turned"); kdec_copied = sem("kdec_copied")
        final_state = sem("final_state"); final_copied = sem("final_copied"); final_out = sem("final_out")
        hgo_squared = sem("hgo_squared"); hgo_summed = sem("hgo_summed"); hgo_rooted = sem("hgo_rooted"); hgo_rstd = sem("hgo_rstd")
        hgo_scaled = sem("hgo_scaled"); mix_hi_done = sem("mix_hi_done"); mix_lo_done = sem("mix_lo_done")
        pads_zeroed = sem("pads_zeroed"); windowed = sem("windowed"); past_summed = sem("past_summed"); past_added = sem("past_added")
        pooled = sem("pooled"); pool_mapped = sem("pool_mapped"); pool_hi = sem("pool_hi"); pool_lo = sem("pool_lo")
        tail_turned = sem("tail_turned"); tail_copied = sem("tail_copied"); tail_out = sem("tail_out"); shift_out = sem("shift_out")
        gate_scaled = sem("gate_scaled"); gate_done = sem("gate_done"); up_scaled = sem("up_scaled"); ffn_mult = sem("ffn_mult")
        ffn_hi_done = sem("ffn_hi_done"); ffn_lo_done = sem("ffn_lo_done")
        x_moe = sem("x_moe"); moe_added = sem("moe_added"); scaled_done = sem("scaled_done"); turned = sem("turned"); y_copied = sem("y_copied"); y_out = sem("y_out")

        router_in = sem("router_in"); logits_zeroed = sem("logits_zeroed"); routed = sem("routed"); route = sem("route"); route_exp = sem("route_exp")
        placed = sem("placed"); hot = sem("hot"); hot_turned = sem("hot_turned"); hot_copied = sem("hot_copied")
        h_turned = sem("h_turned"); h_hi_done = sem("h_hi_done"); h_lo_done = sem("h_lo_done"); h_out = sem("h_out")
        gathered = sem("gathered"); packed_hi = sem("packed_hi"); packed_lo = sem("packed_lo"); gate_slots = sem("gate_slots")
        moe_full = [sem(f"moe_full{i}") for i in range(RAW_RING)]
        moe_hi = sem("moe_hi"); moe_lo = sem("moe_lo"); moe_used = sem("moe_used")
        x_hi_set = sem("x_hi_set"); x_lo_set = sem("x_lo_set"); gate_silu = sem("gate_silu"); act_done = sem("act_done")
        hid_turned = sem("hid_turned"); hid_hi_done = sem("hid_hi_done"); hid_lo_done = sem("hid_lo_done")
        y_hi_done = sem("y_hi_done"); y_lo_done = sem("y_lo_done"); scattered = sem("scattered")
        all_in = sem("all_in"); all_w = sem("all_w"); all_spread = sem("all_spread"); all_col = sem("all_col")
        all_over = sem("all_over"); all_up = sem("all_up"); all_silu = sem("all_silu"); all_act = sem("all_act"); all_down = sem("all_down"); all_added = sem("all_added")

        def unit_source(name, it, s):
            layer = int(name[-1])
            if name[:2] == "in":
                w, col = a["w_in"][layer], ds(it * 512 + s * 128, 128)
            elif name[:3] == "out":
                w, col = a["w_o"][layer], ds(it * 512 + s * 128, 128)
            elif name[:6] == "ffn_up":
                w, col = (a["ffn_w_gate"], a["ffn_w_up"])[s % 2][0], ds(it * 256 + (s // 2) * 128, 128)
            else:
                half = s % 2
                w, col = a["ffn_w_down"][0, half * D_FF_E:(half + 1) * D_FF_E, :], ds(it * 256 + (s // 2) * 128, 128)
            return w[:, col].rearrange("(k p) n -> p k n", p=128)

        def wait_x(eng, version, kt):
            if version == 0:
                eng.wait_ge(x_loaded, kt + 1)
            elif version in (1, 3):
                eng.wait_ge(bank_read, WO0[(version - 1) // 2] + kt + 1)
            elif version == 2:
                eng.wait_ge(bank_read, DN0 + 2 * kt + 2)
            else:
                eng.wait_ge(x_moe, kt + 1)

        TURN = [("gate", 1, k) for k in range(KT)] + [("down", 0, k) for k in range(FE)] + [("up", 1, k) for k in range(KT)]
        PIECES = ((0, 512), (512, 512), (1024, 384))
        ROUTED = 29

        block = ctx.enter_context(nc.Block())

        @block.sync
        def _(sp):
            for name, n0, units, kts in PASSES:
                def load(it, s, check=True):
                    if check:
                        sp.wait_ge(lo_done, n0 + 4 * it + s - 3)
                    sp.dma_start(raw[s][:, 0:kts, :], unit_source(name, it, s)).then_inc(raw_full[s], 16)
                first = 0
                if n0 == 0:
                    for s in range(RING):
                        load(0, s, check=False)
                    first = 1
                with sp.Fori(first, units // RING) as it:
                    for s in range(RING):
                        load(it, s)
                if name == "out0":
                    sp.wait_ge(state_out, 16)
                    for i in range(4):
                        sp.dma_start(state[:, 2 * i:2 * i + 2, :, :].rearrange("k b h v -> k (b h) v"),
                                     a["state_hgrn"][1, 2 * i:2 * i + 2].rearrange("b h k v -> k (b h) v")).then_inc(state_in, 16)
                    sp.wait_ge(pool_mapped, 4)
                    sp.dma_start(pool_w[:, :, :], a["pool_w"][1].rearrange("g c d -> c g d")).then_inc(pool_w_in, 16)
                    sp.dma_start(pool_past[:, :], a["state_pool"][1].rearrange("b r c -> (b r) c")).then_inc(past_in, 16)
            def load_e(j, e, kind, k, turn=None):
                u = j if turn is None else HEAD_UNITS + TURN_UNITS * turn + j
                slot_n = (j if turn is None else HEAD_UNITS + j) % RAW_RING
                if turn is None and j < RAW_RING:
                    if j < RING:
                        sp.wait_ge(lo_done, LAST_UNIT - RING + j + 1)
                    else:
                        sp.wait_ge(packed_lo, 16)
                        sp.wait_ge(h_out, 16)
                else:
                    sp.wait_ge(moe_lo, u - RAW_RING + 1)
                w = a["moe_w_" + kind][0]
                src = w[ds(e, 1), 128 * k:128 * (k + 1), :].rearrange("a p n -> p (a n)")
                dst = raw_e[slot_n][:, :, :].rearrange("p a b -> p (a b)")[:, 0:src.shape[1]]
                sp.dma_start(dst, src).then_inc(moe_full[slot_n], 16)
            for j in range(HEAD_UNITS):
                load_e(j, 0, ("gate", "up")[j // KT], j % KT)
            with sp.Fori(0, N_EXPERTS - 1) as e:
                for j, (kind, ahead, k) in enumerate(TURN):
                    load_e(j, e + ahead, kind, k, turn=e)
            for j in range(FE):
                load_e(j, N_EXPERTS - 1, "down", j, turn=N_EXPERTS - 1)
            sp.wait_ge(scattered, 8)
            sp.wait_ge(route, ROUTED)
            n_rows = sp.value_load(longest_i[0:1, 0:1])
            with sp.If(n_rows > CAP):
                sp.wait_ge(y_lo_done, 2 * N_EXPERTS + 1)
                sp.dma_start(h_all[:, :, :].rearrange("p k t -> p (k t)"), h_saved).then_inc(all_in, 16)
                with sp.Fori(0, N_EXPERTS) as e:
                    with sp.Fori(0, FE) as f:
                        n = e * FE + f
                        sp.wait_ge(all_added, n * KT + KT)
                        for dst, name in ((gate_w_all, "moe_w_gate"), (up_w_all, "moe_w_up")):
                            sp.dma_start(dst[:, :, :], a[name][0][ds(e, 1), :, ds(f * 128, 128)].rearrange("a (k p) n -> p (a k) n", p=128)).then_inc(all_w, 16)
                        sp.dma_start(down_w_all[:, :], a["moe_w_down"][0][ds(e, 1), ds(f * 128, 128), :].rearrange("a p n -> p (a n)")).then_inc(all_w, 16)
            sp.end_ifs()
            sp.wait_ge(y_out, 16 * 3)

        @block.gpsimd
        def _(gp):
            gp.dma_start(o["new_pool_sample"][:, :, 0:POOL_BUF - 1, :], a["state_pool"][:, :, 1:POOL_BUF, :]).then_inc(shift_out, 16)
            gp.memset(eps[:, :], EPS).then_inc(eps_set, 1)

            def square_x(version, out):
                if version:
                    gp.wait_ge(summed, version)
                for kt in range(KT):
                    wait_x(gp, version, kt)
                    gp.tensor_tensor(out[:, kt, :], xT[:, kt, :], xT[:, kt, :], ALU.mult).then_inc(squared, 1)

            for layer in range(DEPTH):
                L = layer
                if layer == 0:
                    square_x(0, square)
                gp.wait_ge(unit_used, IN0[L] + 1)
                gp.memset(up[:, :, 0:PAD], 0.0).then_inc(pads_zeroed, 1)
                gp.wait_ge(x_loaded, KT)
                gp.memset(scores[:, :, :, :], 0.0).then_inc(scores_zeroed, 1)
                gp.memset(segments[:, :, :], 1.0).then_inc(segments_set, 1)
                gp.wait_ge(segments_set, 2 * L + 1)
                gp.memset(segments[:, :, :].rearrange("p h (s t) -> p (h s) t", t=SEG)[:, :, 0:1], 0.0).then_inc(segments_set, 1)
                gp.wait_ge(forget_done, 4 * (L + 1))
                gp.tensor_scalar(keys[:, :, :], proj[:, 1, :, :], -1.0, 1.0, ALU.mult, ALU.add).then_inc(keys_done, 1)
                gp.wait_ge(state_in, 64 * (L + 1))
                for h in range(HEADS):
                    fs = proj[:, 1, h, SEQ:T].unsqueeze(2).broadcast_to([128, DEC, 128])
                    gp.tensor_tensor(state[:, :, h, :], state[:, :, h, :], fs, ALU.mult).then_inc(state_decayed, 1)
                gp.wait_ge(decay_done, L + 1)
                for j, half in enumerate(LEVELS + (SEG,)):
                    if j >= 2:
                        gp.wait_ge(sided_done, 16 * L + 2 * (j - 1))
                    b = decay[:, :, :].rearrange("p h (n t) -> p (h n) t", t=2 * half)
                    d = diff[j % 2][:, :, :].rearrange("p h (n t) -> p (h n) t", t=2 * half)
                    width = 2 * half if half < SEG else half
                    n = HEADS * SEQ // (2 * half)
                    gp.tensor_tensor(d[:, :, 0:width], b[:, :, 0:width],
                                     b[:, :, half - 1:half].broadcast_to([128, n, width]), ALU.subtract).then_inc(diff_done, 1)
                gp.wait_ge(bank_read, IN0[L] + 20)
                src, dst = up, win_a
                for j in range(4):
                    back = 1 << j
                    lo = 2 * back - 1
                    if j:
                        gp.wait_ge(windowed, 8 * L + j)
                    gp.tensor_tensor(dst[:, j:, lo:PAD + SEQ], src[:, j:, lo:PAD + SEQ],
                                     src[:, j:, lo - back:PAD + SEQ - back], ALU.add).then_inc(windowed, 1)
                    src, dst = dst, (win_b if dst is win_a else win_a)
                for g in range(4):
                    w = (win_a, win_b)[g % 2]
                    gp.wait_ge(windowed, 8 * L + 4)
                    gp.tensor_tensor(w[:, g, PAD:2 * PAD], w[:, g, PAD:2 * PAD], corr[:, g, :], ALU.mult).then_inc(windowed, 1)
                gp.wait_ge(sided_done, 16 * L + 16)
                gp.tensor_tensor(diff[0][:, :, SEG:SEQ], decay[:, :, SEG:SEQ],
                                 decay[:, :, SEQ - 1:SEQ].broadcast_to([128, HEADS, SEG]), ALU.subtract).then_inc(diff_done, 1)
                gp.wait_ge(state_done, 32 * (L + 1))
                gp.dma_start(o["new_hgrn_sample"][layer].rearrange("b h k v -> k (b h) v"),
                             state[:, :, :, :].rearrange("k b h v -> k (b h) v")).then_inc(state_out, 16)
                gp.wait_ge(tail_copied, L + 1)
                gp.dma_start(o["new_pool_prompt"][layer, 0], pool_tail[0:POOL_BUF, :]).then_inc(tail_out, 16)
                gp.dma_start(o["new_pool_sample"][layer, :, POOL_BUF - 1, :], pool_tail[POOL_BUF:, :]).then_inc(tail_out, 16)
                gp.wait_ge(hgo_copied, 3 * (L + 1))
                gp.tensor_tensor(hgo_sq[:, :, :], hgo[:, :, :], hgo[:, :, :], ALU.mult).then_inc(hgo_squared, 1)
                gp.wait_ge(final_copied, L + 1)
                gp.dma_start(o["new_hgrn_prompt"][layer, 0].rearrange("h k v -> k h v"), new_state[:, :, :]).then_inc(final_out, 16)
                gp.wait_ge(final_out, 16 * (L + 1))
                gp.wait_ge(tail_out, 32 * (L + 1))
                gp.wait_ge(state_out, 16 * (L + 1))
                if layer == 0:
                    square_x(1, square)
                    square_x(2, square)
            gp.memset(logits[:, :, :], 0.0).then_inc(logits_zeroed, 1)
            square_x(3, square_m)
            def set_x_lo(e, c, u):
                gp.wait_ge(packed_lo, 16)
                if u is None:
                    gp.wait_ge(unit_used, LAST_UNIT)
                else:
                    gp.wait_ge(moe_used, u)
                src = packed[:, ds(e, 1), 1, 512 * c:512 * (c + 1)].rearrange("p a n -> p (a n)")
                gp.tensor_copy(x_lo[:, 4 * c:4 * (c + 1), :].rearrange("p a b -> p (a b)"), src).then_inc(x_lo_set, 1)
            set_x_lo(0, 0, None)
            set_x_lo(0, 1, None)
            set_x_lo(1, 0, HEAD_UNITS - 4)
            with gp.Fori(0, N_EXPERTS - 2) as e:
                set_x_lo(e + 1, 1, HEAD_UNITS + TURN_UNITS * e)
                set_x_lo(e + 2, 0, HEAD_UNITS + TURN_UNITS * (e + 1) - 4)
            set_x_lo(N_EXPERTS - 1, 1, HEAD_UNITS + TURN_UNITS * (N_EXPERTS - 2))
            square_x(4, square_f)
            gp.wait_ge(shift_out, 16)

        @block.scalar
        def _(act):
            act.dma_start(consts[:, :], a["consts"]).then_inc(consts_in, 16)
            act.dma_start(x_rows[:, 0:2, :], a["x_prompt"][0].rearrange("(i p) d -> p i d", p=128)).then_inc(x_in, 16)
            act.dma_start(x_rows[0:DEC, 2, :], a["x_sample"][:, 0, :]).then_inc(x_in, 16)
            for row, name, src in ((V_MIX, "norm_mix", "l (k p) -> (l k) p"), (V_FFN, "norm_ffn", "l (k p) -> (l k) p"),
                                   (V_FINAL, "norm_final", "(k p) -> k p"), (V_LB, "lb_logits", "l (k p) -> (l k) p"),
                                   (V_HG, "hg_norm", "l (k p) -> (l k) p"), (V_POOL, "pool_scale", "l (k p) -> (l k) p")):
                view = a[name].rearrange(src, p=128)
                act.dma_start(vec_rows[row:row + view.shape[0], :], view).then_inc(vecs_in, 16)
            act.dma_start(pool_past[:, :], a["state_pool"][0].rearrange("b r c -> (b r) c")).then_inc(past_in, 16)
            act.dma_start(pool_w[:, :, :], a["pool_w"][0].rearrange("g c d -> c g d")).then_inc(pool_w_in, 16)
            for i in range(4):
                act.dma_start(state[:, 2 * i:2 * i + 2, :, :].rearrange("k b h v -> k (b h) v"),
                              a["state_hgrn"][0, 2 * i:2 * i + 2].rearrange("b h k v -> k (b h) v")).then_inc(state_in, 16)
            act.dma_start(router[:, :, :], a["router"][0].rearrange("(k p) e -> p k e", p=128)).then_inc(router_in, 16)
            act.wait_ge(lb_step, 3)
            act.activation(lb_tmp[:, 1:3, :], lb_tmp[:, 1:3, :], ACT.Exp).then_inc(lb_exp, 1)

            def split(s, k, n, kts, guard=True):
                act.wait_ge(raw_full[s], 16 * (k + 1))
                if guard:
                    act.wait_ge(unit_used, n - 3)
                act.activation(w_hi[s][:, 0:kts, :], raw[s][:, 0:kts, :], ACT.Copy).then_inc(hi_done, 1)

            def weight_pass(name, body, unroll=False):
                i = [p[0] for p in PASSES].index(name)
                _, n0, units, kts = PASSES[i]
                its = units // RING

                def step(it, last):
                    for s in range(RING):
                        n = n0 + 4 * it + s
                        if s == 0:
                            split(3, n0 // 4 + it, n + 3, kts, guard=not (n0 == 0 and isinstance(it, int) and it == 0))
                        elif not last:
                            split(s - 1, n0 // 4 + it + 1, n + 3, kts)
                        elif i + 1 < len(PASSES):
                            split(s - 1, PASSES[i + 1][1] // 4, PASSES[i + 1][1] + s - 1, PASSES[i + 1][3])
                        if body:
                            body(it, s)
                first = 0
                if n0 == 0:
                    for s in range(3):
                        split(s, 0, s, kts, guard=False)
                    step(0, False)
                    first = 1
                if unroll:
                    for it in range(first, its - 1):
                        step(it, False)
                else:
                    with act.Fori(first, its - 1) as it:
                        step(it, False)
                step(its - 1, True)

            def scale_x(version, col):
                for kt in range(KT):
                    wait_x(act, version, kt)
                    act.activation(act_hi[:, kt, :], xT[:, kt, :], ACT.Copy, scale=vecs[:, col + kt:col + kt + 1]).then_inc(norm_hi, 1)

            def root_of_mean(version, columns):
                act.wait_ge(summed, version + 1)
                act.activation(root[:, 0:columns], bank[4][:, 0:columns], ACT.Sqrt, scale=1.0 / D_MODEL, bias=eps[:, :]).then_inc(rooted, 1)

            act.wait_ge(vecs_ready, 1)
            act.wait_ge(eps_set, 1)
            scale_x(0, V_MIX)
            root_of_mean(0, T)
            for layer in range(DEPTH):
                L = layer
                if layer:
                    scale_x(2, V_MIX + KT)
                    root_of_mean(2, T)

                def mixer_step(it, s):
                    if s != RING - 1:
                        return
                    if it == 1:
                        act.wait_ge(bank_read, IN0[L] + 4)
                        act.activation(sig[:, :, :], proj[:, 0, :, :], ACT.Sigmoid).then_inc(sig_done, 1)
                    if it == 2:
                        act.wait_ge(bank_read, IN0[L] + 8)
                        act.activation(proj[:, 1, :, :], proj[:, 1, :, :], ACT.Sigmoid).then_inc(sig_done, 1)
                    if it == 4:
                        act.wait_ge(bank_read, IN0[L] + 16)
                        act.wait_ge(q_gated, L + 1)
                        act.activation(sig[:, :, :], proj[:, 3, :, :], ACT.Sigmoid).then_inc(sig_done, 1)
                weight_pass(f"in{L}", mixer_step, unroll=True)
                act.wait_ge(forget_done, 4 * (L + 1))
                act.activation(logf[:, :, :], proj[:, 1, :, 0:SEQ], ACT.Ln).then_inc(logf_done, 1)
                for i in range(2):
                    act.wait_ge(v_turned, 2 * L + i + 1)
                    act.activation(values[:, i, :], bank[6 + i][:, :], ACT.Copy).then_inc(v_copied, 1)
                for j, half in enumerate(LEVELS + (SEG,)):
                    act.wait_ge(diff_done, 9 * L + j + 1)
                    d = diff[j % 2][:, :, :].rearrange("p h (n t) -> p (h n) t", t=2 * half)
                    right = d if half < SEG else decay[:, :, :].rearrange("p h (n t) -> p (h n) t", t=2 * half)
                    act.activation(d[:, :, 0:half], d[:, :, 0:half], ACT.Exp, scale=-1.0).then_inc(diff_exp, 1)
                    act.activation(d[:, :, half:], right[:, :, half:], ACT.Exp).then_inc(diff_exp, 1)
                for g in range(4):
                    act.wait_ge(pool_mapped, 4 * L + g + 1)
                    act.activation(mix_hi[:, 4 + g, :], bank[2 + g % 2][:, 0:T], ACT.Copy,
                                   scale=vecs[:, V_POOL + 4 * L + g:V_POOL + 4 * L + g + 1]).then_inc(pool_hi, 1)
                act.wait_ge(tail_turned, L + 1)
                act.wait_ge(g_gated, L + 1)
                act.activation(pool_tail[:, :], bank[3][0:POOL_BUF + DEC, :], ACT.Copy).then_inc(tail_copied, 1)
                for i in range(2):
                    act.wait_ge(attended, 3 * L + i + 1)
                    act.activation(hgo[:, :, SEG * i:SEG * (i + 1)], bank[6 + i][:, :].rearrange("p (h t) -> p h t", h=HEADS),
                                   ACT.Copy).then_inc(hgo_copied, 1)
                act.wait_ge(attended, 3 * L + 3)
                act.activation(hgo[:, :, SEQ:T], bank[0][:, 0:HEADS * DEC].rearrange("p (h b) -> p h b", h=HEADS), ACT.Copy).then_inc(hgo_copied, 1)
                act.wait_ge(diff_done, 9 * L + 9)
                act.activation(diff[0][:, :, SEG:SEQ], diff[0][:, :, SEG:SEQ], ACT.Exp, scale=-1.0).then_inc(end_exp, 1)
                act.activation(diff[0][:, :, 0:1], decay[:, :, SEQ - 1:SEQ], ACT.Exp).then_inc(end_exp, 1)
                for i in range(2):
                    act.wait_ge(kdec_turned, 2 * L + i + 1)
                    act.activation(kdecT[:, i, :], bank[6 + i][:, :], ACT.Copy).then_inc(kdec_copied, 1)
                act.wait_ge(final_state, L + 1)
                act.activation(new_state[:, :, :], bank[4][:, :].rearrange("p (h v) -> p h v", h=HEADS), ACT.Copy).then_inc(final_copied, 1)
                for i in range(3):
                    act.wait_ge(hgo_summed, 3 * L + i + 1)
                    act.activation(hg_rstd[:, :, :].rearrange("p h t -> p (h t)")[:, 352 * i:352 * (i + 1)],
                                   bank[(5, 0, 1)[i]][:, 0:352], ACT.Sqrt, scale=1.0 / 128, bias=eps[:, :]).then_inc(hgo_rooted, 1)
                for h in range(HEADS):
                    act.wait_ge(hgo_scaled, 8 * L + 4 + h + 1)
                    act.activation(mix_hi[:, h, :], hg_tmp[:, h, :], ACT.Copy).then_inc(mix_hi_done, 1)
                weight_pass(f"out{L}", None)
                if layer == 0:
                    scale_x(1, V_FFN)
                    root_of_mean(1, T)

                    def ffn_step(it, s):
                        i = s // 2
                        if s % 2 == 0:
                            act.wait_ge(bank_read, GU0 + 4 * it + s + 1)
                            act.activation(gate_act[i][:, :], gate_in[i][:, :], ACT.Silu).then_inc(gate_done, 1)
                        else:
                            act.wait_ge(ffn_mult, 2 * it + i + 1)
                            act.activation(ffn_hi[:, ds(2 * it + i, 1), :].rearrange("p a t -> p (a t)"), gate_act[i][:, :], ACT.Copy).then_inc(ffn_hi_done, 1)
                    weight_pass("ffn_up0", ffn_step)
                    weight_pass("ffn_down0", None)
            act.wait_ge(summed, 4)
            for i, (_, rows) in enumerate(TOKEN_TILES):
                act.activation(root[0:rows, i:i + 1], bank[4][0:rows, i:i + 1], ACT.Sqrt, scale=1.0 / D_MODEL, bias=eps[0:rows, :]).then_inc(rooted, 1)
            act.wait_ge(scaled_done, KT)
            act.dma_start(h_saved, scaled_m[:, :, :].rearrange("p k t -> p (k t)")).then_inc(h_out, 16)
            act.wait_ge(tail_out, 64)
            for i, (_, rows) in enumerate(TOKEN_TILES):
                for c in range(2):
                    act.wait_ge(rstd_done, 3 + i + 1)
                    act.wait_ge(h_turned, 2 * i + c + 1)
                    act.activation(h_hi[0:rows, i, 512 * c:512 * (c + 1)], bank[2 + c][0:rows, :], ACT.Copy, scale=rstd[0:rows, i:i + 1]).then_inc(h_hi_done, 1)
                if i == 0:
                    act.wait_ge(route, 18)
                    act.activation(tops[:, 1, :], tops[:, 1, :], ACT.Exp).then_inc(route_exp, 1)
            for e in range(N_EXPERTS):
                act.wait_ge(hot_turned, e + 1)
                act.activation(slot_hot[:, e, :], bank[e % 2][:, 0:T], ACT.Copy).then_inc(hot_copied, 1)
            act.wait_ge(state_out, 32)
            for n in range(16):
                q, d = n // 4, n % 4
                act.wait_ge(gathered, n + 1)
                act.activation(packed[:, 2 * q:2 * q + 2, 0, 256 * d:256 * (d + 1)].rearrange("p e (d s) -> p e d s", d=2),
                               bank[n % 4][:, :].rearrange("p (d e s) -> p e d s", d=2, e=2), ACT.Copy).then_inc(packed_hi, 1)

            def split_e(j, kts_cols, turn=None):
                u = j if turn is None else HEAD_UNITS + TURN_UNITS * turn + j
                jj = j if turn is None else HEAD_UNITS + j
                uses = jj // RAW_RING if turn is None else TURN_UNITS // RAW_RING * turn + jj // RAW_RING
                act.wait_ge(moe_full[jj % RAW_RING], 16 * (uses + 1))
                if turn is None and j < SPLIT_RING:
                    act.wait_ge(unit_used, LAST_UNIT)
                else:
                    act.wait_ge(moe_used, u - SPLIT_RING + 1)
                act.activation(w_hi[jj % SPLIT_RING][:, 0:kts_cols, :], raw_e[jj % RAW_RING][:, 0:kts_cols, :], ACT.Copy).then_inc(moe_hi, 1)

            def set_x_hi(e, c, u):
                act.wait_ge(packed_lo, 16)
                if u is None:
                    act.wait_ge(unit_used, LAST_UNIT)
                else:
                    act.wait_ge(moe_used, u)
                src = packed[:, ds(e, 1), 0, 512 * c:512 * (c + 1)].rearrange("p a n -> p (a n)")
                act.activation(x_hi[:, 4 * c:4 * (c + 1), :].rearrange("p a b -> p (a b)"), src, ACT.Copy).then_inc(x_hi_set, 1)

            def silu_gate(e, u):
                act.wait_ge(moe_used, u)
                if not isinstance(e, int) or e:
                    act.wait_ge(hid_turned, 3 * e)
                for p, (c0, width) in enumerate(PIECES):
                    act.activation(act_e[:, c0:c0 + width], bank[p][:, 0:width], ACT.Silu).then_inc(gate_silu, 1)

            def round_hidden(e):
                for p, (c0, width) in enumerate(PIECES):
                    act.wait_ge(hid_turned, 3 * e + p + 1)
                    act.activation(hid_hi[:, c0 // 128:(c0 + width) // 128, :], bank[3 + p][:, 0:width].rearrange("p (a b) -> p a b", b=128), ACT.Copy).then_inc(hid_hi_done, 1)

            act.wait_ge(y_lo_done, 1)

            def round_result(e, u):
                act.wait_ge(moe_used, u)
                for c in range(2):
                    act.activation(packed[:, ds(e, 1), 0, 512 * c:512 * (c + 1)].rearrange("p a n -> p (a n)"), bank[6 + c][:, :], ACT.Copy,
                                   scale=slot_gate[:, ds(e, 1)]).then_inc(y_hi_done, 1)

            set_x_hi(0, 0, None)
            set_x_hi(0, 1, None)
            for j in range(HEAD_UNITS + LOAD_AHEAD):
                if j < HEAD_UNITS:
                    split_e(j, FE)
                else:
                    split_e(j - HEAD_UNITS, FE, turn=0)
                if j == KT + LOAD_AHEAD:
                    silu_gate(0, KT)
                if j == HEAD_UNITS - 4 + SPLIT_RING - 1:
                    set_x_hi(1, 0, HEAD_UNITS - 4)

            def turn_e(e, last):
                base = HEAD_UNITS + TURN_UNITS * e
                for j, (kind, _, k) in enumerate(TURN):
                    ahead = j + LOAD_AHEAD
                    if ahead < TURN_UNITS:
                        split_e(ahead, FE if TURN[ahead][0] != "down" else KT, turn=e)
                    else:
                        split_e(ahead - TURN_UNITS, KT if last else FE, turn=e + 1)
                    if j == 0:
                        set_x_hi(e + 1, 1, base)
                    if j == 5:
                        round_hidden(e)
                    if j == KT + 1:
                        silu_gate(e + 1, base + KT)
                    if j == KT + FE + 1:
                        round_result(e, base + KT + FE)
                    if j == TURN_UNITS - 3 and not last:
                        set_x_hi(e + 2, 0, base + TURN_UNITS - 4)
            with act.Fori(0, N_EXPERTS - 2) as e:
                turn_e(e, False)
            turn_e(N_EXPERTS - 2, True)
            round_hidden(N_EXPERTS - 1)
            for j in range(LOAD_AHEAD, FE):
                split_e(j, KT, turn=N_EXPERTS - 1)
            round_result(N_EXPERTS - 1, HEAD_UNITS + TURN_UNITS * (N_EXPERTS - 1) + FE)
            act.wait_ge(route, ROUTED)
            n_rows = act.value_load(longest_i[0:1, 0:1])
            with act.If(n_rows > CAP):
                with act.Fori(0, N_EXPERTS * FE) as n:
                    act.wait_ge(all_up, 2 * n + 1)
                    act.activation(act_all[:, :], bank[0][:, 0:T], ACT.Silu).then_inc(all_silu, 1)
            act.end_ifs()
            act.wait_ge(summed, 5)
            for i, (_, rows) in enumerate(TOKEN_TILES):
                act.activation(root[0:rows, i:i + 1], bank[4][0:rows, i:i + 1], ACT.Sqrt, scale=1.0 / D_MODEL, bias=eps[0:rows, :]).then_inc(rooted, 1)
            for i, (_, rows) in enumerate(TOKEN_TILES):
                for c in range(2):
                    act.wait_ge(rstd_done, 6 + i + 1)
                    act.wait_ge(turned, 2 * i + c + 1)
                    act.activation(y_rows[0:rows, i, 512 * c:512 * (c + 1)], bank[5 + (2 * i + c) % 2][0:rows, :], ACT.Copy,
                                   scale=rstd[0:rows, i:i + 1]).then_inc(y_copied, 1)
                act.wait_ge(y_copied, 2 * (i + 1))
                dst = o["y_prompt"][0, 128 * i:128 * (i + 1), :] if i < 2 else o["y_sample"][:, 0, :]
                act.dma_start(dst, y_rows[0:rows, i, :]).then_inc(y_out, 16)
        @block.vector
        def _(dve):
            dve.wait_ge(vecs_turned, 1)
            dve.tensor_copy(vecs[:, :], bank[7][:, 0:V_COLS]).then_inc(vecs_ready, 1)
            dve.wait_ge(vecs_ready, 1)
            l0, l1 = vecs[:, V_LB:V_LB + HEADS], vecs[:, V_LB + HEADS:V_LB + 2 * HEADS]
            top, e0, e1, inv = (lb_tmp[:, i, :] for i in range(4))
            dve.tensor_tensor(top, l0, l1, ALU.max).then_inc(lb_step, 1)
            dve.wait_ge(lb_step, 1)
            dve.tensor_tensor(e0, l0, top, ALU.subtract).then_inc(lb_step, 1)
            dve.tensor_tensor(e1, l1, top, ALU.subtract).then_inc(lb_step, 1)
            dve.wait_ge(lb_exp, 1)
            dve.tensor_tensor(top, e0, e1, ALU.add).then_inc(lb_step, 1)
            dve.wait_ge(lb_step, 4)
            dve.reciprocal(inv, top).then_inc(lb_step, 1)
            dve.wait_ge(lb_step, 5)
            dve.tensor_tensor(e0, e0, inv, ALU.mult).then_inc(lb_step, 1)
            dve.tensor_tensor(e1, e1, inv, ALU.mult).then_inc(lb_step, 1)
            dve.wait_ge(lb_step, 7)
            dve.tensor_tensor(top, e0, e1, ALU.add).then_inc(lb_step, 1)
            dve.tensor_tensor(lbound[:, 0, :], e0, e0, ALU.subtract).then_inc(lb_step, 1)
            dve.wait_ge(lb_step, 8)
            dve.tensor_tensor(lbound[:, 1, :], top, e0, ALU.subtract).then_inc(lb_step, 1)
            dve.wait_ge(lb_step, 10)
            dve.tensor_scalar(lspan[:, :, :], lbound[:, :, :], -1.0, 1.0, ALU.mult, ALU.add).then_inc(lb_step, 1)
            for kt in range(KT):
                dve.wait_ge(x_turned, kt + 1)
                dve.tensor_copy(xT[:, kt, :], bank[kt % 4][:, 0:T]).then_inc(x_loaded, 1)

            def split(s, n, kts):
                dve.wait_ge(hi_done, n + 1)
                dve.tensor_tensor(w_lo[s][:, 0:kts, :], raw[s][:, 0:kts, :], w_hi[s][:, 0:kts, :].bitcast(f32), ALU.subtract).then_inc(lo_done, 1)

            def weight_pass(name, body, unroll=False):
                i = [p[0] for p in PASSES].index(name)
                _, n0, units, kts = PASSES[i]
                its = units // RING

                def step(it, last):
                    for s in range(RING):
                        n = n0 + 4 * it + s
                        if s == 0:
                            split(3, n + 3, kts)
                        elif not last:
                            split(s - 1, n + 3, kts)
                        elif i + 1 < len(PASSES):
                            split(s - 1, PASSES[i + 1][1] + s - 1, PASSES[i + 1][3])
                        body(it, s)
                if n0 == 0:
                    for s in range(3):
                        split(s, s, kts)
                if unroll:
                    for it in range(its - 1):
                        step(it, False)
                else:
                    with dve.Fori(0, its - 1) as it:
                        step(it, False)
                step(its - 1, True)

            def scale_x(nth, version, col):
                for kt in range(KT):
                    dve.wait_ge(norm_hi, KT * nth + kt + 1)
                    dve.scalar_tensor_tensor(act_lo[:, kt, :], xT[:, kt, :], vecs[:, col + kt:col + kt + 1],
                                             act_hi[:, kt, :].bitcast(f32), ALU.mult, ALU.subtract).then_inc(norm_lo, 1)

            def invert_root(nth):
                dve.wait_ge(rooted, nth + 1)
                dve.reciprocal(rstd[:, :], root[:, :]).then_inc(rstd_done, 1)
                dve.wait_ge(rstd_done, nth + 1)

            dve.wait_ge(x_loaded, KT)
            scale_x(0, 0, V_MIX)
            invert_root(0)
            for layer in range(DEPTH):
                L = layer
                if layer:
                    scale_x(2, 2, V_MIX + KT)
                    invert_root(2)

                def mixer_step(it, s):
                    n = IN0[L] + 4 * it + s
                    dve.wait_ge(unit_used, n + 1)
                    out = proj[:, it, s, :] if it < 4 else up[:, s, PAD:]
                    dve.tensor_tensor(out, bank[s][:, 0:T], rstd[:, :], ALU.mult).then_inc(bank_read, 1)
                    if s == RING - 1 and it == 2:
                        dve.wait_ge(sig_done, 3 * L + 1)
                        dve.wait_ge(bank_read, IN0[L] + 4)
                        dve.tensor_tensor(proj[:, 0, :, :], proj[:, 0, :, :], sig[:, :, :], ALU.mult).then_inc(q_gated, 1)
                        dve.wait_ge(lb_step, 11)
                        dve.wait_ge(sig_done, 3 * L + 2)
                        for h in range(HEADS):
                            dve.tensor_scalar(proj[:, 1, h, :], proj[:, 1, h, :], lspan[:, L, h:h + 1], lbound[:, L, h:h + 1],
                                              ALU.mult, ALU.add).then_inc(forget_done, 1)
                weight_pass(f"in{L}", mixer_step, unroll=True)
                dve.wait_ge(sig_done, 3 * L + 3)
                dve.tensor_tensor(proj[:, 3, :, :], proj[:, 3, :, :], sig[:, :, :], ALU.mult).then_inc(g_gated, 1)
                dve.wait_ge(logf_done, L + 1)
                dve.wait_ge(segments_set, 2 * (L + 1))
                dve.tensor_tensor_scan(decay[:, :, :].rearrange("p h t -> p (h t)"), segments[:, :, :].rearrange("p h t -> p (h t)"),
                                       logf[:, :, :].rearrange("p h t -> p (h t)"), 0.0, ALU.mult, ALU.add).then_inc(decay_done, 1)

                def take(i):
                    dve.wait_ge(scored, 17 * L + i + 1)
                    src = bank[4 + i % 2][:, :].rearrange("p (h t) -> p h t", h=HEADS)
                    if i == 16:
                        dve.tensor_copy(scores_x[:, :, :], src).then_inc(scores_taken, 1)
                        return
                    if i >= 2:
                        dve.wait_ge(scores_taken, 17 * L + i - 1)
                    mask = consts[:, C_MASK + 128 * (i // 2):C_MASK + 128 * (i // 2 + 1)].bitcast(i32)
                    dve.copy_predicated(scores[:, i % 2, :, :], mask.unsqueeze(1).broadcast_to([128, HEADS, SEG]), src).then_inc(scores_taken, 1)

                dve.wait_ge(scores_zeroed, L + 1)
                dve.wait_ge(keys_done, L + 1)
                dve.wait_ge(decay_done, L + 1)
                for j, half in enumerate(LEVELS + (SEG,)):
                    e, z, q, k = (t.rearrange("p h (n t) -> p h n t", t=2 * half)
                                  for t in (diff[j % 2][:, :, :], sided[j % 2][:, :, :], proj[:, 0, :, 0:SEQ], keys[:, :, 0:SEQ]))
                    if j >= 2:
                        dve.wait_ge(scored, 17 * L + 2 * j)
                    dve.wait_ge(diff_exp, 16 * L + 2 * j + 1)
                    dve.tensor_tensor(z[:, :, :, 0:half], e[:, :, :, 0:half], k[:, :, :, 0:half], ALU.mult).then_inc(sided_done, 1)
                    dve.wait_ge(diff_exp, 16 * L + 2 * j + 2)
                    dve.tensor_tensor(z[:, :, :, half:], e[:, :, :, half:], q[:, :, :, half:], ALU.mult).then_inc(sided_done, 1)
                    take(2 * j)
                    take(2 * j + 1)
                    dve.wait_ge(v_spread, 8 * L + j + 1)
                    dve.wait_ge(state_decayed, 4 * (L + 1))
                    for h in range(HEADS):
                        dve.scalar_tensor_tensor(state[:, j, h, :], bank[j % 2][:, 128 * h:128 * (h + 1)], keys[:, h, SEQ + j:SEQ + j + 1],
                                                 state[:, j, h, :], ALU.mult, ALU.add).then_inc(state_done, 1)
                take(16)
                dve.wait_ge(past_summed, L + 1)
                for g in range(4):
                    w = (win_a, win_b)[g % 2]
                    dve.tensor_tensor(w[:, g, PAD + SEQ:], bank[2][:, DEC * g:DEC * (g + 1)], up[:, g, PAD + SEQ:], ALU.add).then_inc(past_added, 1)
                dve.wait_ge(windowed, 8 * (L + 1))
                for g in range(4):
                    w = (win_a, win_b)[g % 2]
                    dve.wait_ge(past_added, 4 * L + g + 1)
                    dve.scalar_tensor_tensor(w[:, g, PAD:], w[:, g, PAD:], 1.0 / WINDOWS[g], up[:, g, PAD:], ALU.mult, ALU.subtract).then_inc(pooled, 1)
                for g in range(4):
                    dve.wait_ge(pool_hi, 4 * L + g + 1)
                    dve.scalar_tensor_tensor(mix_lo[:, 4 + g, :], bank[2 + g % 2][:, 0:T], vecs[:, V_POOL + 4 * L + g:V_POOL + 4 * L + g + 1],
                                             mix_hi[:, 4 + g, :].bitcast(f32), ALU.mult, ALU.subtract).then_inc(pool_lo, 1)
                dve.wait_ge(end_exp, 2 * (L + 1))
                for h in range(HEADS):
                    dve.tensor_scalar(kdec[:, h, 0:SEG], sided[1][:, h, 0:SEG], diff[0][:, h, 0:1], None, ALU.mult).then_inc(kdec_done, 1)
                dve.tensor_tensor(kdec[:, :, SEG:SEQ], keys[:, :, SEG:SEQ], diff[0][:, :, SEG:SEQ], ALU.mult).then_inc(kdec_done, 1)
                dve.wait_ge(hgo_rooted, 3 * (L + 1))
                dve.reciprocal(hg_rstd[:, :, :], hg_rstd[:, :, :]).then_inc(hgo_rstd, 1)
                dve.wait_ge(hgo_rstd, L + 1)
                for h in range(HEADS):
                    dve.scalar_tensor_tensor(hg_tmp[:, h, :], hgo[:, h, :], vecs[:, V_HG + 4 * L + h:V_HG + 4 * L + h + 1],
                                             hg_rstd[:, h, :], ALU.mult, ALU.mult).then_inc(hgo_scaled, 1)
                for h in range(HEADS):
                    dve.wait_ge(hgo_scaled, 8 * L + h + 1)
                    dve.tensor_tensor(hg_tmp[:, h, :], hg_tmp[:, h, :], proj[:, 3, h, :], ALU.mult).then_inc(hgo_scaled, 1)
                for h in range(HEADS):
                    dve.wait_ge(mix_hi_done, 4 * L + h + 1)
                    dve.tensor_tensor(mix_lo[:, h, :], hg_tmp[:, h, :], mix_hi[:, h, :].bitcast(f32), ALU.subtract).then_inc(mix_lo_done, 1)

                def out_step(it, s):
                    kt = 4 * it + s
                    dve.wait_ge(unit_used, WO0[L] + kt + 1)
                    dve.tensor_tensor(xT[:, kt, :], bank[s][:, 0:T], xT[:, kt, :], ALU.add).then_inc(bank_read, 1)
                weight_pass(f"out{L}", out_step, unroll=True)
                if layer == 0:
                    scale_x(1, 1, V_FFN)
                    invert_root(1)

                    def ffn_step(it, s):
                        i = s // 2
                        n = GU0 + 4 * it + s
                        dve.wait_ge(unit_used, n + 1)
                        out = (gate_in, up_in)[s % 2][i]
                        dve.tensor_tensor(out[:, :], bank[s][:, 0:T], rstd[:, :], ALU.mult).then_inc(bank_read, 1)
                        if s % 2:
                            dve.wait_ge(gate_done, 2 * it + i + 1)
                            dve.wait_ge(bank_read, n + 1)
                            dve.tensor_tensor(gate_act[i][:, :], gate_act[i][:, :], up_in[i][:, :], ALU.mult).then_inc(ffn_mult, 1)
                            dve.wait_ge(ffn_hi_done, 2 * it + i + 1)
                            at_ft = ds(2 * it + i, 1)
                            dve.tensor_tensor(ffn_lo[:, at_ft, :].rearrange("p a t -> p (a t)"), gate_act[i][:, :],
                                              ffn_hi[:, at_ft, :].rearrange("p a t -> p (a t)").bitcast(f32), ALU.subtract).then_inc(ffn_lo_done, 1)
                    weight_pass("ffn_up0", ffn_step)

                    def down_step(it, s):
                        if s % 2:
                            dve.wait_ge(unit_used, DN0 + 4 * it + s + 1)
                            col = xT[:, ds(2 * it + s // 2, 1), :].rearrange("p a t -> p (a t)") if not isinstance(it, int) else xT[:, 2 * it + s // 2, :]
                            dve.tensor_tensor(col, bank[s - 1][:, 0:T], col, ALU.add).then_inc(bank_read, 2)
                    weight_pass("ffn_down0", down_step)
            for kt in range(KT):
                wait_x(dve, 3, kt)
                dve.tensor_scalar(scaled_m[:, kt, :], xT[:, kt, :], vecs[:, V_FFN + KT + kt:V_FFN + KT + kt + 1], None, ALU.mult).then_inc(scaled_done, 1)
            for i, (_, rows) in enumerate(TOKEN_TILES):
                dve.wait_ge(rooted, 3 + i + 1)
                dve.reciprocal(rstd[0:rows, i:i + 1], root[0:rows, i:i + 1]).then_inc(rstd_done, 1)
            dve.wait_ge(routed, 1)
            dve.wait_ge(logits_zeroed, 1)
            steps = [0]

            def step_of(ins):
                ins.then_inc(route, 1)
                steps[0] += 1
                dve.wait_ge(route, steps[0])
            for i, (_, rows) in enumerate(TOKEN_TILES):
                dve.wait_ge(rstd_done, 3 + i + 1)
                step_of(dve.tensor_scalar(logits[0:rows, i, :], bank[7][0:rows, 8 * i:8 * (i + 1)], rstd[0:rows, i:i + 1], None, ALU.mult))
            wide = [128, 3, N_EXPERTS, N_EXPERTS]
            each = logits[:, :, :].unsqueeze(2).broadcast_to(wide)
            own = logits[:, :, :].unsqueeze(3).broadcast_to(wide)
            lower = consts[:, C_LOWER:C_LOWER + 64].rearrange("p (e j) -> p e j", e=8)
            step_of(dve.tensor_tensor(greater[:, :, :, :], each, own, ALU.is_gt))
            step_of(dve.tensor_tensor(equal[:, :, :, :], each, own, ALU.is_equal))
            for i in range(3):
                step_of(dve.tensor_tensor(equal[:, i, :, :], equal[:, i, :, :], lower, ALU.mult))
            step_of(dve.tensor_tensor(greater[:, :, :, :], greater[:, :, :, :], equal[:, :, :, :], ALU.add))
            step_of(dve.tensor_reduce(rank[:, :, :], greater[:, :, :, :], AX.X, ALU.add))
            step_of(dve.tensor_single_scalar(first[:, :, :], rank[:, :, :], 0.0, ALU.is_equal))
            step_of(dve.tensor_single_scalar(second[:, :, :], rank[:, :, :], 1.0, ALU.is_equal))
            step_of(dve.tensor_tensor(picked[:, :, :], logits[:, :, :], first[:, :, :], ALU.mult))
            step_of(dve.tensor_reduce(tops[:, 0, :], picked[:, :, :], AX.X, ALU.add))
            step_of(dve.tensor_tensor(picked[:, :, :], logits[:, :, :], second[:, :, :], ALU.mult))
            step_of(dve.tensor_reduce(tops[:, 1, :], picked[:, :, :], AX.X, ALU.add))
            step_of(dve.tensor_tensor(chosen[:, :, :], first[:, :, :], second[:, :, :], ALU.add))
            step_of(dve.tensor_tensor(tops[:, 1, :], tops[:, 1, :], tops[:, 0, :], ALU.subtract))
            dve.wait_ge(route_exp, 1)
            step_of(dve.tensor_scalar(tops[:, 2, :], tops[:, 1, :], 1.0, None, ALU.add))
            step_of(dve.reciprocal(tops[:, 2, :], tops[:, 2, :]))
            step_of(dve.tensor_tensor(tops[:, 3, :], tops[:, 1, :], tops[:, 2, :], ALU.mult))
            per = [128, 3, N_EXPERTS]
            step_of(dve.tensor_tensor(gates[:, :, :], first[:, :, :], tops[:, 2, :].unsqueeze(2).broadcast_to(per), ALU.mult))
            step_of(dve.tensor_tensor(second[:, :, :], second[:, :, :], tops[:, 3, :].unsqueeze(2).broadcast_to(per), ALU.mult))
            step_of(dve.tensor_tensor(gates[:, :, :], gates[:, :, :], second[:, :, :], ALU.add))
            dve.wait_ge(placed, 1)
            flat = slot[:, :, :].rearrange("p i e -> p (i e)")
            step_of(dve.scalar_tensor_tensor(flat, bank[5][:, 0:24], 1.0, chosen[:, :, :].rearrange("p i e -> p (i e)"), ALU.add, ALU.mult))
            step_of(dve.tensor_scalar(flat, flat, -1.0, None, ALU.add))
            step_of(dve.tensor_reduce(longest[:, :], bank[5][:, 24:32], AX.X, ALU.max))
            step_of(dve.tensor_copy(longest_i[:, :], longest[:, :]))
            step_of(dve.scalar_tensor_tensor(over[:, :, :], slot[:, :, :], float(CAP), gates[:, :, :], ALU.is_ge, ALU.mult))
            assert steps[0] == ROUTED, steps[0]
            for i, (_, rows) in enumerate(TOKEN_TILES):
                for e in range(N_EXPERTS):
                    dve.tensor_scalar(token_hot[0:rows, i, e, :], iota[0:rows, :], slot[0:rows, i, e:e + 1], None, ALU.is_equal).then_inc(hot, 1)
            dve.wait_ge(final_out, 32)
            for i, (_, rows) in enumerate(TOKEN_TILES):
                for c in range(2):
                    dve.wait_ge(h_hi_done, 2 * i + c + 1)
                    dve.scalar_tensor_tensor(h_lo[0:rows, i, 512 * c:512 * (c + 1)], bank[2 + c][0:rows, :], rstd[0:rows, i:i + 1],
                                             h_hi[0:rows, i, 512 * c:512 * (c + 1)].bitcast(f32), ALU.mult, ALU.subtract).then_inc(h_lo_done, 1)
            dve.wait_ge(gate_slots, 1)
            dve.tensor_copy(slot_gate[:, :], bank[6][:, 0:N_EXPERTS]).then_inc(y_lo_done, 1)
            for n in range(16):
                q, d = n // 4, n % 4
                dve.wait_ge(packed_hi, n + 1)
                view = [packed[:, 2 * q:2 * q + 2, half, 256 * d:256 * (d + 1)].rearrange("p e (d s) -> p e d s", d=2) for half in range(2)]
                dve.tensor_tensor(view[1], bank[n % 4][:, :].rearrange("p (d e s) -> p e d s", d=2, e=2), view[0].bitcast(f32), ALU.subtract).then_inc(packed_lo, 1)

            def split_e(j, kts_cols, turn=None):
                u = j if turn is None else HEAD_UNITS + TURN_UNITS * turn + j
                jj = j if turn is None else HEAD_UNITS + j
                dve.wait_ge(moe_hi, u + 1)
                hi, lo = w_hi[jj % SPLIT_RING][:, 0:kts_cols, :], w_lo[jj % SPLIT_RING][:, 0:kts_cols, :]
                dve.tensor_tensor(lo, raw_e[jj % RAW_RING][:, 0:kts_cols, :], hi.bitcast(f32), ALU.subtract).then_inc(moe_lo, 1)

            def gate_up(e, u):
                dve.wait_ge(moe_used, u)
                for p, (c0, width) in enumerate(PIECES):
                    dve.wait_ge(gate_silu, 3 * e + p + 1)
                    dve.tensor_tensor(act_e[:, c0:c0 + width], bank[3 + p][:, 0:width], act_e[:, c0:c0 + width], ALU.mult).then_inc(act_done, 1)

            def rest_of_hidden(e):
                for p, (c0, width) in enumerate(PIECES):
                    dve.wait_ge(hid_hi_done, 3 * e + p + 1)
                    ks = slice(c0 // 128, (c0 + width) // 128)
                    dve.tensor_tensor(hid_lo[:, ks, :], bank[3 + p][:, 0:width].rearrange("p (a b) -> p a b", b=128), hid_hi[:, ks, :].bitcast(f32), ALU.subtract).then_inc(hid_lo_done, 1)

            def rest_of_result(e):
                for c in range(2):
                    dve.wait_ge(y_hi_done, 2 * e + c + 1)
                    hi, lo = (packed[:, ds(e, 1), half, 512 * c:512 * (c + 1)].rearrange("p a n -> p (a n)") for half in range(2))
                    dve.scalar_tensor_tensor(lo, bank[6 + c][:, :], slot_gate[:, ds(e, 1)], hi.bitcast(f32), ALU.mult, ALU.subtract).then_inc(y_lo_done, 1)

            for j in range(HEAD_UNITS + LOAD_AHEAD):
                if j < HEAD_UNITS:
                    split_e(j, FE)
                else:
                    split_e(j - HEAD_UNITS, FE, turn=0)

            def turn_e(e, last):
                for j in range(TURN_UNITS):
                    ahead = j + LOAD_AHEAD
                    if j == 0:
                        gate_up(e, HEAD_UNITS + TURN_UNITS * e)
                    if ahead < TURN_UNITS:
                        split_e(ahead, FE if TURN[ahead][0] != "down" else KT, turn=e)
                    else:
                        split_e(ahead - TURN_UNITS, KT if last else FE, turn=e + 1)
                    if j == 5:
                        rest_of_hidden(e)
                    if j == KT + FE + 1:
                        rest_of_result(e)
            with dve.Fori(0, N_EXPERTS - 2) as e:
                turn_e(e, False)
            turn_e(N_EXPERTS - 2, True)
            gate_up(N_EXPERTS - 1, HEAD_UNITS + TURN_UNITS * (N_EXPERTS - 1))
            rest_of_hidden(N_EXPERTS - 1)
            for j in range(LOAD_AHEAD, FE):
                split_e(j, KT, turn=N_EXPERTS - 1)
            rest_of_result(N_EXPERTS - 1)
            for kt in range(KT):
                dve.wait_ge(scattered, kt + 1)
                dve.tensor_tensor(xT[:, kt, :], bank[kt][:, 0:T], xT[:, kt, :], ALU.add).then_inc(moe_added, 1)
            n_rows = dve.value_load(longest_i[0:1, 0:1])
            with dve.If(n_rows > CAP):
                dve.wait_ge(all_in, 16)
                dve.wait_ge(all_spread, 1)
                for kt in range(KT):
                    dve.tensor_tensor(h_all[:, kt, :], bank[2][:, 0:T], h_all[:, kt, :], ALU.mult).then_inc(all_added, 1)
                with dve.Fori(0, N_EXPERTS) as e:
                    dve.tensor_copy(over_col[:, :], over[:, :, ds(e, 1)].rearrange("p i a -> p (i a)")).then_inc(all_col, 1)
                    dve.wait_ge(all_spread, e + 2)
                    dve.tensor_copy(over_all[:, :], bank[2][:, 0:T]).then_inc(all_over, 1)
                    with dve.Fori(0, FE) as f:
                        n = e * FE + f
                        dve.wait_ge(all_silu, n + 1)
                        dve.wait_ge(all_up, 2 * n + 2)
                        dve.tensor_tensor(act_all[:, :], bank[1][:, 0:T], act_all[:, :], ALU.mult).then_inc(all_act, 1)
                        dve.wait_ge(all_act, 2 * n + 1)
                        dve.wait_ge(all_over, e + 1)
                        dve.tensor_tensor(act_all[:, :], act_all[:, :], over_all[:, :], ALU.mult).then_inc(all_act, 1)
                        for kt in range(KT):
                            dve.wait_ge(all_down, n * KT + kt + 1)
                            dve.tensor_tensor(xT[:, kt, :], bank[4 + kt % 4][:, 0:T], xT[:, kt, :], ALU.add).then_inc(all_added, 1)
                dve.wait_ge(all_added, N_EXPERTS * FE * KT + KT)
            dve.end_ifs()
            dve.wait_ge(moe_added, KT)
            for kt in range(KT):
                dve.engine_nop().then_inc(x_moe, 1)
            dve.wait_ge(final_out, 32)
            for kt in range(KT):
                wait_x(dve, 4, kt)
                dve.tensor_scalar(scaled_f[:, kt, :], xT[:, kt, :], vecs[:, V_FINAL + kt:V_FINAL + kt + 1], None, ALU.mult).then_inc(scaled_done, 1)
            for i, (_, rows) in enumerate(TOKEN_TILES):
                dve.wait_ge(rooted, 6 + i + 1)
                dve.reciprocal(rstd[0:rows, i:i + 1], root[0:rows, i:i + 1]).then_inc(rstd_done, 1)

        @block.tensor
        def _(pe):
            pe.wait_ge(consts_in, 16)
            pe.wait_ge(vecs_in, 16 * 6)
            pe.transpose(bank[7][:, 0:V_COLS], vec_rows[:, :], ident[0:V_COLS, 0:V_COLS]).then_inc(vecs_turned, 1)
            pe.wait_ge(x_in, 32)
            for kt in range(KT):
                if kt >= 4:
                    pe.wait_ge(x_loaded, kt - 3)
                for i, (t0, rows) in enumerate(TOKEN_TILES):
                    mm = pe.transpose(bank[kt % 4][:, t0:t0 + rows], x_rows[0:rows, i, 128 * kt:128 * (kt + 1)], ident[0:rows, 0:rows])
                mm.then_inc(x_turned, 1)

            def sum_squares(nth):
                for kt in range(KT):
                    pe.wait_ge(squared, KT * nth + kt + 1)
                    mm = pe.matmul(bank[4][:, 0:T], ones, square[:, kt, :], start=(kt == 0), stop=(kt == KT - 1))
                mm.then_inc(summed, 1)

            def weight_pass(name, hi, lo):
                _, n0, units, kts = PASS[name]
                halves = 2 if name[:8] == "ffn_down" else 1

                def step(it, first=False):
                    for s in range(RING):
                        n = n0 + 4 * it + s
                        half = s % halves
                        out = bank[s - half]
                        pe.wait_ge(lo_done, n + 1)
                        if half == 0 and not first:
                            pe.wait_ge(bank_read, n - 4 + halves)
                        for k in range(kts):
                            c = half * kts + k
                            pe.matmul(out[:, 0:T], w_hi[s][:, k, :], hi[:, c, :], start=(c == 0), stop=False)
                            pe.matmul(out[:, 0:T], w_hi[s][:, k, :], lo[:, c, :], start=False, stop=False)
                            mm = pe.matmul(out[:, 0:T], w_lo[s][:, k, :], hi[:, c, :], start=False,
                                           stop=(c == halves * kts - 1))
                        mm.then_inc(unit_used, 1)
                if n0 == 0:
                    pe.wait_ge(x_loaded, KT)
                    step(0, first=True)
                with pe.Fori(int(n0 == 0), units // RING) as it:
                    step(it)

            for layer in range(DEPTH):
                L = layer
                nth = 2 * L
                sum_squares(nth)
                pe.wait_ge(norm_lo, KT * (nth + 1))
                weight_pass(f"in{L}", act_hi, act_lo)
                q, k, v = proj[:, 0, :, :], keys[:, :, :], proj[:, 2, :, :]
                pe.wait_ge(bank_read, IN0[L] + 20)
                for i in range(2):
                    for h in range(HEADS):
                        mm = pe.transpose(bank[6 + i][:, 128 * h:128 * (h + 1)], v[:, h, SEG * i:SEG * (i + 1)], ident)
                    mm.then_inc(v_turned, 1)
                pe.wait_ge(q_gated, L + 1)
                pe.wait_ge(keys_done, L + 1)

                def score(i, left, right):
                    if i >= 2:
                        pe.wait_ge(scores_taken, 17 * L + i - 1)
                    for h in range(HEADS):
                        mm = pe.matmul(bank[4 + i % 2][:, 128 * h:128 * (h + 1)], left(h), right(h), start=True, stop=True)
                    mm.then_inc(scored, 1)
                for i in range(2):
                    tok = slice(SEG * i, SEG * (i + 1))
                    score(i, lambda h: k[:, h, tok], lambda h: q[:, h, tok])
                for j in range(len(LEVELS) + 1):
                    z = sided[j % 2]
                    pe.wait_ge(sided_done, 16 * L + 2 * j + 2)
                    if j < len(LEVELS):
                        for i in range(2):
                            tok = slice(SEG * i, SEG * (i + 1))
                            score(2 * j + 2 + i, lambda h: z[:, h, tok], lambda h: z[:, h, tok])
                    else:
                        score(16, lambda h: z[:, h, 0:SEG], lambda h: z[:, h, SEG:SEQ])
                    if j >= 2:
                        pe.wait_ge(state_done, 32 * L + 4 * (j - 1))
                    for h in range(HEADS):
                        mm = pe.matmul(bank[j % 2][:, 128 * h:128 * (h + 1)], v[:, h, SEQ + j:SEQ + j + 1].broadcast_to([128, 128]), ident,
                                       start=True, stop=True)
                    mm.then_inc(v_spread, 1)
                pe.wait_ge(past_in, 16 * (L + 1))
                rows = DEC * POOL_BUF
                for g in range(4):
                    mm = pe.matmul(bank[2][:, DEC * g:DEC * (g + 1)], pool_past[:, 128 * g:128 * (g + 1)], pick[0:rows, g, :], start=True, stop=True)
                mm.then_inc(past_summed, 1)
                pe.wait_ge(pool_w_in, 16 * (L + 1))
                for g in range(4):
                    w = (win_a, win_b)[g % 2]
                    pe.wait_ge(pooled, 4 * L + g + 1)
                    if g >= 2:
                        pe.wait_ge(pool_lo, 4 * L + g - 1)
                    pe.matmul(bank[2 + g % 2][:, 0:T], pool_w[:, g, :], w[:, g, PAD:], start=True, stop=True).then_inc(pool_mapped, 1)
                pe.wait_ge(pool_lo, 4 * (L + 1))
                for g in range(4):
                    mm = pe.transpose(bank[3][0:POOL_BUF + DEC, 128 * g:128 * (g + 1)], up[:, g, PAD + SEQ - POOL_BUF:], ident)
                mm.then_inc(tail_turned, 1)
                pe.wait_ge(v_copied, 2 * (L + 1))
                pe.wait_ge(scores_taken, 17 * (L + 1))
                for h in range(HEADS):
                    hs = slice(128 * h, 128 * (h + 1))
                    mm = pe.matmul(bank[6][:, hs], values[:, 0, hs], scores[:, 0, h, :], start=True, stop=True)
                mm.then_inc(attended, 1)
                for h in range(HEADS):
                    hs = slice(128 * h, 128 * (h + 1))
                    pe.matmul(bank[7][:, hs], values[:, 0, hs], scores_x[:, h, :], start=True, stop=False)
                    mm = pe.matmul(bank[7][:, hs], values[:, 1, hs], scores[:, 1, h, :], start=False, stop=True)
                mm.then_inc(attended, 1)
                pe.wait_ge(state_done, 32 * (L + 1))
                for b in range(DEC):
                    for h in range(HEADS):
                        mm = pe.matmul(bank[0][:, DEC * h + b:DEC * h + b + 1], state[:, b, h, :], q[:, h, SEQ + b:SEQ + b + 1], start=True, stop=True)
                mm.then_inc(attended, 1)
                pe.wait_ge(kdec_done, 5 * (L + 1))
                pe.wait_ge(hgo_copied, 3 * L + 2)
                for i in range(2):
                    for h in range(HEADS):
                        mm = pe.transpose(bank[6 + i][:, 128 * h:128 * (h + 1)], kdec[:, h, SEG * i:SEG * (i + 1)], ident)
                    mm.then_inc(kdec_turned, 1)
                pe.wait_ge(kdec_copied, 2 * (L + 1))
                for h in range(HEADS):
                    hs = slice(128 * h, 128 * (h + 1))
                    pe.matmul(bank[4][:, hs], kdecT[:, 0, hs], values[:, 0, hs], start=True, stop=False)
                    mm = pe.matmul(bank[4][:, hs], kdecT[:, 1, hs], values[:, 1, hs], start=False, stop=True)
                mm.then_inc(final_state, 1)
                pe.wait_ge(hgo_squared, L + 1)
                sq = hgo_sq[:, :, :].rearrange("p h t -> p (h t)")
                for i in range(3):
                    pe.matmul(bank[(5, 0, 1)[i]][:, 0:352], ones, sq[:, 352 * i:352 * (i + 1)], start=True, stop=True).then_inc(hgo_summed, 1)
                pe.wait_ge(pool_lo, 4 * (L + 1))
                pe.wait_ge(mix_lo_done, 4 * (L + 1))
                weight_pass(f"out{L}", mix_hi, mix_lo)
                if layer == 0:
                    sum_squares(1)
                    pe.wait_ge(norm_lo, KT * 2)
                    weight_pass("ffn_up0", act_hi, act_lo)
                    pe.wait_ge(ffn_lo_done, FT)
                    weight_pass("ffn_down0", ffn_hi, ffn_lo)
            pe.wait_ge(squared, KT * 4)
            for i, (t0, rows) in enumerate(TOKEN_TILES):
                for kt in range(KT):
                    mm = pe.matmul(bank[4][0:rows, i:i + 1], square_m[:, kt, t0:t0 + rows], ones[:, 0:1], start=(kt == 0), stop=(kt == KT - 1))
            mm.then_inc(summed, 1)
            pe.wait_ge(scaled_done, KT)
            pe.wait_ge(router_in, 16)
            for i, (t0, rows) in enumerate(TOKEN_TILES):
                for kt in range(KT):
                    mm = pe.matmul(bank[7][0:rows, 8 * i:8 * (i + 1)], scaled_m[:, kt, t0:t0 + rows], router[:, kt, :], start=(kt == 0), stop=(kt == KT - 1))
            mm.then_inc(routed, 1)
            for i, (t0, rows) in enumerate(TOKEN_TILES):
                for c in range(2):
                    if i:
                        pe.wait_ge(h_lo_done, 2 * (i - 1) + c + 1)
                    for k in range(4):
                        mm = pe.transpose(bank[2 + c][0:rows, 128 * k:128 * (k + 1)], scaled_m[:, 4 * c + k, t0:t0 + rows], ident)
                    mm.then_inc(h_turned, 1)
                if i == 0:
                    pe.wait_ge(route, 17)
                    for ii, (_, r) in enumerate(TOKEN_TILES):
                        for jj in range(ii):
                            pe.matmul(bank[5][:, 8 * ii:8 * (ii + 1)], ones, chosen[:, jj, :], start=(jj == 0), stop=False)
                        pe.matmul(bank[5][:, 8 * ii:8 * (ii + 1)], before[0:r, :], chosen[0:r, ii, :], start=(ii == 0), stop=True)
                    for ii, (_, r) in enumerate(TOKEN_TILES):
                        mm = pe.matmul(bank[5][:, 24:32], ones[0:r, :], chosen[0:r, ii, :], start=(ii == 0), stop=(ii == 2))
                    mm.then_inc(placed, 1)
            pe.wait_ge(hot, 3 * N_EXPERTS)
            for e in range(N_EXPERTS):
                if e >= 2:
                    pe.wait_ge(hot_copied, e - 1)
                for i, (t0, rows) in enumerate(TOKEN_TILES):
                    mm = pe.transpose(bank[e % 2][:, t0:t0 + rows], token_hot[0:rows, i, e, :].bitcast(f32), ident[0:rows, 0:rows])
                mm.then_inc(hot_turned, 1)
            for e in range(N_EXPERTS):
                for i, (_, rows) in enumerate(TOKEN_TILES):
                    mm = pe.matmul(bank[6][:, e:e + 1], token_hot[0:rows, i, e, :].bitcast(f32), gates[0:rows, i, e:e + 1], start=(i == 0), stop=(i == 2))
            mm.then_inc(gate_slots, 1)
            pe.wait_ge(hot_copied, N_EXPERTS)
            pe.wait_ge(h_lo_done, 6)
            for n in range(16):
                q, d = n // 4, n % 4
                if n >= 4:
                    pe.wait_ge(packed_lo, n - 3)
                for dd in range(2):
                    kt = 2 * d + dd
                    for m in range(6):
                        i, part = m // 2, (h_hi, h_lo)[m % 2]
                        rows = TOKEN_TILES[i][1]
                        mm = pe.matmul(bank[n % 4][:, 256 * dd:256 * (dd + 1)], part[0:rows, i, 128 * kt:128 * (kt + 1)],
                                       token_hot[0:rows, i, 2 * q:2 * q + 2, :].rearrange("p e s -> p (e s)"), start=(m == 0), stop=(m == 5))
                mm.then_inc(gathered, 1)

            def unit_e(kind, k, j, turn=None):
                u = j if turn is None else HEAD_UNITS + TURN_UNITS * turn + j
                jj = j if turn is None else HEAD_UNITS + j
                pe.wait_ge(moe_lo, u + 1)
                hi, lo = (t[jj % SPLIT_RING][:, :, :].rearrange("p a b -> p (a b)") for t in (w_hi, w_lo))
                if kind == "down":
                    s_hi, s_lo, last, first_bank, pieces = hid_hi[:, k, :], hid_lo[:, k, :], FE - 1, 6, ((0, 512), (512, 512))
                else:
                    s_hi, s_lo, last, first_bank, pieces = x_hi[:, k, :], x_lo[:, k, :], KT - 1, 0 if kind == "gate" else 3, PIECES
                for n, (s, w) in enumerate(((s_hi, hi), (s_hi, lo), (s_lo, hi))):
                    for p, (c0, width) in enumerate(pieces):
                        mm = pe.matmul(bank[first_bank + p][:, 0:width], s, w[:, c0:c0 + width], start=(k == 0 and n == 0),
                                       stop=(k == last and n == 2))
                mm.then_inc(moe_used, 1)

            def turn_hidden(e):
                for p, (c0, width) in enumerate(PIECES):
                    pe.wait_ge(act_done, 3 * e + 3)
                    for k in range(width // 128):
                        mm = pe.transpose(bank[3 + p][:, 128 * k:128 * (k + 1)], act_e[:, c0 + 128 * k:c0 + 128 * (k + 1)], ident)
                    mm.then_inc(hid_turned, 1)

            pe.wait_ge(packed_lo, 16)
            pe.wait_ge(y_lo_done, 1)
            pe.wait_ge(x_hi_set, 2)
            pe.wait_ge(x_lo_set, 2)
            for j in range(HEAD_UNITS):
                unit_e(("gate", "up")[j // KT], j % KT, j)

            def turn_e(e):
                for j, (kind, _, k) in enumerate(TURN):
                    if kind == "gate" and k == 0:
                        pe.wait_ge(gate_silu, 3 * e + 3)
                        for ready in (x_hi_set, x_lo_set):
                            pe.wait_ge(ready, 2 * e + 3)
                    if kind == "gate" and k == KT // 2:
                        turn_hidden(e)
                        for ready in (x_hi_set, x_lo_set):
                            pe.wait_ge(ready, 2 * e + 4)
                    if kind == "down" and k == 0:
                        pe.wait_ge(hid_lo_done, 3 * e + 3)
                        pe.wait_ge(y_lo_done, 2 * e + 1)
                    unit_e(kind, k, j, turn=e)
            with pe.Fori(0, N_EXPERTS - 1) as e:
                turn_e(e)
            e = N_EXPERTS - 1
            turn_hidden(e)
            pe.wait_ge(hid_lo_done, 3 * e + 3)
            pe.wait_ge(y_lo_done, 2 * e + 1)
            for j in range(FE):
                unit_e("down", j, j, turn=e)
            last = N_EXPERTS - 1

            def scatter(e, kt):
                for half in range(2):
                    mm = pe.matmul(bank[kt][:, 0:T], packed[:, e, half, 128 * kt:128 * (kt + 1)], slot_hot[:, e, :],
                                   start=(e == 0 and half == 0), stop=(e == last and half == 1))
                return mm
            for e in range(last):
                for kt in range(6):
                    scatter(e, kt)
            pe.wait_ge(y_lo_done, 2 * N_EXPERTS + 1)
            for e in range(last):
                for kt in (6, 7):
                    scatter(e, kt)
            for kt in range(KT):
                scatter(last, kt).then_inc(scattered, 1)
            n_rows = pe.value_load(longest_i[0:1, 0:1])
            with pe.If(n_rows > CAP):
                pe.wait_ge(moe_added, KT)
                for i, (t0, rows) in enumerate(TOKEN_TILES):
                    mm = pe.matmul(bank[2][:, t0:t0 + rows], rstd[0:rows, i:i + 1].broadcast_to([rows, 128]), ident[0:rows, 0:rows], start=True, stop=True)
                mm.then_inc(all_spread, 1)
                pe.wait_ge(all_added, KT)
                with pe.Fori(0, N_EXPERTS) as e:
                    pe.wait_ge(all_col, e + 1)
                    for i, (t0, rows) in enumerate(TOKEN_TILES):
                        mm = pe.matmul(bank[2][:, t0:t0 + rows], over_col[0:rows, i:i + 1].broadcast_to([rows, 128]), ident[0:rows, 0:rows], start=True, stop=True)
                    mm.then_inc(all_spread, 1)
                    with pe.Fori(0, FE) as f:
                        n = e * FE + f
                        pe.wait_ge(all_w, 48 * (n + 1))
                        pe.wait_ge(all_added, n * KT + KT)
                        for b, w in enumerate((gate_w_all, up_w_all)):
                            for kt in range(KT):
                                mm = pe.matmul(bank[b][:, 0:T], w[:, kt, :], h_all[:, kt, :], start=(kt == 0), stop=(kt == KT - 1))
                            mm.then_inc(all_up, 1)
                        pe.wait_ge(all_act, 2 * n + 2)
                        for kt in range(KT):
                            pe.wait_ge(all_added, n * KT + KT + max(kt - 3, 0))
                            pe.matmul(bank[4 + kt % 4][:, 0:T], down_w_all[:, 128 * kt:128 * (kt + 1)], act_all[:, :], start=True, stop=True).then_inc(all_down, 1)
            pe.end_ifs()
            pe.wait_ge(squared, KT * 5)
            for i, (t0, rows) in enumerate(TOKEN_TILES):
                for kt in range(KT):
                    mm = pe.matmul(bank[4][0:rows, i:i + 1], square_f[:, kt, t0:t0 + rows], ones[:, 0:1], start=(kt == 0), stop=(kt == KT - 1))
            mm.then_inc(summed, 1)
            pe.wait_ge(scaled_done, 2 * KT)
            for i, (t0, rows) in enumerate(TOKEN_TILES):
                for c in range(2):
                    n = 2 * i + c
                    if n >= 2:
                        pe.wait_ge(y_copied, n - 1)
                    for k in range(4):
                        mm = pe.transpose(bank[5 + n % 2][0:rows, 128 * k:128 * (k + 1)], scaled_f[:, 4 * c + k, t0:t0 + rows], ident)
                    mm.then_inc(turned, 1)


def constants():
    import numpy as np
    c = np.zeros((128, C_COLS), np.float32)
    i = np.arange(128)
    c[:, C_IDENT:C_IDENT + 128] = np.eye(128)
    c[:, C_ONES:C_ONES + 128] = 1.0
    c[:, C_BEFORE:C_BEFORE + 128] = i[:, None] < i[None, :]
    c[:, C_IOTA:C_IOTA + 128] = i[None, :]
    c[:, C_MASK:C_MASK + 128] = np.eye(128)
    for n, half in enumerate(LEVELS):
        s, t = i[:, None], i[None, :]
        pair = (s // (2 * half) == t // (2 * half)) & (s % (2 * half) < half) & (t % (2 * half) >= half)
        c[:, C_MASK + 128 * (n + 1):C_MASK + 128 * (n + 2)] = pair
    for g, w in enumerate(WINDOWS):
        t = np.arange(PAD)
        c[:, C_CORR + g * PAD:C_CORR + (g + 1) * PAD] = w / np.minimum(t + 1, w).astype(np.float32)
        for b in range(DEC):
            c[POOL_BUF * b + POOL_BUF + 1 - w:POOL_BUF * (b + 1), C_PICK + g * DEC + b] = 1.0
    e = np.arange(N_EXPERTS)
    c[:, C_LOWER:C_LOWER + 64] = (e[None, :] < e[:, None]).reshape(-1)
    return c


_INS = ["x_prompt", "x_sample", "state_hgrn", "state_pool", "lb_logits", "norm_mix", "w_in", "w_o", "hg_norm", "pool_w", "pool_scale",
        "norm_ffn", "ffn_w_gate", "ffn_w_up", "ffn_w_down", "router", "moe_w_gate", "moe_w_up", "moe_w_down", "norm_final"]
_OUTS = [("y_prompt", (1, SEQ, D_MODEL)), ("y_sample", (DEC, 1, D_MODEL)), ("new_hgrn_prompt", (DEPTH, 1, HEADS, 128, 128)),
         ("new_hgrn_sample", (DEPTH, DEC, HEADS, 128, 128)), ("new_pool_prompt", (DEPTH, 1, POOL_BUF, HG_WIDTH)),
         ("new_pool_sample", (DEPTH, DEC, POOL_BUF, HG_WIDTH))]


def kernel(**inputs):
    import numpy as np
    import concourse.bacc as bacc
    from concourse.bass_utils import run_bass_kernel_spmd

    nc = bacc.Bacc("TRN2", target_bir_lowering=False, num_devices=1)
    arrays = {n: np.ascontiguousarray(inputs[n]) for n in _INS}
    arrays["consts"] = constants()
    launched = {f"in_{n}_dram": x for n, x in arrays.items()}
    a = {n: nc.dram_tensor(f"in_{n}_dram", x.shape, mybir.dt.float32, kind="ExternalInput").ap() for n, x in arrays.items()}
    o = {n: nc.dram_tensor(f"out_{n}_dram", s, mybir.dt.float32, kind="ExternalOutput").ap() for n, s in _OUTS}
    build_program(nc, a, o)
    r = run_bass_kernel_spmd(nc, [launched], core_ids=[0])
    return tuple(r.results[0][f"out_{n}_dram"] for n, _ in _OUTS)
```

```python
import concourse.bass as bass
from concourse import mybir
from contextlib import ExitStack

D_MODEL = 1024
SEQ = 256
DEC = 8
DEPTH = 2
T = SEQ + DEC
KT = D_MODEL // 128
HEADS = 4
HG_WIDTH = HEADS * 128
IN_WIDTH = 5 * HG_WIDTH
POOL_BUF = 15
WINDOWS = (2, 4, 8, 16)
D_FF = 2816
FT = D_FF // 128
N_EXPERTS = 8
D_FF_E = 1408
FE = D_FF_E // 128
EPS = 1e-6
CAP = 128
SEG = 128
TOKEN_TILES = ((0, 128), (128, 128), (256, DEC))
LEVELS = (1, 2, 4, 8, 16, 32, 64)
PAD = 16

C_IDENT, C_ONES, C_BEFORE, C_IOTA = 0, 128, 256, 384
C_MASK = 512
C_CORR = C_MASK + 128 * (1 + len(LEVELS))
C_PICK = C_CORR + 4 * PAD
C_LOWER = C_PICK + 4 * DEC
C_COLS = C_LOWER + N_EXPERTS * N_EXPERTS

V_MIX, V_FFN, V_FINAL, V_LB, V_HG, V_POOL = 0, 16, 32, 40, 48, 56
V_COLS = 64

RING = 4
PASSES = []
_n = 0
for _name, _units, _kts in (("in0", 20, KT), ("out0", 8, KT), ("ffn_up0", 2 * FT, KT), ("ffn_down0", 16, FT // 2),
                            ("in1", 20, KT), ("out1", 8, KT)):
    PASSES.append((_name, _n, _units, _kts))
    _n += _units
PASS = {p[0]: p for p in PASSES}
GROUPS = (0, 1, 3, 2, 4)
IN0 = [PASS["in0"][1], PASS["in1"][1]]
WO0 = [PASS["out0"][1], PASS["out1"][1]]
GU0 = PASS["ffn_up0"][1]
DN0 = PASS["ffn_down0"][1]
LAST_UNIT = _n

RAW_RING = 9
SPLIT_RING = 3
HEAD_UNITS = 2 * KT
TURN_UNITS = 2 * KT + FE
LOAD_AHEAD = 2


def build_program(nc, a, o):
    f32 = mybir.dt.float32
    f32r = mybir.dt.float32r
    i32 = mybir.dt.int32
    ALU = mybir.AluOpType
    ACT = mybir.ActivationFunctionType
    AX = mybir.AxisListType
    ds = bass.ds

    ctx = ExitStack()
    with ctx:
        def sb(name, shape, dt=f32):
            return ctx.enter_context(nc.sbuf_tensor("sb_" + name, shape, dt))

        def sem(name):
            return ctx.enter_context(nc.semaphore(name))

        consts = sb("consts", [128, C_COLS])
        ident = consts[:, C_IDENT:C_IDENT + 128]
        ones = consts[:, C_ONES:C_ONES + 128]
        before = consts[:, C_BEFORE:C_BEFORE + 128]
        iota = consts[:, C_IOTA:C_IOTA + 128]
        corr = consts[:, C_CORR:C_CORR + 4 * PAD].rearrange("p (g t) -> p g t", g=4)
        pick = consts[:, C_PICK:C_PICK + 4 * DEC].rearrange("p (g b) -> p g b", g=4)
        xT = sb("xT", [128, KT, T])
        vecs = sb("vecs", [128, V_COLS])
        vec_rows = sb("vec_rows", [V_COLS, 128])
        lbound = sb("lbound", [128, DEPTH, HEADS])
        lspan = sb("lspan", [128, DEPTH, HEADS])
        lb_tmp = sb("lb_tmp", [128, 4, HEADS])
        eps = sb("eps", [128, 1])
        root = sb("root", [128, T])
        rstd = sb("rstd", [128, T])
        pool_w = sb("pool_w", [128, 4, 128])
        raw = [sb(f"raw{i}", [128, FE, 128]) for i in range(RING)]
        w_hi = [sb(f"w_hi{i}", [128, FE, 128], f32r) for i in range(RING)]
        w_lo = [sb(f"w_lo{i}", [128, FE, 128], f32r) for i in range(RING)]
        router = sb("router", [128, KT, N_EXPERTS])
        logits = sb("logits", [128, 3, N_EXPERTS])
        rank = sb("rank", [128, 3, N_EXPERTS])
        first = sb("first", [128, 3, N_EXPERTS])
        second = sb("second", [128, 3, N_EXPERTS])
        chosen = sb("chosen", [128, 3, N_EXPERTS])
        picked = sb("picked", [128, 3, N_EXPERTS])
        tops = sb("tops", [128, 4, 3])
        gates = sb("gates", [128, 3, N_EXPERTS])
        slot = sb("slot", [128, 3, N_EXPERTS])
        over = sb("over", [128, 3, N_EXPERTS])
        slot_gate = sb("slot_gate", [128, N_EXPERTS])
        longest = sb("longest", [128, 1])
        longest_i = sb("longest_i", [128, 1], i32)
        arena_base = (nc.sbuf_base + 31) // 32 * 32
        arena_end = nc.sbuf_usable_end

        def at(name, shape, offset, dt=f32):
            size = 4
            for n in shape[1:]:
                size *= n
            assert arena_base + offset + size <= arena_end, (name, arena_base + offset + size - arena_end)
            return nc.alloc_sbuf_tensor_at("at_" + name, shape, dt, offset=arena_base + offset)

        act_hi = at("act_hi", [128, KT, T], 0, f32r)
        act_lo = at("act_lo", [128, KT, T], 8448, f32r)
        values = at("values", [128, 2, HG_WIDTH], 0)
        kdecT = at("kdecT", [128, 2, HG_WIDTH], 4096)
        hgo = at("hgo", [128, HEADS, T], 8192)
        hgo_sq = at("hgo_sq", [128, HEADS, T], 12416)
        state = at("state", [128, DEC, HEADS, 128], 16896)
        proj = at("proj", [128, 4, HEADS, T], 33280)
        mix_hi = at("mix_hi", [128, KT, T], 50176, f32r)
        mix_lo = at("mix_lo", [128, KT, T], 58624, f32r)
        up = at("up", [128, 4, PAD + T], 67072)
        win_a = at("win_a", [128, 4, PAD + T], 71552)
        win_b = at("win_b", [128, 4, PAD + T], 76032)
        sig = at("sig", [128, HEADS, T], 80512)
        keys = at("keys", [128, HEADS, T], 84736)
        logf = at("logf", [128, HEADS, SEQ], 88960)
        kdec = at("kdec", [128, HEADS, SEQ], 88960)
        decay = at("decay", [128, HEADS, SEQ], 93056)
        diff = [at(f"diff{i}", [128, HEADS, SEQ], 97152 + 4096 * i) for i in range(2)]
        sided = [at(f"sided{i}", [128, HEADS, SEQ], 105344 + 4096 * i) for i in range(2)]
        scores = at("scores", [128, 2, HEADS, SEG], 113536)
        scores_x = at("scores_x", [128, HEADS, SEG], 117632)
        pool_past = at("pool_past", [DEC * POOL_BUF, HG_WIDTH], 119680)
        segments = at("segments", [128, HEADS, SEQ], 109440)
        hg_rstd = at("hg_rstd", [128, HEADS, T], 97152)
        hg_tmp = at("hg_tmp", [128, HEADS, T], 101376)
        new_state = at("new_state", [128, HEADS, 128], 105600)
        pool_tail = at("pool_tail", [POOL_BUF + DEC, HG_WIDTH], 80512)
        square = at("square", [128, KT, T], 84736)
        x_rows = at("x_rows", [128, 3, D_MODEL], 97152)
        ffn_hi = at("ffn_hi", [128, FT, T], 33280, f32r)
        ffn_lo = at("ffn_lo", [128, FT, T], 56512, f32r)
        gate_in = [at(f"gate_in{i}", [128, T], 93440 + 1056 * i) for i in range(2)]
        gate_act = [at(f"gate_act{i}", [128, T], 95552 + 1056 * i) for i in range(2)]
        up_in = [at(f"up_in{i}", [128, T], 97664 + 1056 * i) for i in range(2)]
        packed = at("packed", [128, N_EXPERTS, 2, KT * CAP], 0, f32r)
        slot_hot = at("slot_hot", [128, N_EXPERTS, T], 65536, f32r)
        act_e = at("act_e", [128, D_FF_E], 73984)
        hid_hi = at("hid_hi", [128, FE, CAP], 79616, f32r)
        hid_lo = at("hid_lo", [128, FE, CAP], 85248, f32r)
        raw_e = raw + [at(f"raw_e{i}", [128, FE, 128], 90880 + 5632 * i) for i in range(RAW_RING - RING)]
        x_hi, x_lo = w_hi[3][:, 0:KT, :], w_lo[3][:, 0:KT, :]
        square_m = at("square_m", [128, KT, T], 33280)
        h_hi = at("h_hi", [128, 3, D_MODEL], 73984, f32r)
        scaled_m = at("scaled_m", [128, KT, T], 88960)
        h_lo = at("h_lo", [128, 3, D_MODEL], 97408, f32r)
        token_hot = at("token_hot", [128, 3, N_EXPERTS, CAP], 109696, f32r)
        greater = at("greater", [128, 3, N_EXPERTS, N_EXPERTS], 41728)
        equal = at("equal", [128, 3, N_EXPERTS, N_EXPERTS], 42496)
        h_all = at("h_all", [128, KT, T], 0)
        gate_w_all = at("gate_w_all", [128, KT, 128], 8448)
        up_w_all = at("up_w_all", [128, KT, 128], 12544)
        down_w_all = at("down_w_all", [128, D_MODEL], 16640)
        act_all = at("act_all", [128, T], 20736)
        over_all = at("over_all", [128, T], 21792)
        over_col = at("over_col", [128, 3], 22848)
        square_f = at("square_f", [128, KT, T], 90880)
        scaled_f = at("scaled_f", [128, KT, T], 99328)
        y_rows = at("y_rows", [128, 3, D_MODEL], 107776)

        h_saved = nc.dram_tensor("h_saved", (128, KT * T), f32).ap()
        bank = [ctx.enter_context(nc.psum_tensor(f"bank{i}", [128, 512], f32)) for i in range(8)]

        consts_in = sem("consts_in"); vecs_in = sem("vecs_in"); x_in = sem("x_in")
        state_in = sem("state_in"); past_in = sem("past_in"); pool_w_in = sem("pool_w_in")
        raw_full = [sem(f"raw_full{i}") for i in range(RING)]
        hi_done = sem("hi_done"); lo_done = sem("lo_done"); unit_used = sem("unit_used"); bank_read = sem("bank_read")
        vecs_turned = sem("vecs_turned"); vecs_ready = sem("vecs_ready"); lb_step = sem("lb_step"); lb_exp = sem("lb_exp")
        eps_set = sem("eps_set")
        x_turned = sem("x_turned"); x_loaded = sem("x_loaded")
        squared = sem("squared"); norm_hi = sem("norm_hi"); norm_lo = sem("norm_lo"); summed = sem("summed")
        rooted = sem("rooted"); rstd_done = sem("rstd_done")
        sig_done = sem("sig_done"); q_gated = sem("q_gated"); forget_done = sem("forget_done"); keys_done = sem("keys_done")
        g_gated = sem("g_gated"); logf_done = sem("logf_done"); decay_done = sem("decay_done"); segments_set = sem("segments_set")
        scores_zeroed = sem("scores_zeroed"); diff_done = sem("diff_done"); diff_exp = sem("diff_exp"); sided_done = sem("sided_done")
        scored = sem("scored"); scores_taken = sem("scores_taken")
        v_turned = sem("v_turned"); v_copied = sem("v_copied")
        state_decayed = sem("state_decayed"); v_spread = sem("v_spread"); state_done = sem("state_done"); state_out = sem("state_out")
        attended = sem("attended"); hgo_copied = sem("hgo_copied")
        end_exp = sem("end_exp"); end_diff = sem("end_diff"); kdec_done = sem("kdec_done"); kdec_turned = sem("kdec_turned"); kdec_copied = sem("kdec_copied")
        final_state = sem("final_state"); final_copied = sem("final_copied"); final_out = sem("final_out")
        hgo_squared = sem("hgo_squared"); hgo_summed = sem("hgo_summed"); hgo_rooted = sem("hgo_rooted"); hgo_rstd = sem("hgo_rstd")
        hgo_scaled = sem("hgo_scaled"); mix_hi_done = sem("mix_hi_done"); mix_lo_done = sem("mix_lo_done")
        pads_zeroed = sem("pads_zeroed"); windowed = sem("windowed"); past_summed = sem("past_summed"); past_added = sem("past_added")
        pooled = sem("pooled"); pool_mapped = sem("pool_mapped"); pool_hi = sem("pool_hi"); pool_lo = sem("pool_lo")
        tail_turned = sem("tail_turned"); tail_copied = sem("tail_copied"); tail_out = sem("tail_out"); shift_out = sem("shift_out")
        gate_scaled = sem("gate_scaled"); gate_done = sem("gate_done"); up_scaled = sem("up_scaled"); ffn_mult = sem("ffn_mult")
        ffn_hi_done = sem("ffn_hi_done"); ffn_lo_done = sem("ffn_lo_done")
        x_moe = sem("x_moe"); moe_added = sem("moe_added"); scaled_done = sem("scaled_done"); turned = sem("turned"); y_copied = sem("y_copied"); y_out = sem("y_out")

        router_in = sem("router_in"); logits_zeroed = sem("logits_zeroed"); routed = sem("routed"); route = sem("route"); route_exp = sem("route_exp")
        placed = sem("placed"); hot = sem("hot"); hot_turned = sem("hot_turned"); hot_copied = sem("hot_copied")
        h_turned = sem("h_turned"); h_hi_done = sem("h_hi_done"); h_lo_done = sem("h_lo_done"); h_out = sem("h_out")
        gathered = sem("gathered"); packed_hi = sem("packed_hi"); packed_lo = sem("packed_lo"); gate_slots = sem("gate_slots")
        moe_full = [sem(f"moe_full{i}") for i in range(RAW_RING)]
        moe_hi = sem("moe_hi"); moe_lo = sem("moe_lo"); moe_used = sem("moe_used")
        x_hi_set = sem("x_hi_set"); x_lo_set = sem("x_lo_set"); gate_silu = sem("gate_silu"); act_done = sem("act_done")
        hid_turned = sem("hid_turned"); hid_hi_done = sem("hid_hi_done"); hid_lo_done = sem("hid_lo_done")
        y_hi_done = sem("y_hi_done"); y_lo_done = sem("y_lo_done"); scattered = sem("scattered")
        all_in = sem("all_in"); all_w = sem("all_w"); all_spread = sem("all_spread"); all_col = sem("all_col")
        all_over = sem("all_over"); all_up = sem("all_up"); all_silu = sem("all_silu"); all_act = sem("all_act"); all_down = sem("all_down"); all_added = sem("all_added")

        def unit_source(name, it, s):
            layer = int(name[-1])
            if name[:2] == "in":
                w, col = a["w_in"][layer], ds(GROUPS[it] * 512 + s * 128, 128)
            elif name[:3] == "out":
                w, col = a["w_o"][layer], ds(it * 512 + s * 128, 128)
            elif name[:6] == "ffn_up":
                w, col = (a["ffn_w_gate"], a["ffn_w_up"])[s % 2][0], ds(it * 256 + (s // 2) * 128, 128)
            else:
                half = s % 2
                w, col = a["ffn_w_down"][0, half * D_FF_E:(half + 1) * D_FF_E, :], ds(it * 256 + (s // 2) * 128, 128)
            return w[:, col].rearrange("(k p) n -> p k n", p=128)

        def wait_x(eng, version, kt):
            if version == 0:
                eng.wait_ge(x_loaded, kt + 1)
            elif version in (1, 3):
                eng.wait_ge(bank_read, WO0[(version - 1) // 2] + kt + 1)
            elif version == 2:
                eng.wait_ge(bank_read, DN0 + 2 * kt + 2)
            else:
                eng.wait_ge(x_moe, kt + 1)

        TURN = [("gate", 1, k) for k in range(KT)] + [("down", 0, k) for k in range(FE)] + [("up", 1, k) for k in range(KT)]
        SPREAD = {5: (0, 1), 6: (2, 3), 7: (4, 5, 6, 7)}
        PIECES = ((0, 512), (512, 512), (1024, 384))
        ROUTED = 29

        block = ctx.enter_context(nc.Block())

        @block.sync
        def _(sp):
            for name, n0, units, kts in PASSES:
                def load(it, s, check=True):
                    if check:
                        sp.wait_ge(lo_done, n0 + 4 * it + s - 3)
                    sp.dma_start(raw[s][:, 0:kts, :], unit_source(name, it, s)).then_inc(raw_full[s], 16)
                first = 0
                if n0 == 0:
                    for s in range(RING):
                        load(0, s, check=False)
                    first = 1
                if name[:2] == "in":
                    for it in range(first, units // RING):
                        for s in range(RING):
                            load(it, s)
                else:
                    with sp.Fori(first, units // RING) as it:
                        for s in range(RING):
                            load(it, s)
                if name == "out0":
                    sp.wait_ge(state_out, 16)
                    for i in range(4):
                        sp.dma_start(state[:, 2 * i:2 * i + 2, :, :].rearrange("k b h v -> k (b h) v"),
                                     a["state_hgrn"][1, 2 * i:2 * i + 2].rearrange("b h k v -> k (b h) v")).then_inc(state_in, 16)
                    sp.wait_ge(pool_mapped, 4)
                    sp.dma_start(pool_w[:, :, :], a["pool_w"][1].rearrange("g c d -> c g d")).then_inc(pool_w_in, 16)
                    sp.dma_start(pool_past[:, :], a["state_pool"][1].rearrange("b r c -> (b r) c")).then_inc(past_in, 16)
            def load_e(j, e, kind, k, turn=None):
                u = j if turn is None else HEAD_UNITS + TURN_UNITS * turn + j
                slot_n = (j if turn is None else HEAD_UNITS + j) % RAW_RING
                if turn is None and j < RAW_RING:
                    if j < RING:
                        sp.wait_ge(lo_done, LAST_UNIT - RING + j + 1)
                    else:
                        sp.wait_ge(packed_lo, 16)
                        sp.wait_ge(h_out, 16)
                else:
                    sp.wait_ge(moe_lo, u - RAW_RING + 1)
                w = a["moe_w_" + kind][0]
                src = w[ds(e, 1), 128 * k:128 * (k + 1), :].rearrange("a p n -> p (a n)")
                dst = raw_e[slot_n][:, :, :].rearrange("p a b -> p (a b)")[:, 0:src.shape[1]]
                sp.dma_start(dst, src).then_inc(moe_full[slot_n], 16)
            for j in range(HEAD_UNITS):
                load_e(j, 0, ("gate", "up")[j // KT], j % KT)
            with sp.Fori(0, N_EXPERTS - 1) as e:
                for j, (kind, ahead, k) in enumerate(TURN):
                    load_e(j, e + ahead, kind, k, turn=e)
            for j in range(FE):
                load_e(j, N_EXPERTS - 1, "down", j, turn=N_EXPERTS - 1)
            sp.wait_ge(scattered, 8)
            sp.wait_ge(route, ROUTED)
            n_rows = sp.value_load(longest_i[0:1, 0:1])
            with sp.If(n_rows > CAP):
                sp.wait_ge(y_lo_done, 2 * N_EXPERTS + 1)
                sp.dma_start(h_all[:, :, :].rearrange("p k t -> p (k t)"), h_saved).then_inc(all_in, 16)
                with sp.Fori(0, N_EXPERTS) as e:
                    with sp.Fori(0, FE) as f:
                        n = e * FE + f
                        sp.wait_ge(all_added, n * KT + KT)
                        for dst, name in ((gate_w_all, "moe_w_gate"), (up_w_all, "moe_w_up")):
                            sp.dma_start(dst[:, :, :], a[name][0][ds(e, 1), :, ds(f * 128, 128)].rearrange("a (k p) n -> p (a k) n", p=128)).then_inc(all_w, 16)
                        sp.dma_start(down_w_all[:, :], a["moe_w_down"][0][ds(e, 1), ds(f * 128, 128), :].rearrange("a p n -> p (a n)")).then_inc(all_w, 16)
            sp.end_ifs()
            sp.wait_ge(y_out, 16 * 3)

        @block.gpsimd
        def _(gp):
            gp.dma_start(o["new_pool_sample"][:, :, 0:POOL_BUF - 1, :], a["state_pool"][:, :, 1:POOL_BUF, :]).then_inc(shift_out, 16)
            gp.memset(eps[:, :], EPS).then_inc(eps_set, 1)

            def square_x(version, out):
                if version:
                    gp.wait_ge(summed, version)
                for kt in range(KT):
                    wait_x(gp, version, kt)
                    gp.tensor_tensor(out[:, kt, :], xT[:, kt, :], xT[:, kt, :], ALU.mult).then_inc(squared, 1)

            for layer in range(DEPTH):
                L = layer
                if layer == 0:
                    square_x(0, square)
                gp.wait_ge(unit_used, IN0[L] + 1)
                gp.memset(up[:, :, 0:PAD], 0.0).then_inc(pads_zeroed, 1)
                gp.wait_ge(x_loaded, KT)
                gp.memset(scores[:, :, :, :], 0.0).then_inc(scores_zeroed, 1)
                gp.memset(segments[:, :, :], 1.0).then_inc(segments_set, 1)
                gp.wait_ge(segments_set, 2 * L + 1)
                gp.memset(segments[:, :, :].rearrange("p h (s t) -> p (h s) t", t=SEG)[:, :, 0:1], 0.0).then_inc(segments_set, 1)
                gp.wait_ge(forget_done, 4 * (L + 1))
                gp.tensor_scalar(keys[:, :, :], proj[:, 1, :, :], -1.0, 1.0, ALU.mult, ALU.add).then_inc(keys_done, 1)
                gp.wait_ge(decay_done, L + 1)
                for j, half in enumerate(LEVELS + (SEG,)):
                    if j == 2:
                        gp.wait_ge(state_in, 64 * (L + 1))
                        for h in range(HEADS):
                            fs = proj[:, 1, h, SEQ:T].unsqueeze(2).broadcast_to([128, DEC, 128])
                            gp.tensor_tensor(state[:, :, h, :], state[:, :, h, :], fs, ALU.mult).then_inc(state_decayed, 1)
                    if j >= 2:
                        gp.wait_ge(sided_done, 16 * L + 2 * (j - 1))
                    b = decay[:, :, :].rearrange("p h (n t) -> p (h n) t", t=2 * half)
                    d = diff[j % 2][:, :, :].rearrange("p h (n t) -> p (h n) t", t=2 * half)
                    width = 2 * half if half < SEG else half
                    n = HEADS * SEQ // (2 * half)
                    gp.tensor_tensor(d[:, :, 0:width], b[:, :, 0:width],
                                     b[:, :, half - 1:half].broadcast_to([128, n, width]), ALU.subtract).then_inc(diff_done, 1)
                gp.wait_ge(sided_done, 16 * L + 14)
                gp.tensor_tensor(diff[0][:, :, SEG:SEQ], decay[:, :, SEG:SEQ],
                                 decay[:, :, SEQ - 1:SEQ].broadcast_to([128, HEADS, SEG]), ALU.subtract).then_inc(end_diff, 1)
                gp.wait_ge(bank_read, IN0[L] + 20)
                src, dst = up, win_a
                for j in range(4):
                    back = 1 << j
                    lo = 2 * back - 1
                    if j:
                        gp.wait_ge(windowed, 8 * L + j)
                    gp.tensor_tensor(dst[:, j:, lo:PAD + SEQ], src[:, j:, lo:PAD + SEQ],
                                     src[:, j:, lo - back:PAD + SEQ - back], ALU.add).then_inc(windowed, 1)
                    src, dst = dst, (win_b if dst is win_a else win_a)
                for g in range(4):
                    w = (win_a, win_b)[g % 2]
                    gp.wait_ge(windowed, 8 * L + 4)
                    gp.tensor_tensor(w[:, g, PAD:2 * PAD], w[:, g, PAD:2 * PAD], corr[:, g, :], ALU.mult).then_inc(windowed, 1)
                gp.wait_ge(end_exp, 2 * (L + 1))
                gp.wait_ge(sided_done, 16 * (L + 1))
                gp.tensor_tensor(kdec[:, :, 0:SEG], sided[1][:, :, 0:SEG], diff[0][:, :, 0:1].broadcast_to([128, HEADS, SEG]), ALU.mult).then_inc(kdec_done, 1)
                gp.tensor_tensor(kdec[:, :, SEG:SEQ], keys[:, :, SEG:SEQ], diff[0][:, :, SEG:SEQ], ALU.mult).then_inc(kdec_done, 1)
                gp.wait_ge(state_done, 32 * (L + 1))
                gp.dma_start(o["new_hgrn_sample"][layer].rearrange("b h k v -> k (b h) v"),
                             state[:, :, :, :].rearrange("k b h v -> k (b h) v")).then_inc(state_out, 16)
                gp.wait_ge(tail_copied, L + 1)
                gp.dma_start(o["new_pool_prompt"][layer, 0], pool_tail[0:POOL_BUF, :]).then_inc(tail_out, 16)
                gp.dma_start(o["new_pool_sample"][layer, :, POOL_BUF - 1, :], pool_tail[POOL_BUF:, :]).then_inc(tail_out, 16)
                gp.wait_ge(final_copied, L + 1)
                gp.dma_start(o["new_hgrn_prompt"][layer, 0].rearrange("h k v -> k h v"), new_state[:, :, :]).then_inc(final_out, 16)
                gp.wait_ge(final_out, 16 * (L + 1))
                gp.wait_ge(tail_out, 32 * (L + 1))
                gp.wait_ge(state_out, 16 * (L + 1))
                if layer == 0:
                    square_x(1, square)
                    with gp.Fori(0, FT // 2) as it:
                        for i in range(2):
                            gp.wait_ge(ffn_hi_done, 2 * it + i + 1)
                            at_ft = ds(2 * it + i, 1)
                            gp.tensor_tensor(ffn_lo[:, at_ft, :].rearrange("p a t -> p (a t)"), gate_act[i][:, :],
                                             ffn_hi[:, at_ft, :].rearrange("p a t -> p (a t)").bitcast(f32), ALU.subtract).then_inc(ffn_lo_done, 1)
                    square_x(2, square)
            gp.memset(logits[:, :, :], 0.0).then_inc(logits_zeroed, 1)
            square_x(3, square_m)
            def set_x_lo(e, c, u):
                gp.wait_ge(packed_lo, 16)
                if u is None:
                    gp.wait_ge(unit_used, LAST_UNIT)
                else:
                    gp.wait_ge(moe_used, u)
                src = packed[:, ds(e, 1), 1, 512 * c:512 * (c + 1)].rearrange("p a n -> p (a n)")
                gp.tensor_copy(x_lo[:, 4 * c:4 * (c + 1), :].rearrange("p a b -> p (a b)"), src).then_inc(x_lo_set, 1)
            set_x_lo(0, 0, None)
            set_x_lo(0, 1, None)
            set_x_lo(1, 0, HEAD_UNITS - 4)
            with gp.Fori(0, N_EXPERTS - 2) as e:
                set_x_lo(e + 1, 1, HEAD_UNITS + TURN_UNITS * e)
                set_x_lo(e + 2, 0, HEAD_UNITS + TURN_UNITS * (e + 1) - 4)
            set_x_lo(N_EXPERTS - 1, 1, HEAD_UNITS + TURN_UNITS * (N_EXPERTS - 2))
            square_x(4, square_f)
            gp.wait_ge(shift_out, 16)

        @block.scalar
        def _(act):
            act.dma_start(consts[:, :], a["consts"]).then_inc(consts_in, 16)
            act.dma_start(x_rows[:, 0:2, :], a["x_prompt"][0].rearrange("(i p) d -> p i d", p=128)).then_inc(x_in, 16)
            act.dma_start(x_rows[0:DEC, 2, :], a["x_sample"][:, 0, :]).then_inc(x_in, 16)
            for row, name, src in ((V_MIX, "norm_mix", "l (k p) -> (l k) p"), (V_FFN, "norm_ffn", "l (k p) -> (l k) p"),
                                   (V_FINAL, "norm_final", "(k p) -> k p"), (V_LB, "lb_logits", "l (k p) -> (l k) p"),
                                   (V_HG, "hg_norm", "l (k p) -> (l k) p"), (V_POOL, "pool_scale", "l (k p) -> (l k) p")):
                view = a[name].rearrange(src, p=128)
                act.dma_start(vec_rows[row:row + view.shape[0], :], view).then_inc(vecs_in, 16)
            act.dma_start(pool_past[:, :], a["state_pool"][0].rearrange("b r c -> (b r) c")).then_inc(past_in, 16)
            act.dma_start(pool_w[:, :, :], a["pool_w"][0].rearrange("g c d -> c g d")).then_inc(pool_w_in, 16)
            for i in range(4):
                act.dma_start(state[:, 2 * i:2 * i + 2, :, :].rearrange("k b h v -> k (b h) v"),
                              a["state_hgrn"][0, 2 * i:2 * i + 2].rearrange("b h k v -> k (b h) v")).then_inc(state_in, 16)
            act.dma_start(router[:, :, :], a["router"][0].rearrange("(k p) e -> p k e", p=128)).then_inc(router_in, 16)
            act.wait_ge(lb_step, 3)
            act.activation(lb_tmp[:, 1:3, :], lb_tmp[:, 1:3, :], ACT.Exp).then_inc(lb_exp, 1)

            def split(s, k, n, kts, guard=True):
                act.wait_ge(raw_full[s], 16 * (k + 1))
                if guard:
                    act.wait_ge(unit_used, n - 3)
                act.activation(w_hi[s][:, 0:kts, :], raw[s][:, 0:kts, :], ACT.Copy).then_inc(hi_done, 1)

            def weight_pass(name, body, unroll=False, peel=False):
                i = [p[0] for p in PASSES].index(name)
                _, n0, units, kts = PASSES[i]
                its = units // RING

                def step(it, last):
                    for s in range(RING):
                        n = n0 + 4 * it + s
                        if s == 0:
                            split(3, n0 // 4 + it, n + 3, kts, guard=not (n0 == 0 and isinstance(it, int) and it == 0))
                        elif not last:
                            split(s - 1, n0 // 4 + it + 1, n + 3, kts)
                        elif i + 1 < len(PASSES):
                            split(s - 1, PASSES[i + 1][1] // 4, PASSES[i + 1][1] + s - 1, PASSES[i + 1][3])
                        if body:
                            body(it, s)
                first = 0
                if n0 == 0:
                    for s in range(3):
                        split(s, 0, s, kts, guard=False)
                if n0 == 0 or peel:
                    step(0, False)
                    first = 1
                if unroll:
                    for it in range(first, its - 1):
                        step(it, False)
                else:
                    with act.Fori(first, its - 1) as it:
                        step(it, False)
                step(its - 1, True)

            def scale_x(version, kt):
                col = (V_MIX, V_FFN, V_MIX + KT)[version]
                wait_x(act, version, kt)
                tile = lambda t: t[:, kt, :] if isinstance(kt, int) else t[:, ds(kt, 1), :].rearrange("p a t -> p (a t)")
                gain = vecs[:, col + kt:col + kt + 1] if isinstance(kt, int) else vecs[:, ds(col + kt, 1)]
                act.activation(tile(act_hi), tile(xT), ACT.Copy, scale=gain).then_inc(norm_hi, 1)

            def inverse_root(nth):
                act.wait_ge(summed, nth + 1)
                act.activation(root[:, :], bank[4][:, 0:T], ACT.Ln, scale=1.0 / D_MODEL, bias=eps[:, :]).then_inc(rooted, 1)
                act.wait_ge(rooted, nth + 1)
                act.activation(rstd[:, :], root[:, :], ACT.Exp, scale=-0.5).then_inc(rstd_done, 1)

            def token_norms(n):
                for i, (_, rows) in enumerate(TOKEN_TILES):
                    act.activation(root[0:rows, i:i + 1], bank[4][0:rows, i:i + 1], ACT.Ln, scale=1.0 / D_MODEL, bias=eps[0:rows, :]).then_inc(rooted, 1)
                for i, (_, rows) in enumerate(TOKEN_TILES):
                    act.wait_ge(rooted, n + i + 1)
                    act.activation(rstd[0:rows, i:i + 1], root[0:rows, i:i + 1], ACT.Exp, scale=-0.5).then_inc(rstd_done, 1)

            act.wait_ge(vecs_ready, 1)
            act.wait_ge(eps_set, 1)
            for kt in range(KT):
                scale_x(0, kt)
            inverse_root(0)
            for layer in range(DEPTH):
                L = layer
                if layer:
                    inverse_root(2)

                def mixer_step(it, s):
                    if (it, s) == (1, 0):
                        act.wait_ge(bank_read, IN0[L] + 4)
                        act.activation(sig[:, :, :], proj[:, 0, :, :], ACT.Sigmoid).then_inc(sig_done, 1)
                    if (it, s) == (2, 0):
                        act.wait_ge(bank_read, IN0[L] + 8)
                        act.activation(proj[:, 1, :, :], proj[:, 1, :, :], ACT.Sigmoid).then_inc(sig_done, 1)
                    if (it, s) == (2, 2):
                        act.wait_ge(forget_done, 4 * (L + 1))
                        act.activation(logf[:, :, :], proj[:, 1, :, 0:SEQ], ACT.Ln).then_inc(logf_done, 1)
                    if (it, s) == (3, 0):
                        act.wait_ge(bank_read, IN0[L] + 12)
                        act.wait_ge(q_gated, L + 1)
                        act.activation(sig[:, :, :], proj[:, 3, :, :], ACT.Sigmoid).then_inc(sig_done, 1)
                    if (it, s) in ACT_LEVELS:
                        exp_level(ACT_LEVELS[(it, s)])

                def exp_level(j):
                    half = (LEVELS + (SEG,))[j]
                    act.wait_ge(diff_done, 8 * L + j + 1)
                    d = diff[j % 2][:, :, :].rearrange("p h (n t) -> p (h n) t", t=2 * half)
                    right = d if half < SEG else decay[:, :, :].rearrange("p h (n t) -> p (h n) t", t=2 * half)
                    act.activation(d[:, :, 0:half], d[:, :, 0:half], ACT.Exp, scale=-1.0).then_inc(diff_exp, 1)
                    act.activation(d[:, :, half:], right[:, :, half:], ACT.Exp).then_inc(diff_exp, 1)
                ACT_LEVELS = {(3, 1): 0, (3, 3): 1, (4, 0): 2, (4, 1): 3, (4, 2): 4, (4, 3): 5}
                weight_pass(f"in{L}", mixer_step, unroll=True)
                for i in range(2):
                    act.wait_ge(v_turned, 2 * L + i + 1)
                    act.activation(values[:, i, :], bank[i][:, :], ACT.Copy).then_inc(v_copied, 1)
                for j in (6, 7):
                    exp_level(j)
                act.wait_ge(end_diff, L + 1)
                act.activation(diff[0][:, :, SEG:SEQ], diff[0][:, :, SEG:SEQ], ACT.Exp, scale=-1.0).then_inc(end_exp, 1)
                act.activation(diff[0][:, :, 0:1], decay[:, :, SEQ - 1:SEQ], ACT.Exp).then_inc(end_exp, 1)
                for i in range(3):
                    act.wait_ge(attended, 3 * L + i + 1)
                    tok = slice(SEG * i, SEG * (i + 1)) if i < 2 else slice(SEQ, T)
                    src = bank[(6, 7, 0)[i]][:, 0:HEADS * (SEG if i < 2 else DEC)].rearrange("p (h t) -> p h t", h=HEADS)
                    act.activation(hgo_sq[:, :, tok], src, ACT.Square).then_inc(hgo_squared, 1)
                    act.activation(hgo[:, :, tok], src, ACT.Copy).then_inc(hgo_copied, 1)
                for g in range(4):
                    act.wait_ge(pool_mapped, 4 * L + g + 1)
                    act.activation(mix_hi[:, 4 + g, :], bank[2 + g % 2][:, 0:T], ACT.Copy,
                                   scale=vecs[:, V_POOL + 4 * L + g:V_POOL + 4 * L + g + 1]).then_inc(pool_hi, 1)
                flat_rstd = hg_rstd[:, :, :].rearrange("p h t -> p (h t)")
                act.wait_ge(kdec_done, 2 * (L + 1))
                for i in range(3):
                    act.wait_ge(hgo_summed, 3 * L + i + 1)
                    act.activation(flat_rstd[:, 352 * i:352 * (i + 1)], bank[(5, 0, 1)[i]][:, 0:352], ACT.Ln, scale=1.0 / 128,
                                   bias=eps[:, :]).then_inc(hgo_rooted, 1)
                for i in range(3):
                    act.wait_ge(hgo_rooted, 3 * L + i + 1)
                    piece = flat_rstd[:, 352 * i:352 * (i + 1)]
                    act.activation(piece, piece, ACT.Exp, scale=-0.5).then_inc(hgo_rstd, 1)
                for i in range(2):
                    act.wait_ge(kdec_turned, 2 * L + i + 1)
                    act.activation(kdecT[:, i, :], bank[6 + i][:, :], ACT.Copy).then_inc(kdec_copied, 1)
                for h in range(HEADS):
                    act.wait_ge(hgo_scaled, 8 * L + 4 + h + 1)
                    act.activation(mix_hi[:, h, :], hg_tmp[:, h, :], ACT.Copy).then_inc(mix_hi_done, 1)
                act.wait_ge(final_state, L + 1)
                act.activation(new_state[:, :, :], bank[4][:, :].rearrange("p (h v) -> p h v", h=HEADS), ACT.Copy).then_inc(final_copied, 1)
                act.wait_ge(tail_turned, L + 1)
                act.wait_ge(g_gated, L + 1)
                act.activation(pool_tail[:, :], bank[3][0:POOL_BUF + DEC, :], ACT.Copy).then_inc(tail_copied, 1)

                def out_step(it, s):
                    if 4 * it + s and L == 0:
                        scale_x(1, 4 * it + s - 1)
                weight_pass(f"out{L}", out_step, unroll=True)
                if layer == 0:
                    scale_x(1, KT - 1)
                if layer == 0:
                    inverse_root(1)

                    def ffn_step(it, s):
                        i = s // 2
                        if s % 2 == 0:
                            act.wait_ge(bank_read, GU0 + 4 * it + s + 1)
                            if not (isinstance(it, int) and it == 0):
                                act.wait_ge(ffn_lo_done, 2 * it + i - 1)
                            act.activation(gate_act[i][:, :], gate_in[i][:, :], ACT.Silu).then_inc(gate_done, 1)
                        else:
                            act.wait_ge(ffn_mult, 2 * it + i + 1)
                            act.activation(ffn_hi[:, ds(2 * it + i, 1), :].rearrange("p a t -> p (a t)"), gate_act[i][:, :], ACT.Copy).then_inc(ffn_hi_done, 1)
                    weight_pass("ffn_up0", ffn_step, peel=True)

                    def down_step(it, s):
                        if s >= 2:
                            scale_x(2, 2 * it + s - 2)
                    weight_pass("ffn_down0", down_step)
            act.wait_ge(summed, 4)
            token_norms(3)
            act.wait_ge(scaled_done, KT)
            act.dma_start(h_saved, scaled_m[:, :, :].rearrange("p k t -> p (k t)")).then_inc(h_out, 16)
            act.wait_ge(tail_out, 64)
            for i, (_, rows) in enumerate(TOKEN_TILES):
                for c in range(2):
                    act.wait_ge(rstd_done, 3 + i + 1)
                    act.wait_ge(h_turned, 2 * i + c + 1)
                    act.activation(h_hi[0:rows, i, 512 * c:512 * (c + 1)], bank[2 + c][0:rows, :], ACT.Copy, scale=rstd[0:rows, i:i + 1]).then_inc(h_hi_done, 1)
                if i == 0:
                    act.wait_ge(route, 18)
                    act.activation(tops[:, 1, :], tops[:, 1, :], ACT.Exp).then_inc(route_exp, 1)
            for e in range(N_EXPERTS):
                act.wait_ge(hot_turned, e + 1)
                act.activation(slot_hot[:, e, :], bank[e % 2][:, 0:T], ACT.Copy).then_inc(hot_copied, 1)
            act.wait_ge(state_out, 32)
            for n in range(16):
                q, d = n // 4, n % 4
                act.wait_ge(gathered, n + 1)
                act.activation(packed[:, 2 * q:2 * q + 2, 0, 256 * d:256 * (d + 1)].rearrange("p e (d s) -> p e d s", d=2),
                               bank[n % 4][:, :].rearrange("p (d e s) -> p e d s", d=2, e=2), ACT.Copy).then_inc(packed_hi, 1)

            def split_e(j, kts_cols, turn=None):
                u = j if turn is None else HEAD_UNITS + TURN_UNITS * turn + j
                jj = j if turn is None else HEAD_UNITS + j
                uses = jj // RAW_RING if turn is None else TURN_UNITS // RAW_RING * turn + jj // RAW_RING
                act.wait_ge(moe_full[jj % RAW_RING], 16 * (uses + 1))
                if turn is None and j < SPLIT_RING:
                    act.wait_ge(unit_used, LAST_UNIT)
                else:
                    act.wait_ge(moe_used, u - SPLIT_RING + 1)
                act.activation(w_hi[jj % SPLIT_RING][:, 0:kts_cols, :], raw_e[jj % RAW_RING][:, 0:kts_cols, :], ACT.Copy).then_inc(moe_hi, 1)

            def set_x_hi(e, c, u):
                act.wait_ge(packed_lo, 16)
                if u is None:
                    act.wait_ge(unit_used, LAST_UNIT)
                else:
                    act.wait_ge(moe_used, u)
                src = packed[:, ds(e, 1), 0, 512 * c:512 * (c + 1)].rearrange("p a n -> p (a n)")
                act.activation(x_hi[:, 4 * c:4 * (c + 1), :].rearrange("p a b -> p (a b)"), src, ACT.Copy).then_inc(x_hi_set, 1)

            def silu_gate(e, u):
                act.wait_ge(moe_used, u)
                if not isinstance(e, int) or e:
                    act.wait_ge(hid_turned, 3 * e)
                for p, (c0, width) in enumerate(PIECES):
                    act.activation(act_e[:, c0:c0 + width], bank[p][:, 0:width], ACT.Silu).then_inc(gate_silu, 1)

            def round_hidden(e):
                for p, (c0, width) in enumerate(PIECES):
                    act.wait_ge(hid_turned, 3 * e + p + 1)
                    act.activation(hid_hi[:, c0 // 128:(c0 + width) // 128, :], bank[3 + p][:, 0:width].rearrange("p (a b) -> p a b", b=128), ACT.Copy).then_inc(hid_hi_done, 1)

            act.wait_ge(y_lo_done, 1)

            def round_result(e, u):
                act.wait_ge(moe_used, u)
                for c in range(2):
                    act.activation(packed[:, ds(e, 1), 0, 512 * c:512 * (c + 1)].rearrange("p a n -> p (a n)"), bank[6 + c][:, :], ACT.Copy,
                                   scale=slot_gate[:, ds(e, 1)]).then_inc(y_hi_done, 1)

            set_x_hi(0, 0, None)
            set_x_hi(0, 1, None)
            for j in range(HEAD_UNITS + LOAD_AHEAD):
                if j < HEAD_UNITS:
                    split_e(j, FE)
                else:
                    split_e(j - HEAD_UNITS, FE, turn=0)
                if j == KT + LOAD_AHEAD:
                    silu_gate(0, KT)
                if j == HEAD_UNITS - 4 + SPLIT_RING - 1:
                    set_x_hi(1, 0, HEAD_UNITS - 4)

            def turn_e(e, last):
                base = HEAD_UNITS + TURN_UNITS * e
                for j, (kind, _, k) in enumerate(TURN):
                    ahead = j + LOAD_AHEAD
                    if ahead < TURN_UNITS:
                        split_e(ahead, FE if TURN[ahead][0] != "down" else KT, turn=e)
                    else:
                        split_e(ahead - TURN_UNITS, KT if last else FE, turn=e + 1)
                    if j == 0:
                        set_x_hi(e + 1, 1, base)
                    if j == 5:
                        round_hidden(e)
                    if j == KT + 1:
                        silu_gate(e + 1, base + KT)
                    if j == KT + FE + 1:
                        round_result(e, base + KT + FE)
                    if j == TURN_UNITS - 3 and not last:
                        set_x_hi(e + 2, 0, base + TURN_UNITS - 4)
            with act.Fori(0, N_EXPERTS - 2) as e:
                turn_e(e, False)
            turn_e(N_EXPERTS - 2, True)
            round_hidden(N_EXPERTS - 1)
            for j in range(LOAD_AHEAD, FE):
                split_e(j, KT, turn=N_EXPERTS - 1)
            round_result(N_EXPERTS - 1, HEAD_UNITS + TURN_UNITS * (N_EXPERTS - 1) + FE)
            act.wait_ge(route, ROUTED)
            n_rows = act.value_load(longest_i[0:1, 0:1])
            with act.If(n_rows > CAP):
                with act.Fori(0, N_EXPERTS * FE) as n:
                    act.wait_ge(all_up, 2 * n + 1)
                    act.activation(act_all[:, :], bank[0][:, 0:T], ACT.Silu).then_inc(all_silu, 1)
            act.end_ifs()
            act.wait_ge(summed, 5)
            token_norms(6)
            for i, (_, rows) in enumerate(TOKEN_TILES):
                for c in range(2):
                    act.wait_ge(rstd_done, 6 + i + 1)
                    act.wait_ge(turned, 2 * i + c + 1)
                    act.activation(y_rows[0:rows, i, 512 * c:512 * (c + 1)], bank[5 + (2 * i + c) % 2][0:rows, :], ACT.Copy,
                                   scale=rstd[0:rows, i:i + 1]).then_inc(y_copied, 1)
                act.wait_ge(y_copied, 2 * (i + 1))
                dst = o["y_prompt"][0, 128 * i:128 * (i + 1), :] if i < 2 else o["y_sample"][:, 0, :]
                act.dma_start(dst, y_rows[0:rows, i, :]).then_inc(y_out, 16)
        @block.vector
        def _(dve):
            dve.wait_ge(vecs_turned, 1)
            dve.tensor_copy(vecs[:, :], bank[7][:, 0:V_COLS]).then_inc(vecs_ready, 1)
            dve.wait_ge(vecs_ready, 1)
            l0, l1 = vecs[:, V_LB:V_LB + HEADS], vecs[:, V_LB + HEADS:V_LB + 2 * HEADS]
            top, e0, e1, inv = (lb_tmp[:, i, :] for i in range(4))
            dve.tensor_tensor(top, l0, l1, ALU.max).then_inc(lb_step, 1)
            dve.wait_ge(lb_step, 1)
            dve.tensor_tensor(e0, l0, top, ALU.subtract).then_inc(lb_step, 1)
            dve.tensor_tensor(e1, l1, top, ALU.subtract).then_inc(lb_step, 1)
            dve.wait_ge(lb_exp, 1)
            dve.tensor_tensor(top, e0, e1, ALU.add).then_inc(lb_step, 1)
            dve.wait_ge(lb_step, 4)
            dve.reciprocal(inv, top).then_inc(lb_step, 1)
            dve.wait_ge(lb_step, 5)
            dve.tensor_tensor(e0, e0, inv, ALU.mult).then_inc(lb_step, 1)
            dve.tensor_tensor(e1, e1, inv, ALU.mult).then_inc(lb_step, 1)
            dve.wait_ge(lb_step, 7)
            dve.tensor_tensor(top, e0, e1, ALU.add).then_inc(lb_step, 1)
            dve.tensor_tensor(lbound[:, 0, :], e0, e0, ALU.subtract).then_inc(lb_step, 1)
            dve.wait_ge(lb_step, 8)
            dve.tensor_tensor(lbound[:, 1, :], top, e0, ALU.subtract).then_inc(lb_step, 1)
            dve.wait_ge(lb_step, 10)
            dve.tensor_scalar(lspan[:, :, :], lbound[:, :, :], -1.0, 1.0, ALU.mult, ALU.add).then_inc(lb_step, 1)
            for kt in range(KT):
                dve.wait_ge(x_turned, kt + 1)
                dve.tensor_copy(xT[:, kt, :], bank[kt % 4][:, 0:T]).then_inc(x_loaded, 1)

            def split(s, n, kts):
                dve.wait_ge(hi_done, n + 1)
                dve.tensor_tensor(w_lo[s][:, 0:kts, :], raw[s][:, 0:kts, :], w_hi[s][:, 0:kts, :].bitcast(f32), ALU.subtract).then_inc(lo_done, 1)

            def weight_pass(name, body, unroll=False):
                i = [p[0] for p in PASSES].index(name)
                _, n0, units, kts = PASSES[i]
                its = units // RING

                def step(it, last):
                    for s in range(RING):
                        n = n0 + 4 * it + s
                        if s == 0:
                            split(3, n + 3, kts)
                        elif not last:
                            split(s - 1, n + 3, kts)
                        elif i + 1 < len(PASSES):
                            split(s - 1, PASSES[i + 1][1] + s - 1, PASSES[i + 1][3])
                        body(it, s)
                if n0 == 0:
                    for s in range(3):
                        split(s, s, kts)
                if unroll:
                    for it in range(its - 1):
                        step(it, False)
                else:
                    with dve.Fori(0, its - 1) as it:
                        step(it, False)
                step(its - 1, True)

            def scale_x(version, kt):
                col = (V_MIX, V_FFN, V_MIX + KT)[version]
                dve.wait_ge(norm_hi, KT * version + kt + 1)
                tile = lambda t: t[:, kt, :] if isinstance(kt, int) else t[:, ds(kt, 1), :].rearrange("p a t -> p (a t)")
                gain = vecs[:, col + kt:col + kt + 1] if isinstance(kt, int) else vecs[:, ds(col + kt, 1)]
                dve.scalar_tensor_tensor(tile(act_lo), tile(xT), gain, tile(act_hi).bitcast(f32), ALU.mult, ALU.subtract).then_inc(norm_lo, 1)

            dve.wait_ge(x_loaded, KT)
            for kt in range(KT):
                scale_x(0, kt)
            for layer in range(DEPTH):
                L = layer

                def mixer_step(it, s):
                    n = IN0[L] + 4 * it + s
                    dve.wait_ge(unit_used, n + 1)
                    dve.wait_ge(rstd_done, (1, 3)[L])
                    out = proj[:, GROUPS[it], s, :] if it < 4 else up[:, s, PAD:]
                    dve.tensor_tensor(out, bank[s][:, 0:T], rstd[:, :], ALU.mult).then_inc(bank_read, 1)
                    if (it, s) == (1, 3):
                        dve.wait_ge(sig_done, 3 * L + 1)
                        dve.wait_ge(bank_read, IN0[L] + 4)
                        dve.tensor_tensor(proj[:, 0, :, :], proj[:, 0, :, :], sig[:, :, :], ALU.mult).then_inc(q_gated, 1)
                    if (it, s) == (2, 1):
                        dve.wait_ge(lb_step, 11)
                        dve.wait_ge(sig_done, 3 * L + 2)
                        for h in range(HEADS):
                            dve.tensor_scalar(proj[:, 1, h, :], proj[:, 1, h, :], lspan[:, L, h:h + 1], lbound[:, L, h:h + 1],
                                              ALU.mult, ALU.add).then_inc(forget_done, 1)
                    if (it, s) == (2, 3):
                        dve.wait_ge(logf_done, L + 1)
                        dve.wait_ge(segments_set, 2 * (L + 1))
                        dve.tensor_tensor_scan(decay[:, :, :].rearrange("p h t -> p (h t)"), segments[:, :, :].rearrange("p h t -> p (h t)"),
                                               logf[:, :, :].rearrange("p h t -> p (h t)"), 0.0, ALU.mult, ALU.add).then_inc(decay_done, 1)
                    if (it, s) == (3, 2):
                        side(0)
                    if (it, s) == (3, 3):
                        take(0)
                        take(1)
                    if it == 4:
                        side(s + 1)
                        take(2 * s + 2)
                        take(2 * s + 3)

                def side(j):
                    half = (LEVELS + (SEG,))[j]
                    e, z, q, k = (t.rearrange("p h (n t) -> p h n t", t=2 * half)
                                  for t in (diff[j % 2][:, :, :], sided[j % 2][:, :, :], proj[:, 0, :, 0:SEQ], keys[:, :, 0:SEQ]))
                    if j >= 2:
                        dve.wait_ge(scored, 17 * L + 2 * j)
                    if j == 0:
                        dve.wait_ge(keys_done, L + 1)
                        dve.wait_ge(q_gated, L + 1)
                    if j == 1:
                        dve.wait_ge(decay_done, L + 1)
                    dve.wait_ge(diff_exp, 16 * L + 2 * j + 1)
                    dve.tensor_tensor(z[:, :, :, 0:half], e[:, :, :, 0:half], k[:, :, :, 0:half], ALU.mult).then_inc(sided_done, 1)
                    dve.wait_ge(diff_exp, 16 * L + 2 * j + 2)
                    dve.tensor_tensor(z[:, :, :, half:], e[:, :, :, half:], q[:, :, :, half:], ALU.mult).then_inc(sided_done, 1)

                def take(i):
                    dve.wait_ge(scored, 17 * L + i + 1)
                    src = bank[4 + i % 4][:, :].rearrange("p (h t) -> p h t", h=HEADS)
                    if i == 16:
                        dve.tensor_copy(scores_x[:, :, :], src).then_inc(scores_taken, 1)
                        return
                    if i >= 2:
                        dve.wait_ge(scores_taken, 17 * L + i - 1)
                    else:
                        dve.wait_ge(scores_zeroed, L + 1)
                    mask = consts[:, C_MASK + 128 * (i // 2):C_MASK + 128 * (i // 2 + 1)].bitcast(i32)
                    dve.copy_predicated(scores[:, i % 2, :, :], mask.unsqueeze(1).broadcast_to([128, HEADS, SEG]), src).then_inc(scores_taken, 1)

                def new_sample_state(b):
                    dve.wait_ge(v_spread, 8 * L + b + 1)
                    dve.wait_ge(state_decayed, 4 * (L + 1))
                    for h in range(HEADS):
                        dve.scalar_tensor_tensor(state[:, b, h, :], bank[b % 2][:, 128 * h:128 * (h + 1)], keys[:, h, SEQ + b:SEQ + b + 1],
                                                 state[:, b, h, :], ALU.mult, ALU.add).then_inc(state_done, 1)
                weight_pass(f"in{L}", mixer_step, unroll=True)
                for j in (5, 6, 7):
                    side(j)
                    take(2 * j)
                    take(2 * j + 1)
                    if j > 5:
                        for b in SPREAD[j - 1]:
                            new_sample_state(b)
                take(16)
                for b in SPREAD[7]:
                    new_sample_state(b)
                dve.wait_ge(sig_done, 3 * L + 3)
                dve.tensor_tensor(proj[:, 3, :, :], proj[:, 3, :, :], sig[:, :, :], ALU.mult).then_inc(g_gated, 1)
                dve.wait_ge(past_summed, L + 1)
                for g in range(4):
                    w = (win_a, win_b)[g % 2]
                    dve.tensor_tensor(w[:, g, PAD + SEQ:], bank[2][:, DEC * g:DEC * (g + 1)], up[:, g, PAD + SEQ:], ALU.add).then_inc(past_added, 1)
                dve.wait_ge(g_gated, L + 1)
                dve.wait_ge(hgo_copied, 3 * (L + 1))
                for h in range(HEADS):
                    dve.scalar_tensor_tensor(hg_tmp[:, h, :], hgo[:, h, :], vecs[:, V_HG + 4 * L + h:V_HG + 4 * L + h + 1],
                                             proj[:, 3, h, :], ALU.mult, ALU.mult).then_inc(hgo_scaled, 1)
                dve.wait_ge(windowed, 8 * (L + 1))
                for g in range(4):
                    w = (win_a, win_b)[g % 2]
                    dve.wait_ge(past_added, 4 * L + g + 1)
                    dve.scalar_tensor_tensor(w[:, g, PAD:], w[:, g, PAD:], 1.0 / WINDOWS[g], up[:, g, PAD:], ALU.mult, ALU.subtract).then_inc(pooled, 1)
                for g in range(4):
                    dve.wait_ge(pool_hi, 4 * L + g + 1)
                    dve.scalar_tensor_tensor(mix_lo[:, 4 + g, :], bank[2 + g % 2][:, 0:T], vecs[:, V_POOL + 4 * L + g:V_POOL + 4 * L + g + 1],
                                             mix_hi[:, 4 + g, :].bitcast(f32), ALU.mult, ALU.subtract).then_inc(pool_lo, 1)
                dve.wait_ge(hgo_rstd, 3 * (L + 1))
                for h in range(HEADS):
                    dve.wait_ge(hgo_scaled, 8 * L + h + 1)
                    dve.tensor_tensor(hg_tmp[:, h, :], hg_tmp[:, h, :], hg_rstd[:, h, :], ALU.mult).then_inc(hgo_scaled, 1)
                for h in range(HEADS):
                    dve.wait_ge(mix_hi_done, 4 * L + h + 1)
                    dve.tensor_tensor(mix_lo[:, h, :], hg_tmp[:, h, :], mix_hi[:, h, :].bitcast(f32), ALU.subtract).then_inc(mix_lo_done, 1)

                def scale_m(kt):
                    wait_x(dve, 3, kt)
                    dve.tensor_scalar(scaled_m[:, kt, :], xT[:, kt, :], vecs[:, V_FFN + KT + kt:V_FFN + KT + kt + 1], None, ALU.mult).then_inc(scaled_done, 1)

                def out_step(it, s):
                    kt = 4 * it + s
                    dve.wait_ge(unit_used, WO0[L] + kt + 1)
                    dve.tensor_tensor(xT[:, kt, :], bank[s][:, 0:T], xT[:, kt, :], ALU.add).then_inc(bank_read, 1)
                    if kt and L == 0:
                        scale_x(1, kt - 1)
                    if kt and L == 1:
                        scale_m(kt - 1)
                weight_pass(f"out{L}", out_step, unroll=True)
                if layer == 0:
                    scale_x(1, KT - 1)

                    def ffn_step(it, s):
                        i = s // 2
                        n = GU0 + 4 * it + s
                        dve.wait_ge(unit_used, n + 1)
                        out = (gate_in, up_in)[s % 2][i]
                        dve.wait_ge(rstd_done, 2)
                        dve.tensor_tensor(out[:, :], bank[s][:, 0:T], rstd[:, :], ALU.mult).then_inc(bank_read, 1)
                        if s % 2:
                            dve.wait_ge(gate_done, 2 * it + i + 1)
                            dve.wait_ge(bank_read, n + 1)
                            dve.tensor_tensor(gate_act[i][:, :], gate_act[i][:, :], up_in[i][:, :], ALU.mult).then_inc(ffn_mult, 1)
                    weight_pass("ffn_up0", ffn_step)

                    def down_step(it, s):
                        if s % 2:
                            dve.wait_ge(unit_used, DN0 + 4 * it + s + 1)
                            col = xT[:, ds(2 * it + s // 2, 1), :].rearrange("p a t -> p (a t)") if not isinstance(it, int) else xT[:, 2 * it + s // 2, :]
                            dve.tensor_tensor(col, bank[s - 1][:, 0:T], col, ALU.add).then_inc(bank_read, 2)
                        if s >= 2:
                            scale_x(2, 2 * it + s - 2)
                    weight_pass("ffn_down0", down_step)
            scale_m(KT - 1)
            dve.wait_ge(routed, 1)
            dve.wait_ge(logits_zeroed, 1)
            steps = [0]

            def step_of(ins):
                ins.then_inc(route, 1)
                steps[0] += 1
                dve.wait_ge(route, steps[0])
            for i, (_, rows) in enumerate(TOKEN_TILES):
                dve.wait_ge(rstd_done, 3 + i + 1)
                step_of(dve.tensor_scalar(logits[0:rows, i, :], bank[7][0:rows, 8 * i:8 * (i + 1)], rstd[0:rows, i:i + 1], None, ALU.mult))
            wide = [128, 3, N_EXPERTS, N_EXPERTS]
            each = logits[:, :, :].unsqueeze(2).broadcast_to(wide)
            own = logits[:, :, :].unsqueeze(3).broadcast_to(wide)
            lower = consts[:, C_LOWER:C_LOWER + 64].rearrange("p (e j) -> p e j", e=8)
            step_of(dve.tensor_tensor(greater[:, :, :, :], each, own, ALU.is_gt))
            step_of(dve.tensor_tensor(equal[:, :, :, :], each, own, ALU.is_equal))
            for i in range(3):
                step_of(dve.tensor_tensor(equal[:, i, :, :], equal[:, i, :, :], lower, ALU.mult))
            step_of(dve.tensor_tensor(greater[:, :, :, :], greater[:, :, :, :], equal[:, :, :, :], ALU.add))
            step_of(dve.tensor_reduce(rank[:, :, :], greater[:, :, :, :], AX.X, ALU.add))
            step_of(dve.tensor_single_scalar(first[:, :, :], rank[:, :, :], 0.0, ALU.is_equal))
            step_of(dve.tensor_single_scalar(second[:, :, :], rank[:, :, :], 1.0, ALU.is_equal))
            step_of(dve.tensor_tensor(picked[:, :, :], logits[:, :, :], first[:, :, :], ALU.mult))
            step_of(dve.tensor_reduce(tops[:, 0, :], picked[:, :, :], AX.X, ALU.add))
            step_of(dve.tensor_tensor(picked[:, :, :], logits[:, :, :], second[:, :, :], ALU.mult))
            step_of(dve.tensor_reduce(tops[:, 1, :], picked[:, :, :], AX.X, ALU.add))
            step_of(dve.tensor_tensor(chosen[:, :, :], first[:, :, :], second[:, :, :], ALU.add))
            step_of(dve.tensor_tensor(tops[:, 1, :], tops[:, 1, :], tops[:, 0, :], ALU.subtract))
            dve.wait_ge(route_exp, 1)
            step_of(dve.tensor_scalar(tops[:, 2, :], tops[:, 1, :], 1.0, None, ALU.add))
            step_of(dve.reciprocal(tops[:, 2, :], tops[:, 2, :]))
            step_of(dve.tensor_tensor(tops[:, 3, :], tops[:, 1, :], tops[:, 2, :], ALU.mult))
            per = [128, 3, N_EXPERTS]
            step_of(dve.tensor_tensor(gates[:, :, :], first[:, :, :], tops[:, 2, :].unsqueeze(2).broadcast_to(per), ALU.mult))
            step_of(dve.tensor_tensor(second[:, :, :], second[:, :, :], tops[:, 3, :].unsqueeze(2).broadcast_to(per), ALU.mult))
            step_of(dve.tensor_tensor(gates[:, :, :], gates[:, :, :], second[:, :, :], ALU.add))
            dve.wait_ge(placed, 1)
            flat = slot[:, :, :].rearrange("p i e -> p (i e)")
            step_of(dve.scalar_tensor_tensor(flat, bank[5][:, 0:24], 1.0, chosen[:, :, :].rearrange("p i e -> p (i e)"), ALU.add, ALU.mult))
            step_of(dve.tensor_scalar(flat, flat, -1.0, None, ALU.add))
            step_of(dve.tensor_reduce(longest[:, :], bank[5][:, 24:32], AX.X, ALU.max))
            step_of(dve.tensor_copy(longest_i[:, :], longest[:, :]))
            step_of(dve.scalar_tensor_tensor(over[:, :, :], slot[:, :, :], float(CAP), gates[:, :, :], ALU.is_ge, ALU.mult))
            assert steps[0] == ROUTED, steps[0]
            for i, (_, rows) in enumerate(TOKEN_TILES):
                for e in range(N_EXPERTS):
                    dve.tensor_scalar(token_hot[0:rows, i, e, :], iota[0:rows, :], slot[0:rows, i, e:e + 1], None, ALU.is_equal).then_inc(hot, 1)
            dve.wait_ge(final_out, 32)
            for i, (_, rows) in enumerate(TOKEN_TILES):
                for c in range(2):
                    dve.wait_ge(h_hi_done, 2 * i + c + 1)
                    dve.scalar_tensor_tensor(h_lo[0:rows, i, 512 * c:512 * (c + 1)], bank[2 + c][0:rows, :], rstd[0:rows, i:i + 1],
                                             h_hi[0:rows, i, 512 * c:512 * (c + 1)].bitcast(f32), ALU.mult, ALU.subtract).then_inc(h_lo_done, 1)
            dve.wait_ge(gate_slots, 1)
            dve.tensor_copy(slot_gate[:, :], bank[6][:, 0:N_EXPERTS]).then_inc(y_lo_done, 1)
            for n in range(16):
                q, d = n // 4, n % 4
                dve.wait_ge(packed_hi, n + 1)
                view = [packed[:, 2 * q:2 * q + 2, half, 256 * d:256 * (d + 1)].rearrange("p e (d s) -> p e d s", d=2) for half in range(2)]
                dve.tensor_tensor(view[1], bank[n % 4][:, :].rearrange("p (d e s) -> p e d s", d=2, e=2), view[0].bitcast(f32), ALU.subtract).then_inc(packed_lo, 1)

            def split_e(j, kts_cols, turn=None):
                u = j if turn is None else HEAD_UNITS + TURN_UNITS * turn + j
                jj = j if turn is None else HEAD_UNITS + j
                dve.wait_ge(moe_hi, u + 1)
                hi, lo = w_hi[jj % SPLIT_RING][:, 0:kts_cols, :], w_lo[jj % SPLIT_RING][:, 0:kts_cols, :]
                dve.tensor_tensor(lo, raw_e[jj % RAW_RING][:, 0:kts_cols, :], hi.bitcast(f32), ALU.subtract).then_inc(moe_lo, 1)

            def gate_up(e, u):
                dve.wait_ge(moe_used, u)
                for p, (c0, width) in enumerate(PIECES):
                    dve.wait_ge(gate_silu, 3 * e + p + 1)
                    dve.tensor_tensor(act_e[:, c0:c0 + width], bank[3 + p][:, 0:width], act_e[:, c0:c0 + width], ALU.mult).then_inc(act_done, 1)

            def rest_of_hidden(e):
                for p, (c0, width) in enumerate(PIECES):
                    dve.wait_ge(hid_hi_done, 3 * e + p + 1)
                    ks = slice(c0 // 128, (c0 + width) // 128)
                    dve.tensor_tensor(hid_lo[:, ks, :], bank[3 + p][:, 0:width].rearrange("p (a b) -> p a b", b=128), hid_hi[:, ks, :].bitcast(f32), ALU.subtract).then_inc(hid_lo_done, 1)

            def rest_of_result(e):
                for c in range(2):
                    dve.wait_ge(y_hi_done, 2 * e + c + 1)
                    hi, lo = (packed[:, ds(e, 1), half, 512 * c:512 * (c + 1)].rearrange("p a n -> p (a n)") for half in range(2))
                    dve.scalar_tensor_tensor(lo, bank[6 + c][:, :], slot_gate[:, ds(e, 1)], hi.bitcast(f32), ALU.mult, ALU.subtract).then_inc(y_lo_done, 1)

            for j in range(HEAD_UNITS + LOAD_AHEAD):
                if j < HEAD_UNITS:
                    split_e(j, FE)
                else:
                    split_e(j - HEAD_UNITS, FE, turn=0)

            def turn_e(e, last):
                for j in range(TURN_UNITS):
                    ahead = j + LOAD_AHEAD
                    if j == 0:
                        gate_up(e, HEAD_UNITS + TURN_UNITS * e)
                    if ahead < TURN_UNITS:
                        split_e(ahead, FE if TURN[ahead][0] != "down" else KT, turn=e)
                    else:
                        split_e(ahead - TURN_UNITS, KT if last else FE, turn=e + 1)
                    if j == 5:
                        rest_of_hidden(e)
                    if j == KT + FE + 1:
                        rest_of_result(e)
            with dve.Fori(0, N_EXPERTS - 2) as e:
                turn_e(e, False)
            turn_e(N_EXPERTS - 2, True)
            gate_up(N_EXPERTS - 1, HEAD_UNITS + TURN_UNITS * (N_EXPERTS - 1))
            rest_of_hidden(N_EXPERTS - 1)
            for j in range(LOAD_AHEAD, FE):
                split_e(j, KT, turn=N_EXPERTS - 1)
            rest_of_result(N_EXPERTS - 1)
            for kt in range(KT):
                dve.wait_ge(scattered, kt + 1)
                dve.tensor_tensor(xT[:, kt, :], bank[kt][:, 0:T], xT[:, kt, :], ALU.add).then_inc(moe_added, 1)
            n_rows = dve.value_load(longest_i[0:1, 0:1])
            with dve.If(n_rows > CAP):
                dve.wait_ge(all_in, 16)
                dve.wait_ge(all_spread, 1)
                for kt in range(KT):
                    dve.tensor_tensor(h_all[:, kt, :], bank[2][:, 0:T], h_all[:, kt, :], ALU.mult).then_inc(all_added, 1)
                with dve.Fori(0, N_EXPERTS) as e:
                    dve.tensor_copy(over_col[:, :], over[:, :, ds(e, 1)].rearrange("p i a -> p (i a)")).then_inc(all_col, 1)
                    dve.wait_ge(all_spread, e + 2)
                    dve.tensor_copy(over_all[:, :], bank[2][:, 0:T]).then_inc(all_over, 1)
                    with dve.Fori(0, FE) as f:
                        n = e * FE + f
                        dve.wait_ge(all_silu, n + 1)
                        dve.wait_ge(all_up, 2 * n + 2)
                        dve.tensor_tensor(act_all[:, :], bank[1][:, 0:T], act_all[:, :], ALU.mult).then_inc(all_act, 1)
                        dve.wait_ge(all_act, 2 * n + 1)
                        dve.wait_ge(all_over, e + 1)
                        dve.tensor_tensor(act_all[:, :], act_all[:, :], over_all[:, :], ALU.mult).then_inc(all_act, 1)
                        for kt in range(KT):
                            dve.wait_ge(all_down, n * KT + kt + 1)
                            dve.tensor_tensor(xT[:, kt, :], bank[4 + kt % 4][:, 0:T], xT[:, kt, :], ALU.add).then_inc(all_added, 1)
                dve.wait_ge(all_added, N_EXPERTS * FE * KT + KT)
            dve.end_ifs()
            dve.wait_ge(moe_added, KT)
            for kt in range(KT):
                dve.engine_nop().then_inc(x_moe, 1)
            dve.wait_ge(final_out, 32)
            for kt in range(KT):
                wait_x(dve, 4, kt)
                dve.tensor_scalar(scaled_f[:, kt, :], xT[:, kt, :], vecs[:, V_FINAL + kt:V_FINAL + kt + 1], None, ALU.mult).then_inc(scaled_done, 1)

        @block.tensor
        def _(pe):
            pe.wait_ge(consts_in, 16)
            pe.wait_ge(vecs_in, 16 * 6)
            pe.transpose(bank[7][:, 0:V_COLS], vec_rows[:, :], ident[0:V_COLS, 0:V_COLS]).then_inc(vecs_turned, 1)
            pe.wait_ge(x_in, 32)
            for kt in range(KT):
                if kt >= 4:
                    pe.wait_ge(x_loaded, kt - 3)
                for i, (t0, rows) in enumerate(TOKEN_TILES):
                    mm = pe.transpose(bank[kt % 4][:, t0:t0 + rows], x_rows[0:rows, i, 128 * kt:128 * (kt + 1)], ident[0:rows, 0:rows])
                mm.then_inc(x_turned, 1)

            def sum_squares(nth):
                for kt in range(KT):
                    pe.wait_ge(squared, KT * nth + kt + 1)
                    mm = pe.matmul(bank[4][:, 0:T], ones, square[:, kt, :], start=(kt == 0), stop=(kt == KT - 1))
                mm.then_inc(summed, 1)

            def weight_pass(name, hi, lo, part=(0, None), between=None):
                _, n0, units, kts = PASS[name]
                halves = 2 if name[:8] == "ffn_down" else 1

                def step(it, first=False):
                    for s in range(RING):
                        n = n0 + 4 * it + s
                        half = s % halves
                        out = bank[s - half]
                        pe.wait_ge(lo_done, n + 1)
                        if half == 0 and not first:
                            pe.wait_ge(bank_read, n - 4 + halves)
                        for k in range(kts):
                            c = half * kts + k
                            pe.matmul(out[:, 0:T], w_hi[s][:, k, :], hi[:, c, :], start=(c == 0), stop=False)
                            pe.matmul(out[:, 0:T], w_hi[s][:, k, :], lo[:, c, :], start=False, stop=False)
                            mm = pe.matmul(out[:, 0:T], w_lo[s][:, k, :], hi[:, c, :], start=False,
                                           stop=(c == halves * kts - 1))
                        mm.then_inc(unit_used, 1)
                        if between:
                            between(it, s)
                first = part[0]
                if n0 + 4 * first == 0:
                    pe.wait_ge(x_loaded, KT)
                    step(0, first=True)
                    first = 1
                end = part[1] or units // RING
                if between:
                    for it in range(first, end):
                        step(it)
                else:
                    with pe.Fori(first, end) as it:
                        step(it)

            for layer in range(DEPTH):
                L = layer
                nth = 2 * L
                sum_squares(nth)
                pe.wait_ge(norm_lo, KT * (nth + 1))
                q, k, v = proj[:, 0, :, :], keys[:, :, :], proj[:, 2, :, :]

                def score(i, left, right):
                    if i >= 4:
                        pe.wait_ge(scores_taken, 17 * L + i - 3)
                    for h in range(HEADS):
                        mm = pe.matmul(bank[4 + i % 4][:, 128 * h:128 * (h + 1)], left(h), right(h), start=True, stop=True)
                    mm.then_inc(scored, 1)

                def score_level(j):
                    if j < 0:
                        pe.wait_ge(q_gated, L + 1)
                        pe.wait_ge(keys_done, L + 1)
                    else:
                        pe.wait_ge(sided_done, 16 * L + 2 * j + 2)
                    z = sided[j % 2]
                    if j == len(LEVELS):
                        score(16, lambda h: z[:, h, 0:SEG], lambda h: z[:, h, SEG:SEQ])
                        return
                    for i in range(2):
                        tok = slice(SEG * i, SEG * (i + 1))
                        if j < 0:
                            score(i, lambda h: k[:, h, tok], lambda h: q[:, h, tok])
                        else:
                            score(2 * j + 2 + i, lambda h: z[:, h, tok], lambda h: z[:, h, tok])

                def spread(b):
                    if b >= 2:
                        pe.wait_ge(state_done, 32 * L + 4 * (b - 1))
                    for h in range(HEADS):
                        mm = pe.matmul(bank[b % 2][:, 128 * h:128 * (h + 1)], v[:, h, SEQ + b:SEQ + b + 1].broadcast_to([128, 128]), ident,
                                       start=True, stop=True)
                    mm.then_inc(v_spread, 1)

                PE_LEVELS = {(3, 1): -1, (3, 3): 0, (4, 0): 1, (4, 1): 2, (4, 2): 3, (4, 3): 4}

                def between(it, s):
                    if (it, s) in PE_LEVELS:
                        score_level(PE_LEVELS[(it, s)])
                weight_pass(f"in{L}", act_hi, act_lo, part=(0, 3))
                weight_pass(f"in{L}", act_hi, act_lo, part=(3, 5), between=between)
                pe.wait_ge(bank_read, IN0[L] + 20)
                for i in range(2):
                    for h in range(HEADS):
                        mm = pe.transpose(bank[i][:, 128 * h:128 * (h + 1)], v[:, h, SEG * i:SEG * (i + 1)], ident)
                    mm.then_inc(v_turned, 1)
                pe.wait_ge(past_in, 16 * (L + 1))
                rows = DEC * POOL_BUF
                for g in range(4):
                    mm = pe.matmul(bank[2][:, DEC * g:DEC * (g + 1)], pool_past[:, 128 * g:128 * (g + 1)], pick[0:rows, g, :], start=True, stop=True)
                mm.then_inc(past_summed, 1)
                score_level(5)
                pe.wait_ge(v_copied, 2 * (L + 1))
                for j in (5, 6, 7):
                    if j > 5:
                        score_level(j)
                    for b in SPREAD[j]:
                        spread(b)
                pe.wait_ge(scores_taken, 17 * (L + 1))
                for h in range(HEADS):
                    hs = slice(128 * h, 128 * (h + 1))
                    mm = pe.matmul(bank[6][:, hs], values[:, 0, hs], scores[:, 0, h, :], start=True, stop=True)
                mm.then_inc(attended, 1)
                for h in range(HEADS):
                    hs = slice(128 * h, 128 * (h + 1))
                    pe.matmul(bank[7][:, hs], values[:, 0, hs], scores_x[:, h, :], start=True, stop=False)
                    mm = pe.matmul(bank[7][:, hs], values[:, 1, hs], scores[:, 1, h, :], start=False, stop=True)
                mm.then_inc(attended, 1)
                pe.wait_ge(state_done, 32 * (L + 1))
                for b in range(DEC):
                    for h in range(HEADS):
                        mm = pe.matmul(bank[0][:, DEC * h + b:DEC * h + b + 1], state[:, b, h, :], q[:, h, SEQ + b:SEQ + b + 1], start=True, stop=True)
                mm.then_inc(attended, 1)
                pe.wait_ge(hgo_copied, 3 * (L + 1))
                sq = hgo_sq[:, :, :].rearrange("p h t -> p (h t)")
                pe.wait_ge(pool_w_in, 16 * (L + 1))
                for g in range(4):
                    w = (win_a, win_b)[g % 2]
                    pe.wait_ge(pooled, 4 * L + g + 1)
                    if g >= 2:
                        pe.wait_ge(pool_lo, 4 * L + g - 1)
                    pe.matmul(bank[2 + g % 2][:, 0:T], pool_w[:, g, :], w[:, g, PAD:], start=True, stop=True).then_inc(pool_mapped, 1)
                for i in range(3):
                    pe.matmul(bank[(5, 0, 1)[i]][:, 0:352], ones, sq[:, 352 * i:352 * (i + 1)], start=True, stop=True).then_inc(hgo_summed, 1)
                pe.wait_ge(kdec_done, 2 * (L + 1))
                for i in range(2):
                    for h in range(HEADS):
                        mm = pe.transpose(bank[6 + i][:, 128 * h:128 * (h + 1)], kdec[:, h, SEG * i:SEG * (i + 1)], ident)
                    mm.then_inc(kdec_turned, 1)
                pe.wait_ge(kdec_copied, 2 * (L + 1))
                for h in range(HEADS):
                    hs = slice(128 * h, 128 * (h + 1))
                    pe.matmul(bank[4][:, hs], kdecT[:, 0, hs], values[:, 0, hs], start=True, stop=False)
                    mm = pe.matmul(bank[4][:, hs], kdecT[:, 1, hs], values[:, 1, hs], start=False, stop=True)
                mm.then_inc(final_state, 1)
                pe.wait_ge(pool_lo, 4 * (L + 1))
                for g in range(4):
                    mm = pe.transpose(bank[3][0:POOL_BUF + DEC, 128 * g:128 * (g + 1)], up[:, g, PAD + SEQ - POOL_BUF:], ident)
                mm.then_inc(tail_turned, 1)
                pe.wait_ge(tail_copied, L + 1)
                pe.wait_ge(mix_lo_done, 4 * (L + 1))
                weight_pass(f"out{L}", mix_hi, mix_lo)
                if layer == 0:
                    sum_squares(1)
                    pe.wait_ge(norm_lo, KT * 2)
                    weight_pass("ffn_up0", act_hi, act_lo)
                    pe.wait_ge(ffn_lo_done, FT)
                    weight_pass("ffn_down0", ffn_hi, ffn_lo)
            pe.wait_ge(squared, KT * 4)
            for i, (t0, rows) in enumerate(TOKEN_TILES):
                for kt in range(KT):
                    mm = pe.matmul(bank[4][0:rows, i:i + 1], square_m[:, kt, t0:t0 + rows], ones[:, 0:1], start=(kt == 0), stop=(kt == KT - 1))
            mm.then_inc(summed, 1)
            pe.wait_ge(scaled_done, KT)
            pe.wait_ge(router_in, 16)
            for i, (t0, rows) in enumerate(TOKEN_TILES):
                for kt in range(KT):
                    mm = pe.matmul(bank[7][0:rows, 8 * i:8 * (i + 1)], scaled_m[:, kt, t0:t0 + rows], router[:, kt, :], start=(kt == 0), stop=(kt == KT - 1))
            mm.then_inc(routed, 1)
            for i, (t0, rows) in enumerate(TOKEN_TILES):
                for c in range(2):
                    if i:
                        pe.wait_ge(h_lo_done, 2 * (i - 1) + c + 1)
                    for k in range(4):
                        mm = pe.transpose(bank[2 + c][0:rows, 128 * k:128 * (k + 1)], scaled_m[:, 4 * c + k, t0:t0 + rows], ident)
                    mm.then_inc(h_turned, 1)
                if i == 0:
                    pe.wait_ge(route, 17)
                    for ii, (_, r) in enumerate(TOKEN_TILES):
                        for jj in range(ii):
                            pe.matmul(bank[5][:, 8 * ii:8 * (ii + 1)], ones, chosen[:, jj, :], start=(jj == 0), stop=False)
                        pe.matmul(bank[5][:, 8 * ii:8 * (ii + 1)], before[0:r, :], chosen[0:r, ii, :], start=(ii == 0), stop=True)
                    for ii, (_, r) in enumerate(TOKEN_TILES):
                        mm = pe.matmul(bank[5][:, 24:32], ones[0:r, :], chosen[0:r, ii, :], start=(ii == 0), stop=(ii == 2))
                    mm.then_inc(placed, 1)
            pe.wait_ge(hot, 3 * N_EXPERTS)
            for e in range(N_EXPERTS):
                if e >= 2:
                    pe.wait_ge(hot_copied, e - 1)
                for i, (t0, rows) in enumerate(TOKEN_TILES):
                    mm = pe.transpose(bank[e % 2][:, t0:t0 + rows], token_hot[0:rows, i, e, :].bitcast(f32), ident[0:rows, 0:rows])
                mm.then_inc(hot_turned, 1)
            for e in range(N_EXPERTS):
                for i, (_, rows) in enumerate(TOKEN_TILES):
                    mm = pe.matmul(bank[6][:, e:e + 1], token_hot[0:rows, i, e, :].bitcast(f32), gates[0:rows, i, e:e + 1], start=(i == 0), stop=(i == 2))
            mm.then_inc(gate_slots, 1)
            pe.wait_ge(hot_copied, N_EXPERTS)
            pe.wait_ge(h_lo_done, 6)
            for n in range(16):
                q, d = n // 4, n % 4
                if n >= 4:
                    pe.wait_ge(packed_lo, n - 3)
                for dd in range(2):
                    kt = 2 * d + dd
                    for m in range(6):
                        i, part = m // 2, (h_hi, h_lo)[m % 2]
                        rows = TOKEN_TILES[i][1]
                        mm = pe.matmul(bank[n % 4][:, 256 * dd:256 * (dd + 1)], part[0:rows, i, 128 * kt:128 * (kt + 1)],
                                       token_hot[0:rows, i, 2 * q:2 * q + 2, :].rearrange("p e s -> p (e s)"), start=(m == 0), stop=(m == 5))
                mm.then_inc(gathered, 1)

            def unit_e(kind, k, j, turn=None):
                u = j if turn is None else HEAD_UNITS + TURN_UNITS * turn + j
                jj = j if turn is None else HEAD_UNITS + j
                pe.wait_ge(moe_lo, u + 1)
                hi, lo = (t[jj % SPLIT_RING][:, :, :].rearrange("p a b -> p (a b)") for t in (w_hi, w_lo))
                if kind == "down":
                    s_hi, s_lo, last, first_bank, pieces = hid_hi[:, k, :], hid_lo[:, k, :], FE - 1, 6, ((0, 512), (512, 512))
                else:
                    s_hi, s_lo, last, first_bank, pieces = x_hi[:, k, :], x_lo[:, k, :], KT - 1, 0 if kind == "gate" else 3, PIECES
                for n, (s, w) in enumerate(((s_hi, hi), (s_hi, lo), (s_lo, hi))):
                    for p, (c0, width) in enumerate(pieces):
                        mm = pe.matmul(bank[first_bank + p][:, 0:width], s, w[:, c0:c0 + width], start=(k == 0 and n == 0),
                                       stop=(k == last and n == 2))
                mm.then_inc(moe_used, 1)

            def turn_hidden(e):
                for p, (c0, width) in enumerate(PIECES):
                    pe.wait_ge(act_done, 3 * e + 3)
                    for k in range(width // 128):
                        mm = pe.transpose(bank[3 + p][:, 128 * k:128 * (k + 1)], act_e[:, c0 + 128 * k:c0 + 128 * (k + 1)], ident)
                    mm.then_inc(hid_turned, 1)

            pe.wait_ge(packed_lo, 16)
            pe.wait_ge(y_lo_done, 1)
            pe.wait_ge(x_hi_set, 2)
            pe.wait_ge(x_lo_set, 2)
            for j in range(HEAD_UNITS):
                unit_e(("gate", "up")[j // KT], j % KT, j)

            def turn_e(e):
                for j, (kind, _, k) in enumerate(TURN):
                    if kind == "gate" and k == 0:
                        pe.wait_ge(gate_silu, 3 * e + 3)
                        for ready in (x_hi_set, x_lo_set):
                            pe.wait_ge(ready, 2 * e + 3)
                    if kind == "gate" and k == KT // 2:
                        turn_hidden(e)
                        for ready in (x_hi_set, x_lo_set):
                            pe.wait_ge(ready, 2 * e + 4)
                    if kind == "down" and k == 0:
                        pe.wait_ge(hid_lo_done, 3 * e + 3)
                        pe.wait_ge(y_lo_done, 2 * e + 1)
                    unit_e(kind, k, j, turn=e)
            with pe.Fori(0, N_EXPERTS - 1) as e:
                turn_e(e)
            e = N_EXPERTS - 1
            turn_hidden(e)
            pe.wait_ge(hid_lo_done, 3 * e + 3)
            pe.wait_ge(y_lo_done, 2 * e + 1)
            for j in range(FE):
                unit_e("down", j, j, turn=e)
            last = N_EXPERTS - 1

            def scatter(e, kt):
                for half in range(2):
                    mm = pe.matmul(bank[kt][:, 0:T], packed[:, e, half, 128 * kt:128 * (kt + 1)], slot_hot[:, e, :],
                                   start=(e == 0 and half == 0), stop=(e == last and half == 1))
                return mm
            for e in range(last):
                for kt in range(6):
                    scatter(e, kt)
            pe.wait_ge(y_lo_done, 2 * N_EXPERTS + 1)
            for e in range(last):
                for kt in (6, 7):
                    scatter(e, kt)
            for kt in range(KT):
                scatter(last, kt).then_inc(scattered, 1)
            n_rows = pe.value_load(longest_i[0:1, 0:1])
            with pe.If(n_rows > CAP):
                pe.wait_ge(moe_added, KT)
                for i, (t0, rows) in enumerate(TOKEN_TILES):
                    mm = pe.matmul(bank[2][:, t0:t0 + rows], rstd[0:rows, i:i + 1].broadcast_to([rows, 128]), ident[0:rows, 0:rows], start=True, stop=True)
                mm.then_inc(all_spread, 1)
                pe.wait_ge(all_added, KT)
                with pe.Fori(0, N_EXPERTS) as e:
                    pe.wait_ge(all_col, e + 1)
                    for i, (t0, rows) in enumerate(TOKEN_TILES):
                        mm = pe.matmul(bank[2][:, t0:t0 + rows], over_col[0:rows, i:i + 1].broadcast_to([rows, 128]), ident[0:rows, 0:rows], start=True, stop=True)
                    mm.then_inc(all_spread, 1)
                    with pe.Fori(0, FE) as f:
                        n = e * FE + f
                        pe.wait_ge(all_w, 48 * (n + 1))
                        pe.wait_ge(all_added, n * KT + KT)
                        for b, w in enumerate((gate_w_all, up_w_all)):
                            for kt in range(KT):
                                mm = pe.matmul(bank[b][:, 0:T], w[:, kt, :], h_all[:, kt, :], start=(kt == 0), stop=(kt == KT - 1))
                            mm.then_inc(all_up, 1)
                        pe.wait_ge(all_act, 2 * n + 2)
                        for kt in range(KT):
                            pe.wait_ge(all_added, n * KT + KT + max(kt - 3, 0))
                            pe.matmul(bank[4 + kt % 4][:, 0:T], down_w_all[:, 128 * kt:128 * (kt + 1)], act_all[:, :], start=True, stop=True).then_inc(all_down, 1)
            pe.end_ifs()
            pe.wait_ge(squared, KT * 5)
            for i, (t0, rows) in enumerate(TOKEN_TILES):
                for kt in range(KT):
                    mm = pe.matmul(bank[4][0:rows, i:i + 1], square_f[:, kt, t0:t0 + rows], ones[:, 0:1], start=(kt == 0), stop=(kt == KT - 1))
            mm.then_inc(summed, 1)
            pe.wait_ge(scaled_done, 2 * KT)
            for i, (t0, rows) in enumerate(TOKEN_TILES):
                for c in range(2):
                    n = 2 * i + c
                    if n >= 2:
                        pe.wait_ge(y_copied, n - 1)
                    for k in range(4):
                        mm = pe.transpose(bank[5 + n % 2][0:rows, 128 * k:128 * (k + 1)], scaled_f[:, 4 * c + k, t0:t0 + rows], ident)
                    mm.then_inc(turned, 1)


def constants():
    import numpy as np
    c = np.zeros((128, C_COLS), np.float32)
    i = np.arange(128)
    c[:, C_IDENT:C_IDENT + 128] = np.eye(128)
    c[:, C_ONES:C_ONES + 128] = 1.0
    c[:, C_BEFORE:C_BEFORE + 128] = i[:, None] < i[None, :]
    c[:, C_IOTA:C_IOTA + 128] = i[None, :]
    c[:, C_MASK:C_MASK + 128] = np.eye(128)
    for n, half in enumerate(LEVELS):
        s, t = i[:, None], i[None, :]
        pair = (s // (2 * half) == t // (2 * half)) & (s % (2 * half) < half) & (t % (2 * half) >= half)
        c[:, C_MASK + 128 * (n + 1):C_MASK + 128 * (n + 2)] = pair
    for g, w in enumerate(WINDOWS):
        t = np.arange(PAD)
        c[:, C_CORR + g * PAD:C_CORR + (g + 1) * PAD] = w / np.minimum(t + 1, w).astype(np.float32)
        for b in range(DEC):
            c[POOL_BUF * b + POOL_BUF + 1 - w:POOL_BUF * (b + 1), C_PICK + g * DEC + b] = 1.0
    e = np.arange(N_EXPERTS)
    c[:, C_LOWER:C_LOWER + 64] = (e[None, :] < e[:, None]).reshape(-1)
    return c


_INS = ["x_prompt", "x_sample", "state_hgrn", "state_pool", "lb_logits", "norm_mix", "w_in", "w_o", "hg_norm", "pool_w", "pool_scale",
        "norm_ffn", "ffn_w_gate", "ffn_w_up", "ffn_w_down", "router", "moe_w_gate", "moe_w_up", "moe_w_down", "norm_final"]
_OUTS = [("y_prompt", (1, SEQ, D_MODEL)), ("y_sample", (DEC, 1, D_MODEL)), ("new_hgrn_prompt", (DEPTH, 1, HEADS, 128, 128)),
         ("new_hgrn_sample", (DEPTH, DEC, HEADS, 128, 128)), ("new_pool_prompt", (DEPTH, 1, POOL_BUF, HG_WIDTH)),
         ("new_pool_sample", (DEPTH, DEC, POOL_BUF, HG_WIDTH))]


def kernel(**inputs):
    import numpy as np
    import concourse.bacc as bacc
    from concourse.bass_utils import run_bass_kernel_spmd

    nc = bacc.Bacc("TRN2", target_bir_lowering=False, num_devices=1)
    arrays = {n: np.ascontiguousarray(inputs[n]) for n in _INS}
    arrays["consts"] = constants()
    launched = {f"in_{n}_dram": x for n, x in arrays.items()}
    a = {n: nc.dram_tensor(f"in_{n}_dram", x.shape, mybir.dt.float32, kind="ExternalInput").ap() for n, x in arrays.items()}
    o = {n: nc.dram_tensor(f"out_{n}_dram", s, mybir.dt.float32, kind="ExternalOutput").ap() for n, s in _OUTS}
    build_program(nc, a, o)
    r = run_bass_kernel_spmd(nc, [launched], core_ids=[0])
    return tuple(r.results[0][f"out_{n}_dram"] for n, _ in _OUTS)
```

```python
import concourse.bass as bass
from concourse import mybir
from contextlib import ExitStack

D_MODEL = 1024
SEQ = 256
DEC = 8
DEPTH = 2
T = SEQ + DEC
KT = D_MODEL // 128
HEADS = 4
HG_WIDTH = HEADS * 128
IN_WIDTH = 5 * HG_WIDTH
POOL_BUF = 15
WINDOWS = (2, 4, 8, 16)
D_FF = 2816
FT = D_FF // 128
N_EXPERTS = 8
D_FF_E = 1408
FE = D_FF_E // 128
EPS = 1e-6
CAP = 128
SEG = 128
TOKEN_TILES = ((0, 128), (128, 128), (256, DEC))
LEVELS = (1, 2, 4, 8, 16, 32, 64)
PAD = 16

C_IDENT, C_ONES, C_BEFORE, C_IOTA = 0, 128, 256, 384
C_MASK = 512
C_CORR = C_MASK + 128 * (1 + len(LEVELS))
C_PICK = C_CORR + 4 * PAD
C_LOWER = C_PICK + 4 * DEC
C_COLS = C_LOWER + N_EXPERTS * N_EXPERTS

V_MIX, V_FFN, V_FINAL, V_LB, V_HG, V_POOL = 0, 16, 32, 40, 48, 56
V_COLS = 64

RING = 4
PASSES = []
_n = 0
for _name, _units, _kts in (("in0", 20, KT), ("out0", 8, KT), ("ffn_up0", 2 * FT, KT), ("ffn_down0", 16, FT // 2),
                            ("in1", 20, KT), ("out1", 8, KT)):
    PASSES.append((_name, _n, _units, _kts))
    _n += _units
PASS = {p[0]: p for p in PASSES}
GROUPS = (0, 1, 3, 2, 4)
IN0 = [PASS["in0"][1], PASS["in1"][1]]
WO0 = [PASS["out0"][1], PASS["out1"][1]]
GU0 = PASS["ffn_up0"][1]
DN0 = PASS["ffn_down0"][1]
LAST_UNIT = _n

RAW_RING = 9
SPLIT_RING = 3
HEAD_UNITS = 2 * KT
TURN_UNITS = 2 * KT + FE
LOAD_AHEAD = 2


def build_program(nc, a, o):
    f32 = mybir.dt.float32
    f32r = mybir.dt.float32r
    i32 = mybir.dt.int32
    ALU = mybir.AluOpType
    ACT = mybir.ActivationFunctionType
    AX = mybir.AxisListType
    ds = bass.ds

    ctx = ExitStack()
    with ctx:
        def sb(name, shape, dt=f32):
            return ctx.enter_context(nc.sbuf_tensor("sb_" + name, shape, dt))

        def sem(name):
            return ctx.enter_context(nc.semaphore(name))

        consts = sb("consts", [128, C_COLS])
        ident = consts[:, C_IDENT:C_IDENT + 128]
        ones = consts[:, C_ONES:C_ONES + 128]
        before = consts[:, C_BEFORE:C_BEFORE + 128]
        iota = consts[:, C_IOTA:C_IOTA + 128]
        corr = consts[:, C_CORR:C_CORR + 4 * PAD].rearrange("p (g t) -> p g t", g=4)
        pick = consts[:, C_PICK:C_PICK + 4 * DEC].rearrange("p (g b) -> p g b", g=4)
        xT = sb("xT", [128, KT, T])
        vecs = sb("vecs", [128, V_COLS])
        vec_rows = sb("vec_rows", [V_COLS, 128])
        lbound = sb("lbound", [128, DEPTH, HEADS])
        lspan = sb("lspan", [128, DEPTH, HEADS])
        lb_tmp = sb("lb_tmp", [128, 4, HEADS])
        eps = sb("eps", [128, 1])
        root = sb("root", [128, T])
        rstd = sb("rstd", [128, T])
        pool_w = sb("pool_w", [128, 4, 128])
        sample_kq = sb("sample_kq", [128, HEADS, DEC])
        sample_o = sb("sample_o", [128, HEADS, DEC])
        raw = [sb(f"raw{i}", [128, FE, 128]) for i in range(RING)]
        w_hi = [sb(f"w_hi{i}", [128, FE, 128], f32r) for i in range(RING)]
        w_lo = [sb(f"w_lo{i}", [128, FE, 128], f32r) for i in range(RING)]
        router = sb("router", [128, KT, N_EXPERTS])
        logits = sb("logits", [128, 3, N_EXPERTS])
        rank = sb("rank", [128, 3, N_EXPERTS])
        first = sb("first", [128, 3, N_EXPERTS])
        second = sb("second", [128, 3, N_EXPERTS])
        chosen = sb("chosen", [128, 3, N_EXPERTS])
        picked = sb("picked", [128, 3, N_EXPERTS])
        picked_2 = sb("picked_2", [128, 3, N_EXPERTS])
        logit_rows = sb("logit_rows", [N_EXPERTS, T])
        rstd_tok = sb("rstd_tok", [128, 3])
        tops = sb("tops", [128, 4, 3])
        gates = sb("gates", [128, 3, N_EXPERTS])
        slot = sb("slot", [128, 3, N_EXPERTS])
        over = sb("over", [128, 3, N_EXPERTS])
        slot_gate = sb("slot_gate", [128, N_EXPERTS])
        longest = sb("longest", [128, 1])
        longest_i = sb("longest_i", [128, 1], i32)
        arena_base = (nc.sbuf_base + 31) // 32 * 32
        arena_end = nc.sbuf_usable_end

        def at(name, shape, offset, dt=f32):
            size = 4
            for n in shape[1:]:
                size *= n
            assert arena_base + offset + size <= arena_end, (name, arena_base + offset + size - arena_end)
            return nc.alloc_sbuf_tensor_at("at_" + name, shape, dt, offset=arena_base + offset)

        act_hi = at("act_hi", [128, KT, T], 0, f32r)
        act_lo = at("act_lo", [128, KT, T], 8448, f32r)
        values = at("values", [128, 2, HG_WIDTH], 0)
        kdecT = at("kdecT", [128, 2, HG_WIDTH], 4096)
        hg_rstd = at("hg_rstd", [128, HEADS, T], 8192)
        hgo_sq = at("hgo_sq", [128, HEADS, T], 12416)
        state = at("state", [128, DEC, HEADS, 128], 16896)
        proj = at("proj", [128, 4, HEADS, T], 33280)
        mix_hi = at("mix_hi", [128, KT, T], 50176, f32r)
        mix_lo = at("mix_lo", [128, KT, T], 58624, f32r)
        up = at("up", [128, 4, PAD + T], 67072)
        win_a = at("win_a", [128, 4, PAD + T], 71552)
        win_b = at("win_b", [128, 4, PAD + T], 76032)
        sig = at("sig", [128, HEADS, T], 80512)
        keys = at("keys", [128, HEADS, T], 84736)
        logf = at("logf", [128, HEADS, SEQ], 88960)
        kdec = at("kdec", [128, HEADS, SEQ], 88960)
        decay = at("decay", [128, HEADS, SEQ], 93056)
        diff = [at(f"diff{i}", [128, HEADS, SEQ], 97152 + 4096 * i) for i in range(2)]
        sided = [at(f"sided{i}", [128, HEADS, SEQ], 105344 + 4096 * i) for i in range(2)]
        outer = at("outer", [128, 2, HEADS, 128], 109440)
        scores = at("scores", [128, 2, HEADS, SEG], 113536)
        scores_x = at("scores_x", [128, HEADS, SEG], 117632)
        pool_past = at("pool_past", [DEC * POOL_BUF, HG_WIDTH], 119680)
        segments = at("segments", [128, HEADS, SEQ], 109440)
        hg_tmp = at("hg_tmp", [128, HEADS, T], 80512)
        new_state = at("new_state", [128, HEADS, 128], 117632)
        pool_tail = at("pool_tail", [POOL_BUF + DEC, HG_WIDTH], 119680)
        square_w = at("square_w", [128, KT, T], 71552)
        square = at("square", [128, KT, T], 84736)
        x_rows = at("x_rows", [128, 3, D_MODEL], 97152)
        ffn_hi = at("ffn_hi", [128, FT, T], 33280, f32r)
        ffn_lo = at("ffn_lo", [128, FT, T], 56512, f32r)
        gate_in = [at(f"gate_in{i}", [128, T], 93440 + 1056 * i) for i in range(2)]
        gate_act = [at(f"gate_act{i}", [128, T], 95552 + 1056 * i) for i in range(2)]
        up_in = [at(f"up_in{i}", [128, T], 97664 + 1056 * i) for i in range(2)]
        packed = at("packed", [128, N_EXPERTS, 2, KT * CAP], 0, f32r)
        slot_hot = at("slot_hot", [128, N_EXPERTS, T], 65536, f32r)
        act_e = at("act_e", [128, D_FF_E], 73984)
        hid_hi = at("hid_hi", [128, FE, CAP], 79616, f32r)
        hid_lo = at("hid_lo", [128, FE, CAP], 85248, f32r)
        raw_e = raw + [at(f"raw_e{i}", [128, FE, 128], 90880 + 5632 * i) for i in range(RAW_RING - RING)]
        x_hi, x_lo = w_hi[3][:, 0:KT, :], w_lo[3][:, 0:KT, :]
        square_m = at("square_m", [128, KT, T], 33280)
        h_hi = at("h_hi", [128, 3, D_MODEL], 79616, f32r)
        scaled_m = at("scaled_m", [128, KT, T], 95744)
        h_lo = at("h_lo", [128, 3, D_MODEL], 104192, f32r)
        token_hot = at("token_hot", [128, 3, N_EXPERTS, CAP], 91904, f32r)
        greater = at("greater", [128, 3, N_EXPERTS, N_EXPERTS], 41728)
        equal = at("equal", [128, 3, N_EXPERTS, N_EXPERTS], 42496)
        h_all = at("h_all", [128, KT, T], 0)
        gate_w_all = at("gate_w_all", [128, KT, 128], 8448)
        up_w_all = at("up_w_all", [128, KT, 128], 12544)
        down_w_all = at("down_w_all", [128, D_MODEL], 16640)
        act_all = at("act_all", [128, T], 20736)
        over_all = at("over_all", [128, T], 21792)
        over_col = at("over_col", [128, 3], 22848)
        square_f = at("square_f", [128, KT, T], 90880)
        scaled_f = at("scaled_f", [128, KT, T], 99328)
        y_rows = at("y_rows", [128, 3, D_MODEL], 107776)

        h_saved = nc.dram_tensor("h_saved", (128, KT * T), f32).ap()
        bank = [ctx.enter_context(nc.psum_tensor(f"bank{i}", [128, 512], f32)) for i in range(8)]

        consts_in = sem("consts_in"); tables_in = sem("tables_in"); vecs_in = sem("vecs_in"); x_in = sem("x_in")
        state_in = sem("state_in"); past_in = sem("past_in"); pool_w_in = sem("pool_w_in")
        raw_full = [sem(f"raw_full{i}") for i in range(RING)]
        hi_done = sem("hi_done"); lo_done = sem("lo_done"); unit_used = sem("unit_used"); bank_read = sem("bank_read")
        vecs_turned = sem("vecs_turned"); vecs_ready = sem("vecs_ready"); lb_step = sem("lb_step"); lb_exp = sem("lb_exp")
        eps_set = sem("eps_set")
        x_turned = sem("x_turned"); x_loaded = sem("x_loaded")
        squared = sem("squared"); norm_hi = sem("norm_hi"); norm_lo = sem("norm_lo"); summed = sem("summed")
        rooted = sem("rooted"); rstd_done = sem("rstd_done")
        sig_done = sem("sig_done"); q_gated = sem("q_gated"); forget_done = sem("forget_done"); keys_done = sem("keys_done")
        g_gated = sem("g_gated"); logf_done = sem("logf_done"); decay_done = sem("decay_done"); segments_set = sem("segments_set")
        scores_zeroed = sem("scores_zeroed"); diff_done = sem("diff_done"); diff_exp = sem("diff_exp"); sided_done = sem("sided_done")
        scored = sem("scored"); scores_taken = sem("scores_taken"); scores_put = sem("scores_put")
        kq_done = sem("kq_done"); sampled = sem("sampled"); outer_done = sem("outer_done"); sample_done = sem("sample_done")
        v_turned = sem("v_turned"); v_copied = sem("v_copied")
        state_decayed = sem("state_decayed"); v_spread = sem("v_spread"); state_done = sem("state_done"); state_out = sem("state_out")
        attended = sem("attended")
        end_exp = sem("end_exp"); end_diff = sem("end_diff"); kdec_done = sem("kdec_done"); kdec_turned = sem("kdec_turned"); kdec_copied = sem("kdec_copied")
        final_state = sem("final_state"); final_copied = sem("final_copied"); final_out = sem("final_out")
        hgo_squared = sem("hgo_squared"); hgo_summed = sem("hgo_summed"); hgo_rooted = sem("hgo_rooted"); hgo_rstd = sem("hgo_rstd")
        hgo_scaled = sem("hgo_scaled"); mix_hi_done = sem("mix_hi_done"); mix_lo_done = sem("mix_lo_done")
        pads_zeroed = sem("pads_zeroed"); windowed = sem("windowed"); past_summed = sem("past_summed"); past_added = sem("past_added")
        pooled = sem("pooled"); pool_mapped = sem("pool_mapped"); pool_hi = sem("pool_hi"); pool_lo = sem("pool_lo")
        tail_turned = sem("tail_turned"); tail_copied = sem("tail_copied"); tail_out = sem("tail_out"); shift_out = sem("shift_out")
        gate_done = sem("gate_done"); ffn_mult = sem("ffn_mult")
        ffn_hi_done = sem("ffn_hi_done"); ffn_lo_done = sem("ffn_lo_done")
        moe_added = sem("moe_added"); scaled_done = sem("scaled_done"); turned = sem("turned"); 
        y_left = sem("y_left"); y_right = sem("y_right"); rms_done = sem("rms_done"); rms_inverted = sem("rms_inverted"); y_out = sem("y_out")

        router_in = sem("router_in"); logits_zeroed = sem("logits_zeroed"); routed = sem("routed"); route = sem("route"); route_exp = sem("route_exp")
        placed = sem("placed"); hot = sem("hot"); hot_turned = sem("hot_turned"); hot_copied = sem("hot_copied")
        logits_scaled = sem("logits_scaled"); tokens_turned = sem("tokens_turned"); rstd_turned = sem("rstd_turned")
        head_full = [sem(f"head_full{i}") for i in range(RING)]
        h_turned = sem("h_turned"); h_hi_done = sem("h_hi_done"); h_lo_done = sem("h_lo_done"); h_out = sem("h_out")
        gathered = sem("gathered"); packed_hi = sem("packed_hi"); packed_lo = sem("packed_lo"); gate_slots = sem("gate_slots")
        moe_full = [sem(f"moe_full{i}") for i in range(RAW_RING)]
        moe_hi = sem("moe_hi"); moe_lo = sem("moe_lo"); moe_used = sem("moe_used")
        x_hi_set = sem("x_hi_set"); x_lo_set = sem("x_lo_set"); gate_silu = sem("gate_silu"); act_done = sem("act_done")
        hid_turned = sem("hid_turned"); hid_hi_done = sem("hid_hi_done"); hid_lo_done = sem("hid_lo_done")
        y_hi_done = sem("y_hi_done"); y_lo_done = sem("y_lo_done"); scattered = sem("scattered")
        all_in = sem("all_in"); all_w = sem("all_w"); all_spread = sem("all_spread"); all_col = sem("all_col")
        all_over = sem("all_over"); all_up = sem("all_up"); all_silu = sem("all_silu"); all_act = sem("all_act"); all_down = sem("all_down"); all_added = sem("all_added")

        def unit_source(name, it, s):
            layer = int(name[-1])
            if name[:2] == "in":
                w, col = a["w_in"][layer], ds(GROUPS[it] * 512 + s * 128, 128)
            elif name[:3] == "out":
                w, col = a["w_o"][layer], ds(it * 512 + s * 128, 128)
            elif name[:6] == "ffn_up":
                w, col = (a["ffn_w_gate"], a["ffn_w_up"])[s % 2][0], ds(it * 256 + (s // 2) * 128, 128)
            else:
                half = s % 2
                w, col = a["ffn_w_down"][0, half * D_FF_E:(half + 1) * D_FF_E, :], ds(it * 256 + (s // 2) * 128, 128)
            return w[:, col].rearrange("(k p) n -> p k n", p=128)

        def wait_x(eng, version, kt):
            if version == 0:
                eng.wait_ge(x_loaded, kt + 1)
            elif version in (1, 3):
                eng.wait_ge(bank_read, WO0[(version - 1) // 2] + kt + 1)
            else:
                eng.wait_ge(bank_read, DN0 + 2 * kt + 2)

        TURN = [("gate", 1, k) for k in range(KT)] + [("down", 0, k) for k in range(FE)] + [("up", 1, k) for k in range(KT)]
        SIDE = slice(288, 288 + HEADS * DEC)
        HG_SUMS = ((5, slice(0, HEADS * SEG), slice(0, SEG)), (6, slice(0, HEADS * DEC), slice(SEQ, T)), (4, slice(0, HEADS * SEG), slice(SEG, SEQ)))
        PIECES = ((0, 512), (512, 512), (1024, 384))
        CHOSEN, GAP, ROUTED = 9, 17, 26

        SQUARED = [0] + [KT + n * (2 * KT - 1) for n in range(4)]
        NORM_SUMS = ((3, 0), (4, 0), (4, 1))

        def gather_bank(n):
            return n if n < 4 else 6 + n % 2

        def raw_slot(j, turn):
            return j % RING if turn is None else (j + RING) % RAW_RING

        def wait_raw(eng, j, turn):
            if turn is None:
                eng.wait_ge(head_full[j % RING], 16 * (j // RING + 1))
            else:
                eng.wait_ge(moe_full[raw_slot(j, turn)], 16 * (TURN_UNITS // RAW_RING * turn + j // RAW_RING + 1))

        block = ctx.enter_context(nc.Block())

        @block.sync
        def _(sp):
            sp.dma_start(consts[:, 0:C_BEFORE], a["consts"][:, 0:C_BEFORE]).then_inc(consts_in, 16)
            for row, name, src in ((V_MIX, "norm_mix", "l (k p) -> (l k) p"), (V_FFN, "norm_ffn", "l (k p) -> (l k) p"),
                                   (V_FINAL, "norm_final", "(k p) -> k p"), (V_LB, "lb_logits", "l (k p) -> (l k) p"),
                                   (V_HG, "hg_norm", "l (k p) -> (l k) p"), (V_POOL, "pool_scale", "l (k p) -> (l k) p")):
                view = a[name].rearrange(src, p=128)
                sp.dma_start(vec_rows[row:row + view.shape[0], :], view).then_inc(vecs_in, 16)
            for name, n0, units, kts in PASSES:
                def load(it, s, check=True):
                    if check:
                        sp.wait_ge(lo_done, n0 + 4 * it + s - 3)
                    sp.dma_start(raw[s][:, 0:kts, :], unit_source(name, it, s)).then_inc(raw_full[s], 16)
                first = 0
                if n0 == 0:
                    for s in range(RING):
                        load(0, s, check=False)
                    first = 1
                if name[:2] == "in":
                    for it in range(first, units // RING):
                        for s in range(RING):
                            load(it, s)
                else:
                    with sp.Fori(first, units // RING) as it:
                        for s in range(RING):
                            load(it, s)
                if name == "ffn_up0":
                    sp.wait_ge(state_out, 16)
                    for i in range(4):
                        sp.dma_start(state[:, 2 * i:2 * i + 2, :, :].rearrange("k b h v -> k (b h) v"),
                                     a["state_hgrn"][1, 2 * i:2 * i + 2].rearrange("b h k v -> k (b h) v")).then_inc(state_in, 16)
                    sp.wait_ge(pool_mapped, 4)
                    sp.wait_ge(tail_out, 32)
                    sp.dma_start(pool_w[:, :, :], a["pool_w"][1].rearrange("g c d -> c g d")).then_inc(pool_w_in, 16)
                    sp.dma_start(pool_past[:, :], a["state_pool"][1].rearrange("b r c -> (b r) c")).then_inc(past_in, 16)
            def load_e(j, e, kind, k, turn=None):
                u = j if turn is None else HEAD_UNITS + TURN_UNITS * turn + j
                slot_n = raw_slot(j, turn)
                if turn is None and j < RING:
                    sp.wait_ge(lo_done, LAST_UNIT - RING + j + 1)
                elif turn is None:
                    sp.wait_ge(moe_lo, u - RING + 1)
                elif isinstance(turn, int) and turn == 0 and j < RAW_RING - RING:
                    sp.wait_ge(packed_lo, 16)
                    sp.wait_ge(tail_out, 64)
                    sp.wait_ge(final_out, 32)
                else:
                    sp.wait_ge(moe_lo, u - RAW_RING + 1)
                w = a["moe_w_" + kind][0]
                src = w[ds(e, 1), 128 * k:128 * (k + 1), :].rearrange("a p n -> p (a n)")
                dst = raw_e[slot_n][:, :, :].rearrange("p a b -> p (a b)")[:, 0:src.shape[1]]
                sp.dma_start(dst, src).then_inc((head_full if turn is None else moe_full)[slot_n], 16)
            for j in range(HEAD_UNITS):
                load_e(j, 0, ("gate", "up")[j // KT], j % KT)
            for j, (kind, ahead, k) in enumerate(TURN):
                load_e(j, ahead, kind, k, turn=0)
            with sp.Fori(1, N_EXPERTS - 1) as e:
                for j, (kind, ahead, k) in enumerate(TURN):
                    load_e(j, e + ahead, kind, k, turn=e)
            for j in range(FE):
                load_e(j, N_EXPERTS - 1, "down", j, turn=N_EXPERTS - 1)
            sp.wait_ge(scattered, 8)
            sp.wait_ge(route, ROUTED)
            n_rows = sp.value_load(longest_i[0:1, 0:1])
            with sp.If(n_rows > CAP):
                sp.wait_ge(y_lo_done, 2 * N_EXPERTS + 1)
                sp.dma_start(h_all[:, :, :].rearrange("p k t -> p (k t)"), h_saved).then_inc(all_in, 16)
                with sp.Fori(0, N_EXPERTS) as e:
                    with sp.Fori(0, FE) as f:
                        n = e * FE + f
                        sp.wait_ge(all_added, n * KT + KT)
                        for dst, name in ((gate_w_all, "moe_w_gate"), (up_w_all, "moe_w_up")):
                            sp.dma_start(dst[:, :, :], a[name][0][ds(e, 1), :, ds(f * 128, 128)].rearrange("a (k p) n -> p (a k) n", p=128)).then_inc(all_w, 16)
                        sp.dma_start(down_w_all[:, :], a["moe_w_down"][0][ds(e, 1), ds(f * 128, 128), :].rearrange("a p n -> p (a n)")).then_inc(all_w, 16)
            sp.end_ifs()
            for i, (_, rows) in enumerate(TOKEN_TILES):
                sp.wait_ge(y_left, i + 1)
                sp.wait_ge(y_right, i + 1)
                dst = o["y_prompt"][0, 128 * i:128 * (i + 1), :] if i < 2 else o["y_sample"][:, 0, :]
                sp.dma_start(dst, y_rows[0:rows, i, :]).then_inc(y_out, 16)
            sp.wait_ge(y_out, 16 * 3)

        @block.gpsimd
        def _(gp):
            gp.dma_start(o["new_pool_sample"][:, :, 0:POOL_BUF - 1, :], a["state_pool"][:, :, 1:POOL_BUF, :]).then_inc(shift_out, 16)
            gp.memset(eps[:, :], EPS).then_inc(eps_set, 1)
            gp.memset(logits[:, :, :], 0.0).then_inc(logits_zeroed, 1)

            def square_tile(version, out, kt):
                if version and kt == 0:
                    gp.wait_ge(summed, version)
                wait_x(gp, version, kt)
                n = SQUARED[version] + 2 * kt
                dst = out[:, kt, :] if version == 0 or kt == 0 else out[:, 1 + kt % 2, :]
                gp.tensor_tensor(dst, xT[:, kt, :], xT[:, kt, :], ALU.mult).then_inc(squared, 1)
                if version and kt:
                    gp.wait_ge(squared, n)
                    gp.tensor_tensor(out[:, 0, :], out[:, 0, :], dst, ALU.add).then_inc(squared, 1)

            def square_x(version, out):
                for kt in range(KT):
                    square_tile(version, out, kt)

            for layer in range(DEPTH):
                L = layer
                if layer == 0:
                    square_x(0, square)
                gp.wait_ge(unit_used, IN0[L] + 1)
                gp.memset(up[:, :, 0:PAD], 0.0).then_inc(pads_zeroed, 1)
                gp.wait_ge(x_loaded, KT)
                gp.memset(scores[:, :, :, :], 0.0).then_inc(scores_zeroed, 1)
                gp.memset(segments[:, :, :], 1.0).then_inc(segments_set, 1)
                gp.wait_ge(segments_set, 2 * L + 1)
                gp.memset(segments[:, :, :].rearrange("p h (s t) -> p (h s) t", t=SEG)[:, :, 0:1], 0.0).then_inc(segments_set, 1)
                gp.wait_ge(forget_done, 4 * (L + 1))
                gp.tensor_scalar(keys[:, :, :], proj[:, 1, :, :], -1.0, 1.0, ALU.mult, ALU.add).then_inc(keys_done, 1)
                if L:
                    gp.wait_ge(final_out, 16 * L)
                    gp.wait_ge(tail_out, 32 * L)

                def decay_state(h):
                    gp.wait_ge(state_in, 64 * (L + 1))
                    fs = proj[:, 1, h, SEQ:T].unsqueeze(2).broadcast_to([128, DEC, 128])
                    gp.tensor_tensor(state[:, :, h, :], state[:, :, h, :], fs, ALU.mult).then_inc(state_decayed, 1)
                decay_state(0)
                gp.wait_ge(decay_done, L + 1)
                for j, half in enumerate(LEVELS + (SEG,)):
                    if 2 <= j < 5:
                        decay_state(j - 1)
                    if j >= 2:
                        gp.wait_ge(sided_done, 16 * L + 2 * (j - 1))
                    b = decay[:, :, :].rearrange("p h (n t) -> p (h n) t", t=2 * half)
                    d = diff[j % 2][:, :, :].rearrange("p h (n t) -> p (h n) t", t=2 * half)
                    width = 2 * half if half < SEG else half
                    n = HEADS * SEQ // (2 * half)
                    gp.tensor_tensor(d[:, :, 0:width], b[:, :, 0:width],
                                     b[:, :, half - 1:half].broadcast_to([128, n, width]), ALU.subtract).then_inc(diff_done, 1)
                gp.wait_ge(sided_done, 16 * L + 14)
                gp.tensor_tensor(diff[0][:, :, SEG:SEQ], decay[:, :, SEG:SEQ],
                                 decay[:, :, SEQ - 1:SEQ].broadcast_to([128, HEADS, SEG]), ALU.subtract).then_inc(end_diff, 1)
                gp.wait_ge(end_exp, 2 * (L + 1))
                gp.wait_ge(sided_done, 16 * (L + 1))
                gp.tensor_tensor(kdec[:, :, 0:SEG], sided[1][:, :, 0:SEG], diff[0][:, :, 0:1].broadcast_to([128, HEADS, SEG]), ALU.mult).then_inc(kdec_done, 1)
                gp.tensor_tensor(kdec[:, :, SEG:SEQ], keys[:, :, SEG:SEQ], diff[0][:, :, SEG:SEQ], ALU.mult).then_inc(kdec_done, 1)
                gp.wait_ge(sampled, 5 * (L + 1))
                version, out = ((1, square_w), (3, square_m))[L]
                for b in range(DEC):
                    if b:
                        square_tile(version, out, b - 1)
                    if b == DEC - 1:
                        square_tile(version, out, KT - 1)
                    gp.wait_ge(outer_done, 8 * L + b + 1)
                    gp.wait_ge(state_decayed, 4 * (L + 1))
                    gp.tensor_tensor(state[:, b, :, :], outer[:, b % 2, :, :], state[:, b, :, :], ALU.add).then_inc(state_done, 1)
                gp.wait_ge(state_done, 8 * (L + 1))
                gp.dma_start(o["new_hgrn_sample"][layer].rearrange("b h k v -> k (b h) v"),
                             state[:, :, :, :].rearrange("k b h v -> k (b h) v")).then_inc(state_out, 16)
                gp.wait_ge(tail_copied, L + 1)
                gp.dma_start(o["new_pool_prompt"][layer, 0], pool_tail[0:POOL_BUF, :]).then_inc(tail_out, 16)
                gp.dma_start(o["new_pool_sample"][layer, :, POOL_BUF - 1, :], pool_tail[POOL_BUF:, :]).then_inc(tail_out, 16)
                gp.wait_ge(final_copied, L + 1)
                gp.dma_start(o["new_hgrn_prompt"][layer, 0].rearrange("h k v -> k h v"), new_state[:, :, :]).then_inc(final_out, 16)
                if layer == 0:
                    with gp.Fori(0, FT // 2) as it:
                        for i in range(2):
                            gp.wait_ge(ffn_hi_done, 2 * it + i + 1)
                            at_ft = ds(2 * it + i, 1)
                            gp.tensor_tensor(ffn_lo[:, at_ft, :].rearrange("p a t -> p (a t)"), gate_act[i][:, :],
                                             ffn_hi[:, at_ft, :].rearrange("p a t -> p (a t)").bitcast(f32), ALU.subtract).then_inc(ffn_lo_done, 1)
                    square_x(2, square)
            def set_x_lo(e, c, u):
                gp.wait_ge(packed_lo, 4 if isinstance(e, int) and e < 2 else 16)
                gp.wait_ge(moe_used, u)
                gp.wait_ge(x_lo_set, 2)
                src = packed[:, ds(e, 1), 1, 512 * c:512 * (c + 1)].rearrange("p a n -> p (a n)")
                gp.tensor_copy(x_lo[:, 4 * c:4 * (c + 1), :].rearrange("p a b -> p (a b)"), src).then_inc(x_lo_set, 1)
            set_x_lo(1, 0, HEAD_UNITS - 4)
            with gp.Fori(0, N_EXPERTS - 2) as e:
                set_x_lo(e + 1, 1, HEAD_UNITS + TURN_UNITS * e)
                set_x_lo(e + 2, 0, HEAD_UNITS + TURN_UNITS * (e + 1) - 4)
            set_x_lo(N_EXPERTS - 1, 1, HEAD_UNITS + TURN_UNITS * (N_EXPERTS - 2))
            gp.wait_ge(shift_out, 16)

        @block.scalar
        def _(act):
            for i in range(2):
                act.dma_start(x_rows[:, i, :], a["x_prompt"][0, 128 * i:128 * (i + 1), :]).then_inc(x_in, 16)
            act.dma_start(x_rows[0:DEC, 2, :], a["x_sample"][:, 0, :]).then_inc(x_in, 16)
            act.wait_ge(x_in, 48)
            act.dma_start(consts[:, C_BEFORE:], a["consts"][:, C_BEFORE:]).then_inc(tables_in, 16)
            act.dma_start(pool_past[:, :], a["state_pool"][0].rearrange("b r c -> (b r) c")).then_inc(past_in, 16)
            act.dma_start(pool_w[:, :, :], a["pool_w"][0].rearrange("g c d -> c g d")).then_inc(pool_w_in, 16)
            for i in range(4):
                act.dma_start(state[:, 2 * i:2 * i + 2, :, :].rearrange("k b h v -> k (b h) v"),
                              a["state_hgrn"][0, 2 * i:2 * i + 2].rearrange("b h k v -> k (b h) v")).then_inc(state_in, 16)
            act.dma_start(router[:, :, :], a["router"][0].rearrange("(k p) e -> p k e", p=128)).then_inc(router_in, 16)
            act.wait_ge(lb_step, 3)
            act.activation(lb_tmp[:, 1:3, :], lb_tmp[:, 1:3, :], ACT.Exp).then_inc(lb_exp, 1)

            def split(s, k, n, kts, guard=True):
                act.wait_ge(raw_full[s], 16 * (k + 1))
                if guard:
                    act.wait_ge(unit_used, n - 3)
                act.activation(w_hi[s][:, 0:kts, :], raw[s][:, 0:kts, :], ACT.Copy).then_inc(hi_done, 1)

            def weight_pass(name, body, unroll=False, peel=False):
                i = [p[0] for p in PASSES].index(name)
                _, n0, units, kts = PASSES[i]
                its = units // RING

                def step(it, last):
                    for s in range(RING):
                        n = n0 + 4 * it + s
                        if s == 0 and name[:3] == "out" and it == 0:
                            pass
                        elif s == 0:
                            split(3, n0 // 4 + it, n + 3, kts, guard=not (n0 == 0 and isinstance(it, int) and it == 0))
                        elif not last:
                            split(s - 1, n0 // 4 + it + 1, n + 3, kts)
                        elif i + 1 < len(PASSES):
                            split(s - 1, PASSES[i + 1][1] // 4, PASSES[i + 1][1] + s - 1, PASSES[i + 1][3])
                        if body:
                            body(it, s)
                first = 0
                if n0 == 0:
                    for s in range(3):
                        split(s, 0, s, kts, guard=False)
                    inverse_root(0)
                if n0 == 0 or peel:
                    step(0, False)
                    first = 1
                if unroll:
                    for it in range(first, its - 1):
                        step(it, False)
                else:
                    with act.Fori(first, its - 1) as it:
                        step(it, False)
                step(its - 1, True)

            def scale_x(version, kt):
                col = (V_MIX, V_FFN, V_MIX + KT)[version]
                wait_x(act, version, kt)
                tile = lambda t: t[:, kt, :] if isinstance(kt, int) else t[:, ds(kt, 1), :].rearrange("p a t -> p (a t)")
                gain = vecs[:, col + kt:col + kt + 1] if isinstance(kt, int) else vecs[:, ds(col + kt, 1)]
                act.activation(tile(act_hi), tile(xT), ACT.Copy, scale=gain).then_inc(norm_hi, 1)

            def inverse_root(nth, b=4):
                act.wait_ge(summed, nth + 1)
                act.activation(root[:, :], bank[b][:, 0:T], ACT.Ln, scale=1.0 / D_MODEL, bias=eps[:, :]).then_inc(rooted, 1)
                act.wait_ge(rooted, nth + 1)
                act.activation(rstd[:, :], root[:, :], ACT.Exp, scale=-0.5).then_inc(rstd_done, 1)

            act.wait_ge(vecs_ready, 1)
            act.wait_ge(eps_set, 1)
            for kt in range(KT):
                scale_x(0, kt)
            for layer in range(DEPTH):
                L = layer
                if layer:
                    inverse_root(2)

                def mixer_step(it, s):
                    if (it, s) == (1, 0):
                        act.wait_ge(bank_read, IN0[L] + 4)
                        act.activation(sig[:, :, :], proj[:, 0, :, :], ACT.Sigmoid).then_inc(sig_done, 1)
                    if (it, s) == (2, 0):
                        act.wait_ge(bank_read, IN0[L] + 8)
                        act.activation(proj[:, 1, :, :], proj[:, 1, :, :], ACT.Sigmoid).then_inc(sig_done, 1)
                    if (it, s) == (2, 2):
                        act.wait_ge(forget_done, 4 * (L + 1))
                        act.activation(logf[:, :, :], proj[:, 1, :, 0:SEQ], ACT.Ln).then_inc(logf_done, 1)
                    if (it, s) == (3, 0):
                        act.wait_ge(bank_read, IN0[L] + 12)
                        act.wait_ge(q_gated, L + 1)
                        act.activation(sig[:, :, :], proj[:, 3, :, :], ACT.Sigmoid).then_inc(sig_done, 1)
                    if (it, s) in ACT_LEVELS:
                        exp_level(ACT_LEVELS[(it, s)])

                def exp_level(j):
                    half = (LEVELS + (SEG,))[j]
                    act.wait_ge(diff_done, 8 * L + j + 1)
                    d = diff[j % 2][:, :, :].rearrange("p h (n t) -> p (h n) t", t=2 * half)
                    right = d if half < SEG else decay[:, :, :].rearrange("p h (n t) -> p (h n) t", t=2 * half)
                    act.activation(d[:, :, 0:half], d[:, :, 0:half], ACT.Exp, scale=-1.0).then_inc(diff_exp, 1)
                    act.activation(d[:, :, half:], right[:, :, half:], ACT.Exp).then_inc(diff_exp, 1)
                ACT_LEVELS = {(3, 1): 0, (3, 2): 1, (3, 3): 2, (4, 0): 3, (4, 1): 4, (4, 2): 5, (4, 3): 6}
                weight_pass(f"in{L}", mixer_step, unroll=True)
                split(3, WO0[L] // 4, WO0[L] + 3, KT)

                def put(i):
                    act.wait_ge(scored, 17 * L + i + 1)
                    src = bank[4 + i % 4][:, :].rearrange("p (h t) -> p h t", h=HEADS)
                    if i == 16:
                        act.activation(scores_x[:, :, :], src, ACT.Copy).then_inc(scores_put, 1)
                        return
                    act.wait_ge(scores_taken, 12 * (L + 1))
                    half = LEVELS[i // 2 - 1]
                    for s0 in range(0, SEG, 2 * half):
                        t = slice(s0 + half, s0 + 2 * half)
                        done = act.activation(scores[s0:s0 + half, i % 2, :, t], src[s0:s0 + half, :, t], ACT.Copy)
                    done.then_inc(scores_put, 1)

                def square_heads(k, src):
                    act.activation(hgo_sq[:, :, HG_SUMS[k][2]], src, ACT.Square).then_inc(hgo_squared, 1)
                for i in range(2):
                    act.wait_ge(v_turned, 2 * L + i + 1)
                    act.activation(values[:, i, :], bank[i][:, :], ACT.Copy).then_inc(v_copied, 1)
                put(12)
                put(13)
                exp_level(7)
                put(14)
                put(15)
                act.wait_ge(end_diff, L + 1)
                act.activation(diff[0][:, :, SEG:SEQ], diff[0][:, :, SEG:SEQ], ACT.Exp, scale=-1.0).then_inc(end_exp, 1)
                act.activation(diff[0][:, :, 0:1], decay[:, :, SEQ - 1:SEQ], ACT.Exp).then_inc(end_exp, 1)
                put(16)
                act.wait_ge(attended, 2 * L + 1)
                square_heads(0, bank[6][:, :].rearrange("p (h t) -> p h t", h=HEADS))
                act.wait_ge(sample_done, 2 * (L + 1))
                square_heads(1, sample_o[:, :, :])
                for g in range(4):
                    act.wait_ge(pool_mapped, 4 * L + g + 1)
                    act.activation(mix_hi[:, 4 + g, :], bank[g][:, 0:T], ACT.Copy,
                                   scale=vecs[:, V_POOL + 4 * L + g:V_POOL + 4 * L + g + 1]).then_inc(pool_hi, 1)
                    if g == 1:
                        act.wait_ge(attended, 2 * L + 2)
                        square_heads(2, bank[7][:, :].rearrange("p (h t) -> p h t", h=HEADS))
                for k, (n, cols, tok) in enumerate(HG_SUMS):
                    act.wait_ge(hgo_summed, 3 * L + k + 1)
                    act.activation(hg_rstd[:, :, tok], bank[n][:, cols].rearrange("p (h t) -> p h t", h=HEADS), ACT.Ln, scale=1.0 / 128,
                                   bias=eps[:, :]).then_inc(hgo_rooted, 1)
                for k, (_, _, tok) in enumerate(HG_SUMS):
                    act.wait_ge(hgo_rooted, 3 * L + k + 1)
                    act.activation(hg_rstd[:, :, tok], hg_rstd[:, :, tok], ACT.Exp, scale=-0.5).then_inc(hgo_rstd, 1)
                for h in range(HEADS):
                    act.wait_ge(hgo_scaled, 16 * L + 12 + h + 1)
                    act.activation(mix_hi[:, h, :], hg_tmp[:, h, :], ACT.Copy).then_inc(mix_hi_done, 1)
                for i in range(2):
                    act.wait_ge(kdec_turned, 2 * L + i + 1)
                    act.activation(kdecT[:, i, :], bank[6 + i][:, :], ACT.Copy).then_inc(kdec_copied, 1)

                def copy_final():
                    act.wait_ge(final_state, L + 1)
                    act.activation(new_state[:, :, :], bank[6][:, :].rearrange("p (h v) -> p h v", h=HEADS), ACT.Copy).then_inc(final_copied, 1)

                def copy_tail():
                    act.wait_ge(tail_turned, L + 1)
                    act.activation(pool_tail[:, :], bank[7][0:POOL_BUF + DEC, :], ACT.Copy).then_inc(tail_copied, 1)

                def multiply_kv(b):
                    act.wait_ge(v_spread, 8 * L + b + 1)
                    if b >= 2:
                        act.wait_ge(state_done, 8 * L + b - 1)
                    for h in range(HEADS):
                        done = act.activation(outer[:, b % 2, h, :], bank[4 + b % 2][:, 128 * h:128 * (h + 1)], ACT.Copy,
                                              scale=keys[:, h, SEQ + b:SEQ + b + 1])
                    done.then_inc(outer_done, 1)

                def out_step(it, s):
                    if (it, s) == (0, 1):
                        copy_final()
                    if 4 * it + s and L == 0:
                        scale_x(1, 4 * it + s - 1)
                    if (it, s) == (0, 2):
                        copy_tail()
                    if 4 * it + s:
                        multiply_kv(4 * it + s - 1)
                weight_pass(f"out{L}", out_step, unroll=True)
                if layer == 0:
                    scale_x(1, KT - 1)
                multiply_kv(DEC - 1)
                if layer == 0:
                    inverse_root(1, 7)

                    def ffn_step(it, s):
                        if s == 0 and isinstance(it, int) and it == 0:
                            return
                        it, s = (it, s - 1) if s else (it - 1, RING - 1)
                        i = s // 2
                        if s % 2 == 0:
                            act.wait_ge(bank_read, GU0 + 4 * it + s + 1)
                            if not (isinstance(it, int) and it == 0):
                                act.wait_ge(ffn_lo_done, 2 * it + i - 1)
                            act.activation(gate_act[i][:, :], gate_in[i][:, :], ACT.Silu).then_inc(gate_done, 1)
                        else:
                            act.wait_ge(ffn_mult, 2 * it + i + 1)
                            act.activation(ffn_hi[:, ds(2 * it + i, 1), :].rearrange("p a t -> p (a t)"), gate_act[i][:, :], ACT.Copy).then_inc(ffn_hi_done, 1)
                    weight_pass("ffn_up0", ffn_step, peel=True)
                    ffn_step(FT // 2, 0)

                    def down_step(it, s):
                        if s >= 2:
                            scale_x(2, 2 * it + s - 2)
                    weight_pass("ffn_down0", down_step)
            def split_e(j, kts_cols, turn=None):
                u = j if turn is None else HEAD_UNITS + TURN_UNITS * turn + j
                jj = j if turn is None else HEAD_UNITS + j
                wait_raw(act, j, turn)
                if turn is None and j < SPLIT_RING:
                    act.wait_ge(unit_used, LAST_UNIT)
                else:
                    act.wait_ge(moe_used, u - SPLIT_RING + 1)
                act.activation(w_hi[jj % SPLIT_RING][:, 0:kts_cols, :], raw_e[raw_slot(j, turn)][:, 0:kts_cols, :], ACT.Copy).then_inc(moe_hi, 1)

            def round_packed(n):
                q, d = n // 4, n % 4
                act.wait_ge(gathered, n + 1)
                act.activation(packed[:, 2 * q:2 * q + 2, 0, 256 * d:256 * (d + 1)].rearrange("p e (d s) -> p e d s", d=2),
                               bank[gather_bank(n)][:, :].rearrange("p (d e s) -> p e d s", d=2, e=2), ACT.Copy).then_inc(packed_hi, 1)
            split_e(0, FE)
            inverse_root(3, 7)
            act.wait_ge(scaled_done, KT)
            act.dma_start(h_saved, scaled_m[:, :, :].rearrange("p k t -> p (k t)")).then_inc(h_out, 16)
            split_e(1, FE)
            act.wait_ge(rstd_turned, 2)
            for i, (_, rows) in enumerate(TOKEN_TILES):
                for c in range(2):
                    act.wait_ge(h_turned, 2 * i + c + 1)
                    act.activation(h_hi[0:rows, i, 512 * c:512 * (c + 1)], bank[(0, 1, 2, 3, 4, 6)[2 * i + c]][0:rows, :], ACT.Copy, scale=rstd_tok[0:rows, i:i + 1]).then_inc(h_hi_done, 1)
            act.wait_ge(route, GAP)
            act.activation(tops[:, 1, :], tops[:, 1, :], ACT.Exp).then_inc(route_exp, 1)
            act.wait_ge(state_out, 32)
            def set_x_hi(e, c, u):
                if u is None:
                    act.wait_ge(packed_hi, 2 * c + 2)
                else:
                    act.wait_ge(packed_lo, 4 if isinstance(e, int) and e < 2 else 16)
                if u is None:
                    act.wait_ge(unit_used, LAST_UNIT)
                else:
                    act.wait_ge(moe_used, u)
                src = packed[:, ds(e, 1), 0, 512 * c:512 * (c + 1)].rearrange("p a n -> p (a n)")
                act.activation(x_hi[:, 4 * c:4 * (c + 1), :].rearrange("p a b -> p (a b)"), src, ACT.Copy).then_inc(x_hi_set, 1)

            def silu_gate(e, u):
                act.wait_ge(moe_used, u)
                if not isinstance(e, int) or e:
                    act.wait_ge(hid_turned, 3 * e)
                for p, (c0, width) in enumerate(PIECES):
                    act.activation(act_e[:, c0:c0 + width], bank[p][:, 0:width], ACT.Silu).then_inc(gate_silu, 1)

            def round_hidden(e):
                for p, (c0, width) in enumerate(PIECES):
                    act.wait_ge(hid_turned, 3 * e + p + 1)
                    act.activation(hid_hi[:, c0 // 128:(c0 + width) // 128, :], bank[3 + p][:, 0:width].rearrange("p (a b) -> p a b", b=128), ACT.Copy).then_inc(hid_hi_done, 1)

            def round_result(e, u):
                act.wait_ge(moe_used, u)
                for c in range(2):
                    act.activation(packed[:, ds(e, 1), 0, 512 * c:512 * (c + 1)].rearrange("p a n -> p (a n)"), bank[6 + c][:, :], ACT.Copy,
                                   scale=slot_gate[:, ds(e, 1)]).then_inc(y_hi_done, 1)

            for c in range(2):
                round_packed(2 * c)
                round_packed(2 * c + 1)
                set_x_hi(0, c, None)
            for j in range(2, HEAD_UNITS + LOAD_AHEAD):
                if j < HEAD_UNITS:
                    split_e(j, FE)
                else:
                    split_e(j - HEAD_UNITS, FE, turn=0)
                if 0 <= j - 3 < N_EXPERTS:
                    act.wait_ge(hot_turned, j - 2)
                    act.activation(slot_hot[:, j - 3, :], bank[3 + j % 2][:, 0:T], ACT.Copy).then_inc(hot_copied, 1)
                if 0 <= j - 3 < 12:
                    round_packed(4 + j - 3)
                if j == KT + LOAD_AHEAD:
                    silu_gate(0, KT)
                if j == HEAD_UNITS - 4 + SPLIT_RING - 1:
                    set_x_hi(1, 0, HEAD_UNITS - 4)
            act.wait_ge(y_lo_done, 1)

            def turn_e(e, last):
                base = HEAD_UNITS + TURN_UNITS * e
                for j, (kind, _, k) in enumerate(TURN):
                    ahead = j + LOAD_AHEAD
                    if ahead < TURN_UNITS:
                        split_e(ahead, FE if TURN[ahead][0] != "down" else KT, turn=e)
                    else:
                        split_e(ahead - TURN_UNITS, KT if last else FE, turn=e + 1)
                    if j == 0:
                        set_x_hi(e + 1, 1, base)
                    if j == 5:
                        round_hidden(e)
                    if j == KT + 1:
                        silu_gate(e + 1, base + KT)
                    if j == KT + FE + 1:
                        round_result(e, base + KT + FE)
                    if j == TURN_UNITS - 3 and not last:
                        set_x_hi(e + 2, 0, base + TURN_UNITS - 4)
            with act.Fori(0, N_EXPERTS - 2) as e:
                turn_e(e, False)
            turn_e(N_EXPERTS - 2, True)
            round_hidden(N_EXPERTS - 1)
            for j in range(LOAD_AHEAD, FE):
                split_e(j, KT, turn=N_EXPERTS - 1)
            round_result(N_EXPERTS - 1, HEAD_UNITS + TURN_UNITS * (N_EXPERTS - 1) + FE)
            act.wait_ge(route, ROUTED)
            n_rows = act.value_load(longest_i[0:1, 0:1])
            with act.If(n_rows > CAP):
                with act.Fori(0, N_EXPERTS * FE) as n:
                    act.wait_ge(all_up, 2 * n + 1)
                    act.activation(act_all[:, :], bank[0][:, 0:T], ACT.Silu).then_inc(all_silu, 1)
                act.wait_ge(all_added, N_EXPERTS * FE * KT + KT)
            act.end_ifs()
            act.activation(root[:, 0:1], eps[:, :], ACT.Sqrt).then_inc(rms_done, 1)
            act.wait_ge(moe_added, KT)
            for kt in range(KT):
                act.activation(square_f[:, kt, :], xT[:, kt, :], ACT.Square).then_inc(squared, 1)
            act.wait_ge(summed, 5)
            act.wait_ge(rms_done, 1)
            for i, (_, rows) in enumerate(TOKEN_TILES):
                b, c = NORM_SUMS[i]
                act.activation(root[0:rows, i:i + 1], bank[b][0:rows, c:c + 1], ACT.Sqrt, scale=1.0 / D_MODEL, bias=eps[0:rows, :]).then_inc(rms_done, 1)
            act.wait_ge(rms_inverted, 3)
            for i, (_, rows) in enumerate(TOKEN_TILES):
                act.wait_ge(turned, i + 1)
                act.activation(y_rows[0:rows, i, 0:512], bank[i][0:rows, :], ACT.Copy, scale=rstd_tok[0:rows, i:i + 1]).then_inc(y_left, 1)

        @block.vector
        def _(dve):
            dve.wait_ge(vecs_turned, 1)
            dve.tensor_copy(vecs[:, :], bank[7][:, 0:V_COLS]).then_inc(vecs_ready, 1)
            dve.wait_ge(vecs_ready, 1)
            l0, l1 = vecs[:, V_LB:V_LB + HEADS], vecs[:, V_LB + HEADS:V_LB + 2 * HEADS]
            top, e0, e1, inv = (lb_tmp[:, i, :] for i in range(4))
            dve.tensor_tensor(top, l0, l1, ALU.max).then_inc(lb_step, 1)
            dve.wait_ge(lb_step, 1)
            dve.tensor_tensor(e0, l0, top, ALU.subtract).then_inc(lb_step, 1)
            dve.tensor_tensor(e1, l1, top, ALU.subtract).then_inc(lb_step, 1)
            dve.wait_ge(lb_exp, 1)
            dve.tensor_tensor(top, e0, e1, ALU.add).then_inc(lb_step, 1)
            dve.wait_ge(lb_step, 4)
            dve.reciprocal(inv, top).then_inc(lb_step, 1)
            dve.wait_ge(lb_step, 5)
            dve.tensor_tensor(e0, e0, inv, ALU.mult).then_inc(lb_step, 1)
            dve.tensor_tensor(e1, e1, inv, ALU.mult).then_inc(lb_step, 1)
            dve.wait_ge(lb_step, 7)
            dve.tensor_tensor(top, e0, e1, ALU.add).then_inc(lb_step, 1)
            dve.tensor_tensor(lbound[:, 0, :], e0, e0, ALU.subtract).then_inc(lb_step, 1)
            dve.wait_ge(lb_step, 8)
            dve.tensor_tensor(lbound[:, 1, :], top, e0, ALU.subtract).then_inc(lb_step, 1)
            dve.wait_ge(lb_step, 10)
            dve.tensor_scalar(lspan[:, :, :], lbound[:, :, :], -1.0, 1.0, ALU.mult, ALU.add).then_inc(lb_step, 1)
            for kt in range(KT):
                dve.wait_ge(x_turned, kt + 1)
                dve.tensor_copy(xT[:, kt, :], bank[kt % 4][:, 0:T]).then_inc(x_loaded, 1)

            def split(s, n, kts):
                dve.wait_ge(hi_done, n + 1)
                dve.tensor_tensor(w_lo[s][:, 0:kts, :], raw[s][:, 0:kts, :], w_hi[s][:, 0:kts, :].bitcast(f32), ALU.subtract).then_inc(lo_done, 1)

            def weight_pass(name, body, unroll=False):
                i = [p[0] for p in PASSES].index(name)
                _, n0, units, kts = PASSES[i]
                its = units // RING

                def step(it, last):
                    for s in range(RING):
                        n = n0 + 4 * it + s
                        if s == 0 and name[:3] == "out" and it == 0:
                            pass
                        elif s == 0:
                            split(3, n + 3, kts)
                        elif not last:
                            split(s - 1, n + 3, kts)
                        elif i + 1 < len(PASSES):
                            split(s - 1, PASSES[i + 1][1] + s - 1, PASSES[i + 1][3])
                        body(it, s)
                if n0 == 0:
                    for s in range(3):
                        split(s, s, kts)
                if unroll:
                    for it in range(its - 1):
                        step(it, False)
                else:
                    with dve.Fori(0, its - 1) as it:
                        step(it, False)
                step(its - 1, True)

            def scale_x(version, kt):
                col = (V_MIX, V_FFN, V_MIX + KT)[version]
                dve.wait_ge(norm_hi, KT * version + kt + 1)
                tile = lambda t: t[:, kt, :] if isinstance(kt, int) else t[:, ds(kt, 1), :].rearrange("p a t -> p (a t)")
                gain = vecs[:, col + kt:col + kt + 1] if isinstance(kt, int) else vecs[:, ds(col + kt, 1)]
                dve.scalar_tensor_tensor(tile(act_lo), tile(xT), gain, tile(act_hi).bitcast(f32), ALU.mult, ALU.subtract).then_inc(norm_lo, 1)

            dve.wait_ge(x_loaded, KT)
            for kt in range(KT):
                scale_x(0, kt)
            dve.wait_ge(tables_in, 16)
            for layer in range(DEPTH):
                L = layer

                def mixer_step(it, s):
                    n = IN0[L] + 4 * it + s
                    m = 4 * (it - 3) + s - 2
                    if m >= 0:
                        side(m)
                        take(2 * m)
                        take(2 * m + 1)
                    dve.wait_ge(unit_used, n + 1)
                    dve.wait_ge(rstd_done, (1, 3)[L])
                    out = proj[:, GROUPS[it], s, :] if it < 4 else up[:, s, PAD:]
                    dve.tensor_tensor(out, bank[s][:, 0:T], rstd[:, :], ALU.mult).then_inc(bank_read, 1)
                    if (it, s) == (1, 3):
                        dve.wait_ge(sig_done, 3 * L + 1)
                        dve.wait_ge(bank_read, IN0[L] + 4)
                        dve.tensor_tensor(proj[:, 0, :, :], proj[:, 0, :, :], sig[:, :, :], ALU.mult).then_inc(q_gated, 1)
                    if (it, s) == (2, 1):
                        dve.wait_ge(lb_step, 11)
                        dve.wait_ge(sig_done, 3 * L + 2)
                        for h in range(HEADS):
                            dve.tensor_scalar(proj[:, 1, h, :], proj[:, 1, h, :], lspan[:, L, h:h + 1], lbound[:, L, h:h + 1],
                                              ALU.mult, ALU.add).then_inc(forget_done, 1)
                    if (it, s) == (2, 3):
                        dve.wait_ge(logf_done, L + 1)
                        dve.wait_ge(segments_set, 2 * (L + 1))
                        dve.tensor_tensor_scan(decay[:, :, :].rearrange("p h t -> p (h t)"), segments[:, :, :].rearrange("p h t -> p (h t)"),
                                               logf[:, :, :].rearrange("p h t -> p (h t)"), 0.0, ALU.mult, ALU.add).then_inc(decay_done, 1)
                    if (it, s) == (3, 3):
                        dve.tensor_tensor(sample_kq[:, :, :], keys[:, :, SEQ:T], proj[:, 0, :, SEQ:T], ALU.mult).then_inc(kq_done, 1)

                def side(j):
                    half = (LEVELS + (SEG,))[j]
                    e, z, q, k = (t.rearrange("p h (n t) -> p h n t", t=2 * half)
                                  for t in (diff[j % 2][:, :, :], sided[j % 2][:, :, :], proj[:, 0, :, 0:SEQ], keys[:, :, 0:SEQ]))
                    if j >= 2:
                        dve.wait_ge(scored, 17 * L + 2 * j)
                    if j == 0:
                        dve.wait_ge(keys_done, L + 1)
                        dve.wait_ge(q_gated, L + 1)
                    if j == 1:
                        dve.wait_ge(decay_done, L + 1)
                    dve.wait_ge(diff_exp, 16 * L + 2 * j + 1)
                    dve.tensor_tensor(z[:, :, :, 0:half], e[:, :, :, 0:half], k[:, :, :, 0:half], ALU.mult).then_inc(sided_done, 1)
                    dve.wait_ge(diff_exp, 16 * L + 2 * j + 2)
                    dve.tensor_tensor(z[:, :, :, half:], e[:, :, :, half:], q[:, :, :, half:], ALU.mult).then_inc(sided_done, 1)

                def take(i):
                    dve.wait_ge(scored, 17 * L + i + 1)
                    src = bank[4 + i % 4][:, :].rearrange("p (h t) -> p h t", h=HEADS)
                    if i >= 2:
                        dve.wait_ge(scores_taken, 12 * L + i - 1)
                    else:
                        dve.wait_ge(scores_zeroed, L + 1)
                    mask = consts[:, C_MASK + 128 * (i // 2):C_MASK + 128 * (i // 2 + 1)].bitcast(i32)
                    dve.copy_predicated(scores[:, i % 2, :, :], mask.unsqueeze(1).broadcast_to([128, HEADS, SEG]), src).then_inc(scores_taken, 1)

                def scale_heads(src, tok):
                    for h in range(HEADS):
                        dve.scalar_tensor_tensor(hg_tmp[:, h, tok], src[:, h, :], vecs[:, V_HG + 4 * L + h:V_HG + 4 * L + h + 1],
                                                 proj[:, 3, h, tok], ALU.mult, ALU.mult).then_inc(hgo_scaled, 1)
                weight_pass(f"in{L}", mixer_step, unroll=True)
                split(3, WO0[L] + 3, KT)
                side(6)
                dve.wait_ge(bank_read, IN0[L] + 20)
                dve.wait_ge(pads_zeroed, L + 1)
                src, dst = up, win_a
                for j in range(4):
                    back = 1 << j
                    lo = 2 * back - 1
                    if j:
                        dve.wait_ge(windowed, 8 * L + j)
                    if j == 2:
                        side(7)
                    dve.tensor_tensor(dst[:, j:, lo:PAD + SEQ], src[:, j:, lo:PAD + SEQ],
                                      src[:, j:, lo - back:PAD + SEQ - back], ALU.add).then_inc(windowed, 1)
                    src, dst = dst, (win_b if dst is win_a else win_a)
                dve.wait_ge(windowed, 8 * L + 4)
                for g in range(4):
                    w = (win_a, win_b)[g % 2]
                    dve.tensor_tensor(w[:, g, PAD:2 * PAD], w[:, g, PAD:2 * PAD], corr[:, g, :], ALU.mult).then_inc(windowed, 1)
                dve.wait_ge(sampled, 5 * (L + 1))
                vs = proj[:, 2, :, SEQ:T]
                dve.wait_ge(bank_read, IN0[L] + 16)
                dve.tensor_tensor(sample_o[:, :, :], bank[3][:, SIDE].rearrange("p (h b) -> p h b", h=HEADS), vs, ALU.mult).then_inc(sample_done, 1)
                dve.wait_ge(sample_done, 2 * L + 1)
                dve.tensor_tensor(sample_o[:, :, :], bank[2][:, SIDE].rearrange("p (h b) -> p h b", h=HEADS), sample_o[:, :, :], ALU.add).then_inc(sample_done, 1)
                dve.wait_ge(sig_done, 3 * L + 3)
                dve.tensor_tensor(proj[:, 3, :, :], proj[:, 3, :, :], sig[:, :, :], ALU.mult).then_inc(g_gated, 1)
                dve.wait_ge(g_gated, L + 1)
                dve.wait_ge(sample_done, 2 * (L + 1))
                scale_heads(sample_o, slice(SEQ, T))
                dve.wait_ge(past_summed, L + 1)
                for g in range(4):
                    w = (win_a, win_b)[g % 2]
                    dve.tensor_tensor(w[:, g, PAD + SEQ:], bank[2][:, DEC * g:DEC * (g + 1)], up[:, g, PAD + SEQ:], ALU.add).then_inc(past_added, 1)
                dve.wait_ge(hgo_squared, 3 * L + 1)
                scale_heads(bank[6][:, :].rearrange("p (h t) -> p h t", h=HEADS), slice(0, SEG))
                dve.wait_ge(windowed, 8 * (L + 1))
                for g in range(4):
                    w = (win_a, win_b)[g % 2]
                    dve.wait_ge(past_added, 4 * L + g + 1)
                    dve.scalar_tensor_tensor(w[:, g, PAD:], w[:, g, PAD:], 1.0 / WINDOWS[g], up[:, g, PAD:], ALU.mult, ALU.subtract).then_inc(pooled, 1)
                dve.wait_ge(hgo_squared, 3 * L + 3)
                scale_heads(bank[7][:, :].rearrange("p (h t) -> p h t", h=HEADS), slice(SEG, SEQ))
                for g in range(4):
                    dve.wait_ge(pool_hi, 4 * L + g + 1)
                    dve.scalar_tensor_tensor(mix_lo[:, 4 + g, :], bank[g][:, 0:T], vecs[:, V_POOL + 4 * L + g:V_POOL + 4 * L + g + 1],
                                             mix_hi[:, 4 + g, :].bitcast(f32), ALU.mult, ALU.subtract).then_inc(pool_lo, 1)
                dve.wait_ge(hgo_rstd, 3 * (L + 1))
                dve.wait_ge(hgo_scaled, 16 * L + 12)
                for h in range(HEADS):
                    dve.tensor_tensor(hg_tmp[:, h, :], hg_tmp[:, h, :], hg_rstd[:, h, :], ALU.mult).then_inc(hgo_scaled, 1)
                for h in range(HEADS):
                    dve.wait_ge(mix_hi_done, 4 * L + h + 1)
                    dve.tensor_tensor(mix_lo[:, h, :], hg_tmp[:, h, :], mix_hi[:, h, :].bitcast(f32), ALU.subtract).then_inc(mix_lo_done, 1)

                def scale_m(kt):
                    wait_x(dve, 3, kt)
                    dve.tensor_scalar(scaled_m[:, kt, :], xT[:, kt, :], vecs[:, V_FFN + KT + kt:V_FFN + KT + kt + 1], None, ALU.mult).then_inc(scaled_done, 1)

                def out_step(it, s):
                    kt = 4 * it + s
                    dve.wait_ge(unit_used, WO0[L] + kt + 1)
                    dve.tensor_tensor(xT[:, kt, :], bank[s][:, 0:T], xT[:, kt, :], ALU.add).then_inc(bank_read, 1)
                    if kt and L == 0:
                        scale_x(1, kt - 1)
                    if kt and L == 1:
                        scale_m(kt - 1)
                weight_pass(f"out{L}", out_step, unroll=True)
                if layer == 0:
                    scale_x(1, KT - 1)

                    def ffn_step(it, s):
                        i = s // 2
                        n = GU0 + 4 * it + s
                        dve.wait_ge(unit_used, n + 1)
                        out = (gate_in, up_in)[s % 2][i]
                        dve.wait_ge(rstd_done, 2)
                        dve.tensor_tensor(out[:, :], bank[s][:, 0:T], rstd[:, :], ALU.mult).then_inc(bank_read, 1)
                        if s % 2:
                            dve.wait_ge(gate_done, 2 * it + i + 1)
                            dve.wait_ge(bank_read, n + 1)
                            dve.tensor_tensor(gate_act[i][:, :], gate_act[i][:, :], up_in[i][:, :], ALU.mult).then_inc(ffn_mult, 1)
                    weight_pass("ffn_up0", ffn_step)

                    def down_step(it, s):
                        if s % 2:
                            dve.wait_ge(unit_used, DN0 + 4 * it + s + 1)
                            col = xT[:, ds(2 * it + s // 2, 1), :].rearrange("p a t -> p (a t)") if not isinstance(it, int) else xT[:, 2 * it + s // 2, :]
                            dve.tensor_tensor(col, bank[s - 1][:, 0:T], col, ALU.add).then_inc(bank_read, 2)
                        if s >= 2:
                            scale_x(2, 2 * it + s - 2)
                    weight_pass("ffn_down0", down_step)
            scale_m(KT - 1)

            def split_e(j, kts_cols, turn=None):
                u = j if turn is None else HEAD_UNITS + TURN_UNITS * turn + j
                jj = j if turn is None else HEAD_UNITS + j
                dve.wait_ge(moe_hi, u + 1)
                hi, lo = w_hi[jj % SPLIT_RING][:, 0:kts_cols, :], w_lo[jj % SPLIT_RING][:, 0:kts_cols, :]
                dve.tensor_tensor(lo, raw_e[raw_slot(j, turn)][:, 0:kts_cols, :], hi.bitcast(f32), ALU.subtract).then_inc(moe_lo, 1)

            def rest_of_tokens(n):
                i, c = n // 2, n % 2
                rows = TOKEN_TILES[i][1]
                dve.wait_ge(h_hi_done, n + 1)
                dve.scalar_tensor_tensor(h_lo[0:rows, i, 512 * c:512 * (c + 1)], bank[(0, 1, 2, 3, 4, 6)[n]][0:rows, :], rstd_tok[0:rows, i:i + 1],
                                         h_hi[0:rows, i, 512 * c:512 * (c + 1)].bitcast(f32), ALU.mult, ALU.subtract).then_inc(h_lo_done, 1)

            def rest_of_packed(n):
                q, d = n // 4, n % 4
                dve.wait_ge(packed_hi, n + 1)
                view = [packed[:, 2 * q:2 * q + 2, half, 256 * d:256 * (d + 1)].rearrange("p e (d s) -> p e d s", d=2) for half in range(2)]
                dve.tensor_tensor(view[1], bank[gather_bank(n)][:, :].rearrange("p (d e s) -> p e d s", d=2, e=2), view[0].bitcast(f32), ALU.subtract).then_inc(packed_lo, 1)
            split_e(0, FE)
            dve.wait_ge(rstd_done, 4)
            dve.wait_ge(routed, 1)
            dve.tensor_tensor(logit_rows[:, :], bank[6][0:N_EXPERTS, 0:T], rstd[0:N_EXPERTS, :], ALU.mult).then_inc(logits_scaled, 1)
            dve.wait_ge(logits_zeroed, 1)
            dve.wait_ge(tokens_turned, 1)
            n_last = TOKEN_TILES[2][1]
            spread_rstd = bank[5][:, 128:512].rearrange("p (i t) -> p i t", i=3)
            dve.tensor_copy(rstd_tok[:, 0:2], spread_rstd[:, 0:2, 0]).then_inc(rstd_turned, 1)
            dve.tensor_copy(rstd_tok[0:n_last, 2:3], spread_rstd[0:n_last, 2, 0:1]).then_inc(rstd_turned, 1)
            steps = [0]

            def step_of(ins, last=True):
                ins.then_inc(route, 1)
                steps[0] += 1
                if last:
                    dve.wait_ge(route, steps[0])
            step_of(dve.tensor_copy(logits[:, 0:2, :], bank[5][:, 0:16].rearrange("p (i e) -> p i e", i=2)), last=False)
            step_of(dve.tensor_copy(logits[0:n_last, 2, :], bank[5][0:n_last, 16:24]))
            wide = [128, 3, N_EXPERTS, N_EXPERTS]
            each = logits[:, :, :].unsqueeze(2).broadcast_to(wide)
            own = logits[:, :, :].unsqueeze(3).broadcast_to(wide)
            lower = consts[:, C_LOWER:C_LOWER + 64].unsqueeze(1).broadcast_to([128, 3, 64])
            equal_flat = equal[:, :, :, :].rearrange("p i e j -> p i (e j)")
            step_of(dve.tensor_tensor(equal[:, :, :, :], each, own, ALU.is_equal), last=False)
            step_of(dve.tensor_tensor(greater[:, :, :, :], each, own, ALU.is_gt))
            step_of(dve.tensor_tensor(equal_flat, equal_flat, lower, ALU.mult))
            step_of(dve.tensor_tensor(greater[:, :, :, :], greater[:, :, :, :], equal[:, :, :, :], ALU.add))
            step_of(dve.tensor_reduce(rank[:, :, :], greater[:, :, :, :], AX.X, ALU.add))
            step_of(dve.tensor_single_scalar(first[:, :, :], rank[:, :, :], 0.0, ALU.is_equal), last=False)
            step_of(dve.tensor_single_scalar(chosen[:, :, :], rank[:, :, :], 2.0, ALU.is_lt))
            assert steps[0] == CHOSEN, steps[0]
            step_of(dve.tensor_single_scalar(second[:, :, :], rank[:, :, :], 1.0, ALU.is_equal))
            step_of(dve.tensor_tensor(picked[:, :, :], logits[:, :, :], first[:, :, :], ALU.mult), last=False)
            step_of(dve.tensor_tensor(picked_2[:, :, :], logits[:, :, :], second[:, :, :], ALU.mult))
            step_of(dve.tensor_reduce(tops[:, 0, :], picked[:, :, :], AX.X, ALU.add), last=False)
            step_of(dve.tensor_reduce(tops[:, 1, :], picked_2[:, :, :], AX.X, ALU.add))
            dve.wait_ge(state_done, 2 * DEC)
            for n in range(4):
                rest_of_tokens(n)
            dve.wait_ge(placed, 1)
            flat = slot[:, :, :].rearrange("p i e -> p (i e)")
            step_of(dve.scalar_tensor_tensor(flat, bank[7][:, 0:24], 1.0, chosen[:, :, :].rearrange("p i e -> p (i e)"), ALU.add, ALU.mult))
            step_of(dve.tensor_scalar(flat, flat, -1.0, None, ALU.add))
            step_of(dve.tensor_tensor(tops[:, 1, :], tops[:, 1, :], tops[:, 0, :], ALU.subtract), last=False)
            dve.wait_ge(h_out, 16)
            dve.wait_ge(h_turned, 6)

            def mark_slots(e0, e1):
                for i, (_, rows) in enumerate(TOKEN_TILES):
                    shape = [rows, e1 - e0, CAP]
                    dve.tensor_tensor(token_hot[0:rows, i, e0:e1, :], iota[0:rows, :].unsqueeze(1).broadcast_to(shape),
                                      slot[0:rows, i, e0:e1].unsqueeze(2).broadcast_to(shape), ALU.is_equal).then_inc(hot, 1)
            mark_slots(0, 2)
            for n in (4, 5):
                rest_of_tokens(n)
            mark_slots(2, N_EXPERTS)
            dve.wait_ge(route_exp, 1)
            step_of(dve.tensor_scalar(tops[:, 2, :], tops[:, 1, :], 1.0, None, ALU.add))
            step_of(dve.reciprocal(tops[:, 2, :], tops[:, 2, :]))
            step_of(dve.tensor_tensor(tops[:, 3, :], tops[:, 1, :], tops[:, 2, :], ALU.mult))
            per = [128, 3, N_EXPERTS]
            step_of(dve.tensor_tensor(gates[:, :, :], first[:, :, :], tops[:, 2, :].unsqueeze(2).broadcast_to(per), ALU.mult), last=False)
            step_of(dve.tensor_tensor(second[:, :, :], second[:, :, :], tops[:, 3, :].unsqueeze(2).broadcast_to(per), ALU.mult))
            step_of(dve.tensor_tensor(gates[:, :, :], gates[:, :, :], second[:, :, :], ALU.add))
            step_of(dve.tensor_reduce(longest[:, :], bank[7][:, 24:32], AX.X, ALU.max))
            step_of(dve.tensor_copy(longest_i[:, :], longest[:, :]), last=False)
            step_of(dve.scalar_tensor_tensor(over[:, :, :], slot[:, :, :], float(CAP), gates[:, :, :], ALU.is_ge, ALU.mult))
            assert steps[0] == ROUTED, steps[0]
            dve.wait_ge(unit_used, LAST_UNIT)
            for c in range(2):
                rest_of_packed(2 * c)
                rest_of_packed(2 * c + 1)
                dve.wait_ge(packed_lo, 2 * c + 2)
                dve.tensor_copy(x_lo[:, 4 * c:4 * (c + 1), :].rearrange("p a b -> p (a b)"), packed[:, 0, 1, 512 * c:512 * (c + 1)]).then_inc(x_lo_set, 1)
            split_e(1, FE)

            def gate_up(e, u):
                dve.wait_ge(moe_used, u)
                for p, (c0, width) in enumerate(PIECES):
                    dve.wait_ge(gate_silu, 3 * e + p + 1)
                    dve.tensor_tensor(act_e[:, c0:c0 + width], bank[3 + p][:, 0:width], act_e[:, c0:c0 + width], ALU.mult).then_inc(act_done, 1)

            def rest_of_hidden(e):
                for p, (c0, width) in enumerate(PIECES):
                    dve.wait_ge(hid_hi_done, 3 * e + p + 1)
                    ks = slice(c0 // 128, (c0 + width) // 128)
                    dve.tensor_tensor(hid_lo[:, ks, :], bank[3 + p][:, 0:width].rearrange("p (a b) -> p a b", b=128), hid_hi[:, ks, :].bitcast(f32), ALU.subtract).then_inc(hid_lo_done, 1)

            def rest_of_result(e):
                for c in range(2):
                    dve.wait_ge(y_hi_done, 2 * e + c + 1)
                    hi, lo = (packed[:, ds(e, 1), half, 512 * c:512 * (c + 1)].rearrange("p a n -> p (a n)") for half in range(2))
                    dve.scalar_tensor_tensor(lo, bank[6 + c][:, :], slot_gate[:, ds(e, 1)], hi.bitcast(f32), ALU.mult, ALU.subtract).then_inc(y_lo_done, 1)

            for j in range(2, HEAD_UNITS + LOAD_AHEAD):
                if j < HEAD_UNITS:
                    split_e(j, FE)
                else:
                    split_e(j - HEAD_UNITS, FE, turn=0)
                if j == 3:
                    dve.wait_ge(gate_slots, 1)
                    dve.tensor_copy(slot_gate[:, :], bank[5][:, 0:N_EXPERTS]).then_inc(y_lo_done, 1)
                if 0 <= j - 3 < 12:
                    rest_of_packed(4 + j - 3)

            def turn_e(e, last):
                for j in range(TURN_UNITS):
                    ahead = j + LOAD_AHEAD
                    if j == 0:
                        gate_up(e, HEAD_UNITS + TURN_UNITS * e)
                    if ahead < TURN_UNITS:
                        split_e(ahead, FE if TURN[ahead][0] != "down" else KT, turn=e)
                    else:
                        split_e(ahead - TURN_UNITS, KT if last else FE, turn=e + 1)
                    if j == 5:
                        rest_of_hidden(e)
                    if j == KT + FE + 1:
                        rest_of_result(e)
            with dve.Fori(0, N_EXPERTS - 2) as e:
                turn_e(e, False)
            turn_e(N_EXPERTS - 2, True)
            gate_up(N_EXPERTS - 1, HEAD_UNITS + TURN_UNITS * (N_EXPERTS - 1))
            rest_of_hidden(N_EXPERTS - 1)
            for j in range(LOAD_AHEAD, FE):
                split_e(j, KT, turn=N_EXPERTS - 1)
            rest_of_result(N_EXPERTS - 1)
            for kt in range(KT):
                dve.wait_ge(scattered, kt + 1)
                dve.tensor_tensor(xT[:, kt, :], bank[kt][:, 0:T], xT[:, kt, :], ALU.add).then_inc(moe_added, 1)
            n_rows = dve.value_load(longest_i[0:1, 0:1])
            with dve.If(n_rows > CAP):
                dve.wait_ge(all_in, 16)
                for kt in range(KT):
                    dve.tensor_tensor(h_all[:, kt, :], rstd[:, :], h_all[:, kt, :], ALU.mult).then_inc(all_added, 1)
                with dve.Fori(0, N_EXPERTS) as e:
                    dve.tensor_copy(over_col[:, :], over[:, :, ds(e, 1)].rearrange("p i a -> p (i a)")).then_inc(all_col, 1)
                    dve.wait_ge(all_spread, e + 1)
                    dve.tensor_copy(over_all[:, :], bank[2][:, 0:T]).then_inc(all_over, 1)
                    with dve.Fori(0, FE) as f:
                        n = e * FE + f
                        dve.wait_ge(all_silu, n + 1)
                        dve.wait_ge(all_up, 2 * n + 2)
                        dve.tensor_tensor(act_all[:, :], bank[1][:, 0:T], act_all[:, :], ALU.mult).then_inc(all_act, 1)
                        dve.wait_ge(all_act, 2 * n + 1)
                        dve.wait_ge(all_over, e + 1)
                        dve.tensor_tensor(act_all[:, :], act_all[:, :], over_all[:, :], ALU.mult).then_inc(all_act, 1)
                        for kt in range(KT):
                            dve.wait_ge(all_down, n * KT + kt + 1)
                            dve.tensor_tensor(xT[:, kt, :], bank[4 + kt % 4][:, 0:T], xT[:, kt, :], ALU.add).then_inc(all_added, 1)
                dve.wait_ge(all_added, N_EXPERTS * FE * KT + KT)
            dve.end_ifs()
            dve.wait_ge(moe_added, KT)
            for kt in range(KT):
                dve.tensor_scalar(scaled_f[:, kt, :], xT[:, kt, :], vecs[:, V_FINAL + kt:V_FINAL + kt + 1], None, ALU.mult).then_inc(scaled_done, 1)
            for i, (_, rows) in enumerate(TOKEN_TILES):
                dve.wait_ge(rms_done, i + 2)
                dve.reciprocal(rstd_tok[0:rows, i:i + 1], root[0:rows, i:i + 1]).then_inc(rms_inverted, 1)
            dve.wait_ge(rms_inverted, 3)
            for i, (_, rows) in enumerate(TOKEN_TILES):
                dve.wait_ge(turned, 3 + i + 1)
                dve.tensor_scalar(y_rows[0:rows, i, 512:1024], bank[5 + i][0:rows, :], rstd_tok[0:rows, i:i + 1], None, ALU.mult).then_inc(y_right, 1)

        @block.tensor
        def _(pe):
            pe.wait_ge(consts_in, 16)
            pe.wait_ge(vecs_in, 16 * 6)
            pe.transpose(bank[7][:, 0:V_COLS], vec_rows[:, :], ident[0:V_COLS, 0:V_COLS]).then_inc(vecs_turned, 1)
            pe.wait_ge(x_in, 48)
            for kt in range(KT):
                if kt >= 4:
                    pe.wait_ge(x_loaded, kt - 3)
                for i, (t0, rows) in enumerate(TOKEN_TILES):
                    mm = pe.transpose(bank[kt % 4][:, t0:t0 + rows], x_rows[0:rows, i, 128 * kt:128 * (kt + 1)], ident[0:rows, 0:rows])
                mm.then_inc(x_turned, 1)

            def sum_squares(nth, square, b):
                tiles = KT if nth == 0 else 1
                for kt in range(tiles):
                    pe.wait_ge(squared, kt + 1 if nth == 0 else SQUARED[nth + 1])
                    mm = pe.matmul(bank[b][:, 0:T], ones, square[:, kt, :], start=(kt == 0), stop=(kt == tiles - 1))
                mm.then_inc(summed, 1)

            def weight_pass(name, hi, lo, part=(0, None), between=None, operand=None):
                _, n0, units, kts = PASS[name]
                halves = 2 if name[:8] == "ffn_down" else 1

                def step(it, first=False):
                    for s in range(RING):
                        n = n0 + 4 * it + s
                        half = s % halves
                        out = bank[s - half]
                        pe.wait_ge(lo_done, n + 1)
                        if half == 0 and not first:
                            pe.wait_ge(bank_read, n - 4 + halves)
                        for k in range(kts):
                            c = half * kts + k
                            if operand:
                                operand(c)
                            pe.matmul(out[:, 0:T], w_hi[s][:, k, :], hi[:, c, :], start=(c == 0), stop=False)
                            pe.matmul(out[:, 0:T], w_hi[s][:, k, :], lo[:, c, :], start=False, stop=False)
                            mm = pe.matmul(out[:, 0:T], w_lo[s][:, k, :], hi[:, c, :], start=False,
                                           stop=(c == halves * kts - 1))
                        mm.then_inc(unit_used, 1)
                        if between:
                            between(it, s)
                first = part[0]
                end = part[1] or units // RING
                if between or operand:
                    for it in range(first, end):
                        step(it, first=(n0 + 4 * it == 0))
                else:
                    with pe.Fori(first, end) as it:
                        step(it)

            for layer in range(DEPTH):
                L = layer
                nth = 2 * L
                pe.wait_ge(norm_lo, KT * (nth + 1))
                q, k, v = proj[:, 0, :, :], keys[:, :, :], proj[:, 2, :, :]

                def score(i, left, right):
                    if i == 16:
                        pe.wait_ge(scores_put, 5 * L + 1)
                    elif i >= 4:
                        pe.wait_ge(scores_taken, 12 * L + i - 3)
                    for h in range(HEADS):
                        mm = pe.matmul(bank[4 + i % 4][:, 128 * h:128 * (h + 1)], left(h), right(h), start=True, stop=True)
                    mm.then_inc(scored, 1)

                def score_level(j):
                    if j < 0:
                        pe.wait_ge(q_gated, L + 1)
                        pe.wait_ge(keys_done, L + 1)
                    else:
                        pe.wait_ge(sided_done, 16 * L + 2 * j + 2)
                    z = sided[j % 2]
                    if j == len(LEVELS):
                        score(16, lambda h: z[:, h, 0:SEG], lambda h: z[:, h, SEG:SEQ])
                        return
                    for i in range(2):
                        tok = slice(SEG * i, SEG * (i + 1))
                        if j < 0:
                            score(i, lambda h: k[:, h, tok], lambda h: q[:, h, tok])
                        else:
                            score(2 * j + 2 + i, lambda h: z[:, h, tok], lambda h: z[:, h, tok])

                def spread(b):
                    if b >= 2:
                        pe.wait_ge(outer_done, 8 * L + b - 1)
                    for h in range(HEADS):
                        mm = pe.matmul(bank[4 + b % 2][:, 128 * h:128 * (h + 1)], v[:, h, SEQ + b:SEQ + b + 1].broadcast_to([128, 128]), ident,
                                       start=True, stop=True)
                    mm.then_inc(v_spread, 1)

                PE_LEVELS = {(3, 1): -1, (3, 2): 0, (3, 3): 1, (4, 0): 2, (4, 1): 3, (4, 2): 4, (4, 3): 5}

                def between(it, s):
                    if (it, s) in PE_LEVELS:
                        score_level(PE_LEVELS[(it, s)])

                def sample_head(h):
                    pe.wait_ge(state_decayed, 4 * L + h + 1)
                    for b in range(DEC):
                        c = SIDE.start + DEC * h + b
                        mm = pe.matmul(bank[2][:, c:c + 1], state[:, b, h, :], q[:, h, SEQ + b:SEQ + b + 1], start=True, stop=True)
                    mm.then_inc(sampled, 1)
                def sums_beside(it, s):
                    if s == 0:
                        sum_squares(2 * L, square, 4)
                pe.wait_ge(x_loaded, KT)
                weight_pass(f"in{L}", act_hi, act_lo, part=(0, 1), between=sums_beside)
                weight_pass(f"in{L}", act_hi, act_lo, part=(1, 3))
                weight_pass(f"in{L}", act_hi, act_lo, part=(3, 5), between=between)
                pe.wait_ge(bank_read, IN0[L] + 20)
                for i in range(2):
                    for h in range(HEADS):
                        mm = pe.transpose(bank[i][:, 128 * h:128 * (h + 1)], v[:, h, SEG * i:SEG * (i + 1)], ident)
                    mm.then_inc(v_turned, 1)
                pe.wait_ge(tables_in, 16)
                pe.wait_ge(past_in, 16 * (L + 1))
                rows = DEC * POOL_BUF
                for g in range(4):
                    mm = pe.matmul(bank[2][:, DEC * g:DEC * (g + 1)], pool_past[:, 128 * g:128 * (g + 1)], pick[0:rows, g, :], start=True, stop=True)
                mm.then_inc(past_summed, 1)
                pe.wait_ge(kq_done, L + 1)
                pe.matmul(bank[3][:, SIDE], ones, sample_kq[:, :, :].rearrange("p h b -> p (h b)"), start=True, stop=True).then_inc(sampled, 1)
                sample_head(0)
                score_level(6)
                sample_head(1)
                score_level(7)
                sample_head(2)
                pe.wait_ge(v_copied, 2 * (L + 1))
                pe.wait_ge(scores_put, 5 * L + 3)
                for h in range(HEADS):
                    hs = slice(128 * h, 128 * (h + 1))
                    mm = pe.matmul(bank[6][:, hs], values[:, 0, hs], scores[:, 0, h, :], start=True, stop=True)
                mm.then_inc(attended, 1)
                sample_head(3)
                pe.wait_ge(scores_put, 5 * (L + 1))
                for h in range(HEADS):
                    hs = slice(128 * h, 128 * (h + 1))
                    pe.matmul(bank[7][:, hs], values[:, 0, hs], scores_x[:, h, :], start=True, stop=False)
                    mm = pe.matmul(bank[7][:, hs], values[:, 1, hs], scores[:, 1, h, :], start=False, stop=True)
                mm.then_inc(attended, 1)

                def sum_heads(k):
                    n, cols, tok = HG_SUMS[k]
                    pe.wait_ge(hgo_squared, 3 * L + k + 1)
                    pe.matmul(bank[n][:, cols], ones, hgo_sq[:, :, tok], start=True, stop=True).then_inc(hgo_summed, 1)
                sum_heads(0)
                pe.wait_ge(pool_w_in, 16 * (L + 1))
                pe.wait_ge(sample_done, 2 * (L + 1))
                pe.wait_ge(past_added, 4 * (L + 1))
                for g in range(4):
                    w = (win_a, win_b)[g % 2]
                    pe.wait_ge(pooled, 4 * L + g + 1)
                    pe.matmul(bank[g][:, 0:T], pool_w[:, g, :], w[:, g, PAD:], start=True, stop=True).then_inc(pool_mapped, 1)
                pe.wait_ge(hgo_scaled, 16 * L + 8)
                sum_heads(1)
                sum_heads(2)

                def out_part(s, ks):
                    for k in ks:
                        if s == 0 and k < HEADS:
                            pe.wait_ge(mix_lo_done, 4 * L + k + 1)
                        for n, (w, x) in enumerate(((w_hi, mix_hi), (w_hi, mix_lo), (w_lo, mix_hi))):
                            mm = pe.matmul(bank[s][:, 0:T], w[s][:, k, :], x[:, k, :], start=(k == HEADS and n == 0),
                                           stop=(k == HEADS - 1 and n == 2))
                    return mm
                pe.wait_ge(pool_lo, 4 * (L + 1))
                for s in range(RING):
                    pe.wait_ge(lo_done, WO0[L] + s + 1)
                    out_part(s, range(HEADS, 2 * HEADS))
                pe.wait_ge(kdec_done, 2 * (L + 1))
                pe.wait_ge(hgo_scaled, 16 * L + 12)
                pe.wait_ge(hgo_rooted, 3 * L + 2)
                for i in range(2):
                    for h in range(HEADS):
                        mm = pe.transpose(bank[6 + i][:, 128 * h:128 * (h + 1)], kdec[:, h, SEG * i:SEG * (i + 1)], ident)
                    mm.then_inc(kdec_turned, 1)

                def route_tile(kt):
                    if kt == 0:
                        pe.wait_ge(final_copied, L + 1)
                        pe.wait_ge(router_in, 16)
                    pe.wait_ge(scaled_done, kt + 1)
                    mm = pe.matmul(bank[6][0:N_EXPERTS, 0:T], router[:, kt, :], scaled_m[:, kt, :], start=(kt == 0), stop=(kt == KT - 1))
                    if kt == KT - 1:
                        mm.then_inc(routed, 1)

                def beside_out(it, s):
                    if (it, s) == (0, 0):
                        pe.wait_ge(kdec_copied, 2 * (L + 1))
                        for h in range(HEADS):
                            hs = slice(128 * h, 128 * (h + 1))
                            pe.matmul(bank[6][:, hs], kdecT[:, 0, hs], values[:, 0, hs], start=True, stop=False)
                            mm = pe.matmul(bank[6][:, hs], kdecT[:, 1, hs], values[:, 1, hs], start=False, stop=True)
                        mm.then_inc(final_state, 1)
                    if (it, s) == (0, 1):
                        for g in range(4):
                            mm = pe.transpose(bank[7][0:POOL_BUF + DEC, 128 * g:128 * (g + 1)], up[:, g, PAD + SEQ - POOL_BUF:], ident)
                        mm.then_inc(tail_turned, 1)
                    spread(4 * it + s)
                    n = 4 * it + s
                    for kt in {3: (0, 1), 4: (2,), 5: (3,), 6: (4,), 7: (5,)}.get(n, ()):
                        if L:
                            route_tile(kt)
                for s in range(RING):
                    out_part(s, range(HEADS)).then_inc(unit_used, 1)
                    beside_out(0, s)
                weight_pass(f"out{L}", mix_hi, mix_lo, part=(1, 2), between=beside_out)
                if L:
                    route_tile(6)
                    route_tile(7)
                pe.wait_ge(tail_copied, L + 1)
                if L:
                    sum_squares(3, square_m, 7)
                if layer == 0:
                    pe.wait_ge(norm_lo, KT * 2)

                    def sums_beside(it, s):
                        if s == 0:
                            sum_squares(1, square_w, 7)
                    weight_pass("ffn_up0", act_hi, act_lo, part=(0, 1), between=sums_beside)
                    weight_pass("ffn_up0", act_hi, act_lo, part=(1, None))
                    weight_pass("ffn_down0", ffn_hi, ffn_lo, part=(0, 1),
                                operand=lambda c: pe.wait_ge(ffn_lo_done, c + 1))
                    weight_pass("ffn_down0", ffn_hi, ffn_lo, part=(1, None))
            for n in range(6):
                i, c = n // 2, n % 2
                t0, rows = TOKEN_TILES[i]
                if n == 0:
                    pe.wait_ge(bank_read, LAST_UNIT)
                if n == 4:
                    pe.wait_ge(outer_done, 2 * DEC)
                if n == 5:
                    pe.wait_ge(logits_scaled, 1)
                    for ii, (tt, r) in enumerate(TOKEN_TILES):
                        pe.transpose(bank[5][0:r, 8 * ii:8 * (ii + 1)], logit_rows[:, tt:tt + r], ident[0:N_EXPERTS, 0:N_EXPERTS])
                        mm = pe.transpose(bank[5][0:r, 128 * (ii + 1):128 * (ii + 2)], rstd[:, tt:tt + r], ident)
                    mm.then_inc(tokens_turned, 1)
                    pe.wait_ge(route, CHOSEN)
                    for ii, (_, r) in enumerate(TOKEN_TILES):
                        for jj in range(ii):
                            pe.matmul(bank[7][:, 8 * ii:8 * (ii + 1)], ones, chosen[:, jj, :], start=(jj == 0), stop=False)
                        pe.matmul(bank[7][:, 8 * ii:8 * (ii + 1)], before[0:r, :], chosen[0:r, ii, :], start=(ii == 0), stop=True)
                    for ii, (_, r) in enumerate(TOKEN_TILES):
                        mm = pe.matmul(bank[7][:, 24:32], ones[0:r, :], chosen[0:r, ii, :], start=(ii == 0), stop=(ii == 2))
                    mm.then_inc(placed, 1)
                for k in range(4):
                    mm = pe.transpose(bank[(0, 1, 2, 3, 4, 6)[n]][0:rows, 128 * k:128 * (k + 1)], scaled_m[:, 4 * c + k, t0:t0 + rows], ident)
                mm.then_inc(h_turned, 1)

            def gather(n):
                q, d = n // 4, n % 4
                if n >= 6:
                    pe.wait_ge(packed_lo, n - 1)
                for dd in range(2):
                    kt = 2 * d + dd
                    for m in range(6):
                        i, part = m // 2, (h_hi, h_lo)[m % 2]
                        rows = TOKEN_TILES[i][1]
                        mm = pe.matmul(bank[gather_bank(n)][:, 256 * dd:256 * (dd + 1)], part[0:rows, i, 128 * kt:128 * (kt + 1)],
                                       token_hot[0:rows, i, 2 * q:2 * q + 2, :].rearrange("p e s -> p (e s)"), start=(m == 0), stop=(m == 5))
                mm.then_inc(gathered, 1)

            def turn_hot(e):
                if e >= 2:
                    pe.wait_ge(hot_copied, e - 1)
                for i, (t0, rows) in enumerate(TOKEN_TILES):
                    mm = pe.transpose(bank[3 + (e + 1) % 2][:, t0:t0 + rows], token_hot[0:rows, i, e, :].bitcast(f32), ident[0:rows, 0:rows])
                mm.then_inc(hot_turned, 1)
            pe.wait_ge(hot, 3)
            pe.wait_ge(h_lo_done, 6)
            for n in range(4):
                gather(n)

            def unit_e(kind, k, j, turn=None):
                u = j if turn is None else HEAD_UNITS + TURN_UNITS * turn + j
                jj = j if turn is None else HEAD_UNITS + j
                pe.wait_ge(moe_lo, u + 1)
                hi, lo = (t[jj % SPLIT_RING][:, :, :].rearrange("p a b -> p (a b)") for t in (w_hi, w_lo))
                if kind == "down":
                    s_hi, s_lo, last, first_bank, pieces = hid_hi[:, k, :], hid_lo[:, k, :], FE - 1, 6, ((0, 512), (512, 512))
                else:
                    s_hi, s_lo, last, first_bank, pieces = x_hi[:, k, :], x_lo[:, k, :], KT - 1, 0 if kind == "gate" else 3, PIECES
                for n, (s, w) in enumerate(((s_hi, hi), (s_hi, lo), (s_lo, hi))):
                    for p, (c0, width) in enumerate(pieces):
                        mm = pe.matmul(bank[first_bank + p][:, 0:width], s, w[:, c0:c0 + width], start=(k == 0 and n == 0),
                                       stop=(k == last and n == 2))
                mm.then_inc(moe_used, 1)

            def turn_hidden(e):
                for p, (c0, width) in enumerate(PIECES):
                    pe.wait_ge(act_done, 3 * e + 3)
                    for k in range(width // 128):
                        mm = pe.transpose(bank[3 + p][:, 128 * k:128 * (k + 1)], act_e[:, c0 + 128 * k:c0 + 128 * (k + 1)], ident)
                    mm.then_inc(hid_turned, 1)

            pe.wait_ge(packed_lo, 4)
            pe.wait_ge(x_hi_set, 2)
            pe.wait_ge(x_lo_set, 2)
            for j in range(HEAD_UNITS):
                if j == KT:
                    pe.wait_ge(hot_copied, N_EXPERTS)
                    pe.wait_ge(y_lo_done, 1)
                unit_e(("gate", "up")[j // KT], j % KT, j)
                if j == 0:
                    pe.wait_ge(hot, 6)
                    pe.wait_ge(route, ROUTED)
                    for e in range(N_EXPERTS):
                        for i, (_, rows) in enumerate(TOKEN_TILES):
                            mm = pe.matmul(bank[5][:, e:e + 1], token_hot[0:rows, i, e, :].bitcast(f32), gates[0:rows, i, e:e + 1], start=(i == 0), stop=(i == 2))
                    mm.then_inc(gate_slots, 1)
                if j < N_EXPERTS:
                    turn_hot(j)
                if j < 12:
                    gather(4 + j)

            def turn_e(e):
                for j, (kind, _, k) in enumerate(TURN):
                    if kind == "gate" and k == 0:
                        pe.wait_ge(gate_silu, 3 * e + 3)
                        for ready in (x_hi_set, x_lo_set):
                            pe.wait_ge(ready, 2 * e + 3)
                    if kind == "gate" and k == KT // 2:
                        turn_hidden(e)
                        for ready in (x_hi_set, x_lo_set):
                            pe.wait_ge(ready, 2 * e + 4)
                    if kind == "down" and k == 0:
                        pe.wait_ge(hid_lo_done, 3 * e + 3)
                        pe.wait_ge(y_lo_done, 2 * e + 1)
                    unit_e(kind, k, j, turn=e)
            with pe.Fori(0, N_EXPERTS - 1) as e:
                turn_e(e)
            last = N_EXPERTS - 1

            def scatter(e, kt):
                for half in range(2):
                    mm = pe.matmul(bank[kt][:, 0:T], packed[:, e, half, 128 * kt:128 * (kt + 1)], slot_hot[:, e, :],
                                   start=(e == 0 and half == 0), stop=(e == last and half == 1))
                return mm
            pe.wait_ge(gate_silu, 3 * N_EXPERTS)
            pe.wait_ge(y_lo_done, 2 * last + 1)
            for kt in range(3):
                for e in range(last):
                    scatter(e, kt)
            turn_hidden(last)
            for j in range(FE):
                if j % 4 == 0:
                    pe.wait_ge(hid_lo_done, 3 * last + j // 4 + 1)
                unit_e("down", j, j, turn=last)
            for kt in range(3, 6):
                for e in range(last):
                    scatter(e, kt)
            pe.wait_ge(y_lo_done, 2 * N_EXPERTS + 1)
            for kt in range(6):
                scatter(last, kt).then_inc(scattered, 1)
            for kt in range(6, KT):
                for e in range(last):
                    scatter(e, kt)
                scatter(last, kt).then_inc(scattered, 1)
            n_rows = pe.value_load(longest_i[0:1, 0:1])
            with pe.If(n_rows > CAP):
                pe.wait_ge(moe_added, KT)
                pe.wait_ge(all_added, KT)
                with pe.Fori(0, N_EXPERTS) as e:
                    pe.wait_ge(all_col, e + 1)
                    for i, (t0, rows) in enumerate(TOKEN_TILES):
                        mm = pe.matmul(bank[2][:, t0:t0 + rows], over_col[0:rows, i:i + 1].broadcast_to([rows, 128]), ident[0:rows, 0:rows], start=True, stop=True)
                    mm.then_inc(all_spread, 1)
                    with pe.Fori(0, FE) as f:
                        n = e * FE + f
                        pe.wait_ge(all_w, 48 * (n + 1))
                        pe.wait_ge(all_added, n * KT + KT)
                        for b, w in enumerate((gate_w_all, up_w_all)):
                            for kt in range(KT):
                                mm = pe.matmul(bank[b][:, 0:T], w[:, kt, :], h_all[:, kt, :], start=(kt == 0), stop=(kt == KT - 1))
                            mm.then_inc(all_up, 1)
                        pe.wait_ge(all_act, 2 * n + 2)
                        for kt in range(KT):
                            pe.wait_ge(all_added, n * KT + KT + max(kt - 3, 0))
                            pe.matmul(bank[4 + kt % 4][:, 0:T], down_w_all[:, 128 * kt:128 * (kt + 1)], act_all[:, :], start=True, stop=True).then_inc(all_down, 1)
                pe.wait_ge(all_added, N_EXPERTS * FE * KT + KT)
            pe.end_ifs()
            def sum_token_squares(i, kt):
                t0, rows = TOKEN_TILES[i]
                b, c = NORM_SUMS[i]
                return pe.matmul(bank[b][0:rows, c:c + 1], square_f[:, kt, t0:t0 + rows], ones[:, 0:1], start=(kt == 0), stop=(kt == KT - 1))
            pe.wait_ge(moe_added, KT)
            for c in range(2):
                for kt in range(4 * c, 4 * (c + 1)):
                    pe.wait_ge(squared, SQUARED[4] + kt + 1)
                    for i in range(2):
                        sum_token_squares(i, kt)
                if c:
                    for kt in range(KT):
                        mm = sum_token_squares(2, kt)
                    mm.then_inc(summed, 1)
                pe.wait_ge(scaled_done, KT + 4 * (c + 1))
                for i, (t0, rows) in enumerate(TOKEN_TILES):
                    for k in range(4):
                        mm = pe.transpose(bank[5 * c + i][0:rows, 128 * k:128 * (k + 1)], scaled_f[:, 4 * c + k, t0:t0 + rows], ident)
                    mm.then_inc(turned, 1)


def constants():
    import numpy as np
    c = np.zeros((128, C_COLS), np.float32)
    i = np.arange(128)
    c[:, C_IDENT:C_IDENT + 128] = np.eye(128)
    c[:, C_ONES:C_ONES + 128] = 1.0
    c[:, C_BEFORE:C_BEFORE + 128] = i[:, None] < i[None, :]
    c[:, C_IOTA:C_IOTA + 128] = i[None, :]
    c[:, C_MASK:C_MASK + 128] = np.eye(128)
    for n, half in enumerate(LEVELS):
        s, t = i[:, None], i[None, :]
        pair = (s // (2 * half) == t // (2 * half)) & (s % (2 * half) < half) & (t % (2 * half) >= half)
        c[:, C_MASK + 128 * (n + 1):C_MASK + 128 * (n + 2)] = pair
    for g, w in enumerate(WINDOWS):
        t = np.arange(PAD)
        c[:, C_CORR + g * PAD:C_CORR + (g + 1) * PAD] = w / np.minimum(t + 1, w).astype(np.float32)
        for b in range(DEC):
            c[POOL_BUF * b + POOL_BUF + 1 - w:POOL_BUF * (b + 1), C_PICK + g * DEC + b] = 1.0
    e = np.arange(N_EXPERTS)
    c[:, C_LOWER:C_LOWER + 64] = (e[None, :] < e[:, None]).reshape(-1)
    return c


_INS = ["x_prompt", "x_sample", "state_hgrn", "state_pool", "lb_logits", "norm_mix", "w_in", "w_o", "hg_norm", "pool_w", "pool_scale",
        "norm_ffn", "ffn_w_gate", "ffn_w_up", "ffn_w_down", "router", "moe_w_gate", "moe_w_up", "moe_w_down", "norm_final"]
_OUTS = [("y_prompt", (1, SEQ, D_MODEL)), ("y_sample", (DEC, 1, D_MODEL)), ("new_hgrn_prompt", (DEPTH, 1, HEADS, 128, 128)),
         ("new_hgrn_sample", (DEPTH, DEC, HEADS, 128, 128)), ("new_pool_prompt", (DEPTH, 1, POOL_BUF, HG_WIDTH)),
         ("new_pool_sample", (DEPTH, DEC, POOL_BUF, HG_WIDTH))]


def kernel(**inputs):
    import numpy as np
    import concourse.bacc as bacc
    from concourse.bass_utils import run_bass_kernel_spmd

    nc = bacc.Bacc("TRN2", target_bir_lowering=False, num_devices=1)
    arrays = {n: np.ascontiguousarray(inputs[n]) for n in _INS}
    arrays["consts"] = constants()
    launched = {f"in_{n}_dram": x for n, x in arrays.items()}
    a = {n: nc.dram_tensor(f"in_{n}_dram", x.shape, mybir.dt.float32, kind="ExternalInput").ap() for n, x in arrays.items()}
    o = {n: nc.dram_tensor(f"out_{n}_dram", s, mybir.dt.float32, kind="ExternalOutput").ap() for n, s in _OUTS}
    build_program(nc, a, o)
    r = run_bass_kernel_spmd(nc, [launched], core_ids=[0])
    return tuple(r.results[0][f"out_{n}_dram"] for n, _ in _OUTS)
```
